# Optimizing a Trainium2 kernel written in Bass

```python
import jax, jax.numpy as jnp
from jax import lax
import numpy as np

D_MODEL = 1024
BATCH = 1
SEQ = 1024
DEPTH = 1
DEC_BATCH = 8
DEC_SEQ = 8
PAST_LEN = 8192
PAGE_SIZE = 128

N_BRANCH = 4
W_BR = D_MODEL // 2
POOL_WINDOWS = (2, 4, 8, 16)
N_POOL_GROUPS = 4
POOL_GW = W_BR // N_POOL_GROUPS
POOL_PREV = max(POOL_WINDOWS) - 1
SCONV_K = 3
CCONV_K = 31
CHUNK = 128
N_SGU_GROUPS = 4
SGU_GW = W_BR // N_SGU_GROUPS
N_MEM = 256
N_XHEADS = 4
XHEAD_DIM = D_MODEL // N_XHEADS
D_FF = 4 * D_MODEL
EPS = 1e-6
SPLIT_POINTS = (W_BR, 2 * W_BR, 3 * W_BR, 4 * W_BR, 6 * W_BR, 8 * W_BR)
PROJ_W = 8 * W_BR + N_BRANCH * D_MODEL

kernel_name = 'gated_parallel_pool_conv_sgu_conformer_decoder_step'

def rmsnorm(x, g):
    xf = x.astype(jnp.float32)
    y = xf * lax.rsqrt(jnp.mean(xf * xf, axis=-1, keepdims=True) + EPS)
    return (y * g.astype(jnp.float32)).astype(x.dtype)

def layernorm(x, g, b):
    xf = x.astype(jnp.float32)
    xc = xf - jnp.mean(xf, axis=-1, keepdims=True)
    var = jnp.mean(xc * xc, axis=-1, keepdims=True)
    y = xc * lax.rsqrt(var + EPS) * g.astype(jnp.float32) + b.astype(jnp.float32)
    return y.astype(x.dtype)

def pool_mix(ext, pos0, pool_w, pool_scale):
    L = ext.shape[1] - POOL_PREV
    ef = ext.astype(jnp.float32)
    c = jnp.cumsum(ef, axis=1)
    c = jnp.concatenate([jnp.zeros_like(c[:, :1]), c], axis=1)
    pos = pos0 + jnp.arange(L)
    outs = []
    for g, w in enumerate(POOL_WINDOWS):
        sl = slice(g * POOL_GW, (g + 1) * POOL_GW)
        win_sum = c[:, POOL_PREV + 1:, sl] - c[:, POOL_PREV + 1 - w:POOL_PREV + 1 - w + L, sl]
        cnt = jnp.minimum(pos + 1, w).astype(jnp.float32)[None, :, None]
        p = win_sum / cnt - ef[:, POOL_PREV:, sl]
        outs.append(p.astype(pool_w.dtype) @ pool_w[g])
    return jnp.concatenate(outs, axis=-1) * pool_scale

def causal_dwconv(ext, w):
    C = ext.shape[-1]
    return lax.conv_general_dilated(ext, w[:, None, :].astype(ext.dtype), window_strides=(1,), padding='VALID',
                                    dimension_numbers=('NWC', 'WIO', 'NWC'), feature_group_count=C)

def chunk_spatial_mix(v, w_s, b_s):
    Bn, L, _ = v.shape
    Lp = -(-L // CHUNK) * CHUNK
    vp = jnp.pad(v, ((0, 0), (0, Lp - L), (0, 0))).reshape(Bn, Lp // CHUNK, CHUNK, N_SGU_GROUPS, SGU_GW)
    causal = jnp.tril(jnp.ones((CHUNK, CHUNK), dtype=bool))
    ws = jnp.where(causal[None], w_s, jnp.zeros_like(w_s))
    s = jnp.einsum('gts,bnsgc->bntgc', ws, vp) + jnp.transpose(b_s)[None, None, :, :, None]
    return s.reshape(Bn, Lp, W_BR)[:, :L]

def mixer_block(h, pool_prev, sconv_prev, cconv_prev, pos0, w_in, pool_w, pool_scale, sconv_w,
                sgu_ln_g, sgu_ln_b, sgu_w, sgu_b, cconv_w, cconv_b, cconv_ln_g, cconv_ln_b,
                w_branch, b_gate, w_mix_out):
    Bn, L, _ = h.shape
    z = h @ w_in
    a_u, b_h, b_b, b_c, c_uv, d_in, g_in = jnp.split(z, SPLIT_POINTS, axis=-1)
    pool_ext = jnp.concatenate([pool_prev, a_u], axis=1)
    a_out = pool_mix(pool_ext, pos0, pool_w, pool_scale)
    new_pool = pool_ext[:, -POOL_PREV:]
    sc_ext = jnp.concatenate([sconv_prev, b_c * b_h], axis=1)
    b_out = b_b * causal_dwconv(sc_ext, sconv_w)
    new_sconv = sc_ext[:, -(SCONV_K - 1):]
    c_u, c_v = jnp.split(jax.nn.gelu(c_uv), 2, axis=-1)
    c_vn = layernorm(c_v, sgu_ln_g, sgu_ln_b)
    c_out = c_u * chunk_spatial_mix(c_vn, sgu_w, sgu_b)
    d_a, d_b = jnp.split(d_in, 2, axis=-1)
    cc_ext = jnp.concatenate([cconv_prev, d_a * jax.nn.sigmoid(d_b)], axis=1)
    d_c = causal_dwconv(cc_ext, cconv_w) + cconv_b
    d_out = jax.nn.silu(layernorm(d_c, cconv_ln_g, cconv_ln_b))
    new_cconv = cc_ext[:, -(CCONV_K - 1):]
    branches = jnp.stack([a_out, b_out, c_out, d_out], axis=2)
    proj = jnp.einsum('blkw,kwd->blkd', branches, w_branch)
    gates = jax.nn.sigmoid(g_in.reshape(Bn, L, N_BRANCH, D_MODEL) + b_gate)
    merged = jnp.sum(gates * proj, axis=2)
    return merged @ w_mix_out, new_pool, new_sconv, new_cconv, c_vn

def mem_kv(mem, g, w_k, w_v):
    Bn = mem.shape[0]
    m = rmsnorm(mem, g)
    k = (m @ w_k).reshape(Bn, N_MEM, N_XHEADS, XHEAD_DIM)
    v = (m @ w_v).reshape(Bn, N_MEM, N_XHEADS, XHEAD_DIM)
    return k, v

def cross_attend(h, k, v, w_q, w_o):
    Bn, L, _ = h.shape
    q = (h @ w_q).reshape(Bn, L, N_XHEADS, XHEAD_DIM)
    s = jnp.einsum('blhd,bmhd->bhlm', q, k).astype(jnp.float32) * (XHEAD_DIM ** -0.5)
    p = jax.nn.softmax(s, axis=-1).astype(v.dtype)
    o = jnp.einsum('bhlm,bmhd->blhd', p, v).reshape(Bn, L, D_MODEL)
    return o @ w_o

def sq_relu_mlp(h, w1, w2):
    return jnp.square(jax.nn.relu(h @ w1)) @ w2

def run_trunk(x, pool_prev, sconv_prev, cconv_prev, mem_k, mem_v, pos0, P):
    pools, sconvs, cconvs, vs = [], [], [], []
    for l in range(DEPTH):
        h = rmsnorm(x, P['norm_mix_g'][l])
        m, npool, nsc, ncc, vn = mixer_block(
            h, pool_prev[l], sconv_prev[l], cconv_prev[l], pos0,
            P['w_in'][l], P['pool_w'][l], P['pool_scale'][l], P['sconv_w'][l],
            P['sgu_ln_g'][l], P['sgu_ln_b'][l], P['sgu_w'][l], P['sgu_b'][l],
            P['cconv_w'][l], P['cconv_b'][l], P['cconv_ln_g'][l], P['cconv_ln_b'][l],
            P['w_branch'][l], P['b_gate'][l], P['w_mix_out'][l])
        x = x + m
        x = x + cross_attend(rmsnorm(x, P['norm_x_g'][l]), mem_k[l], mem_v[l], P['w_xq'][l], P['w_xo'][l])
        x = x + sq_relu_mlp(rmsnorm(x, P['norm_ffn_g'][l]), P['w_ff1'][l], P['w_ff2'][l])
        pools.append(npool)
        sconvs.append(nsc)
        cconvs.append(ncc)
        vs.append(vn)
    return rmsnorm(x, P['norm_f_g']), pools, sconvs, cconvs, vs

def setup_inputs(seed: int = 0) -> dict:
    key = jax.random.key(seed)
    ks = iter(jax.random.split(key, 48))
    def nrm(shape, scale):
        return scale * jax.random.normal(next(ks), shape, jnp.float32)
    def gain(shape):
        return 1.0 + 0.05 * jax.random.normal(next(ks), shape, jnp.float32)
    dD = D_MODEL ** -0.5
    return {
        'x_prompt': nrm((BATCH, SEQ, D_MODEL), 1.0),
        'x_sample': nrm((DEC_BATCH, DEC_SEQ, D_MODEL), 1.0),
        'state_pool': nrm((DEPTH, DEC_BATCH, POOL_PREV, W_BR), 1.0),
        'state_sconv': nrm((DEPTH, DEC_BATCH, SCONV_K - 1, W_BR), 1.0),
        'state_cconv': nrm((DEPTH, DEC_BATCH, CCONV_K - 1, W_BR), 0.5),
        'cache_mem_k': nrm((DEPTH, DEC_BATCH, N_MEM, N_XHEADS, XHEAD_DIM), 1.0),
        'cache_mem_v': nrm((DEPTH, DEC_BATCH, N_MEM, N_XHEADS, XHEAD_DIM), 1.0),
        'mem_prompt': nrm((BATCH, N_MEM, D_MODEL), 1.0),
        'norm_mix_g': gain((DEPTH, D_MODEL)),
        'w_in': nrm((DEPTH, D_MODEL, PROJ_W), dD),
        'pool_w': nrm((DEPTH, N_POOL_GROUPS, POOL_GW, POOL_GW), POOL_GW ** -0.5),
        'pool_scale': 1.0 + 0.1 * jax.random.normal(next(ks), (DEPTH, W_BR), jnp.float32),
        'sconv_w': nrm((DEPTH, SCONV_K, W_BR), SCONV_K ** -0.5),
        'sgu_ln_g': gain((DEPTH, W_BR)),
        'sgu_ln_b': nrm((DEPTH, W_BR), 0.02),
        'sgu_w': nrm((DEPTH, N_SGU_GROUPS, CHUNK, CHUNK), CHUNK ** -0.5),
        'sgu_b': 1.0 + 0.02 * jax.random.normal(next(ks), (DEPTH, N_SGU_GROUPS, CHUNK), jnp.float32),
        'cconv_w': nrm((DEPTH, CCONV_K, W_BR), CCONV_K ** -0.5),
        'cconv_b': nrm((DEPTH, W_BR), 0.02),
        'cconv_ln_g': gain((DEPTH, W_BR)),
        'cconv_ln_b': nrm((DEPTH, W_BR), 0.02),
        'w_branch': nrm((DEPTH, N_BRANCH, W_BR, D_MODEL), W_BR ** -0.5),
        'b_gate': nrm((DEPTH, N_BRANCH, D_MODEL), 0.02),
        'w_mix_out': nrm((DEPTH, D_MODEL, D_MODEL), dD),
        'norm_x_g': gain((DEPTH, D_MODEL)),
        'norm_mem_g': gain((DEPTH, D_MODEL)),
        'w_xq': nrm((DEPTH, D_MODEL, D_MODEL), dD),
        'w_xk': nrm((DEPTH, D_MODEL, D_MODEL), dD),
        'w_xv': nrm((DEPTH, D_MODEL, D_MODEL), dD),
        'w_xo': nrm((DEPTH, D_MODEL, D_MODEL), dD),
        'norm_ffn_g': gain((DEPTH, D_MODEL)),
        'w_ff1': nrm((DEPTH, D_MODEL, D_FF), dD),
        'w_ff2': nrm((DEPTH, D_FF, D_MODEL), D_FF ** -0.5),
        'norm_f_g': gain((D_MODEL,)),
    }

def reference(x_prompt, x_sample, state_pool, state_sconv, state_cconv, cache_mem_k, cache_mem_v, mem_prompt,
              norm_mix_g, w_in, pool_w, pool_scale, sconv_w, sgu_ln_g, sgu_ln_b, sgu_w, sgu_b,
              cconv_w, cconv_b, cconv_ln_g, cconv_ln_b, w_branch, b_gate, w_mix_out,
              norm_x_g, norm_mem_g, w_xq, w_xk, w_xv, w_xo, norm_ffn_g, w_ff1, w_ff2, norm_f_g):
    P = {'norm_mix_g': norm_mix_g, 'w_in': w_in, 'pool_w': pool_w, 'pool_scale': pool_scale,
         'sconv_w': sconv_w, 'sgu_ln_g': sgu_ln_g, 'sgu_ln_b': sgu_ln_b, 'sgu_w': sgu_w, 'sgu_b': sgu_b,
         'cconv_w': cconv_w, 'cconv_b': cconv_b, 'cconv_ln_g': cconv_ln_g, 'cconv_ln_b': cconv_ln_b,
         'w_branch': w_branch, 'b_gate': b_gate, 'w_mix_out': w_mix_out, 'norm_x_g': norm_x_g,
         'w_xq': w_xq, 'w_xo': w_xo, 'norm_ffn_g': norm_ffn_g, 'w_ff1': w_ff1, 'w_ff2': w_ff2,
         'norm_f_g': norm_f_g}
    dt = x_prompt.dtype
    kv = [mem_kv(mem_prompt, norm_mem_g[l], w_xk[l], w_xv[l]) for l in range(DEPTH)]
    mem_k_prompt = jnp.stack([k for k, _ in kv])
    mem_v_prompt = jnp.stack([v for _, v in kv])
    zp = jnp.zeros((DEPTH, BATCH, POOL_PREV, W_BR), dt)
    zs = jnp.zeros((DEPTH, BATCH, SCONV_K - 1, W_BR), dt)
    zc = jnp.zeros((DEPTH, BATCH, CCONV_K - 1, W_BR), dt)
    y_prompt, pool_p, sconv_p, cconv_p, _ = run_trunk(x_prompt, zp, zs, zc, mem_k_prompt, mem_v_prompt, 0, P)
    y_sample, pool_s, sconv_s, cconv_s, v_s = run_trunk(x_sample, state_pool, state_sconv, state_cconv,
                                                        cache_mem_k, cache_mem_v, PAST_LEN, P)
    new_pool_prompt = jnp.stack(pool_p)
    new_sconv_prompt = jnp.stack(sconv_p)
    new_cconv_prompt = jnp.stack(cconv_p)
    new_pool_sample = jnp.stack(pool_s)
    new_sconv_sample = jnp.stack(sconv_s)
    new_cconv_sample = jnp.stack(cconv_s)
    sgu_v_sample = jnp.stack(v_s)
    return (y_prompt, y_sample, new_pool_prompt, new_sconv_prompt, new_cconv_prompt, mem_k_prompt, mem_v_prompt,
            new_pool_sample, new_sconv_sample, new_cconv_sample, sgu_v_sample)


_drawn_inputs = setup_inputs


def setup_inputs(seed=0):
    import zlib

    import numpy as np

    out = dict(_drawn_inputs(seed))
    spreads = {}
    factors = {'sgu_ln_b': 3.012,
     'sgu_b': 21.745,
     'cconv_b': 5.457,
     'cconv_ln_g': 3.695,
     'cconv_ln_b': 22.647,
     'b_gate': 8.0,
     'norm_x_g': 8.0,
     'pool_scale': 3.337,
     'norm_ffn_g': 2.907}
    for name, (base, spread) in spreads.items():
        noise = np.random.default_rng([zlib.crc32(name.encode()), seed]).standard_normal(out[name].shape)
        drawn = base * np.exp(spread * noise) if base else spread * noise
        out[name] = __import__('jax').numpy.asarray(drawn.astype(out[name].dtype))
    for name, factor in factors.items():
        out[name] = (out[name] * factor).astype(out[name].dtype)
    return out
```

```python
from contextlib import ExitStack

import numpy as np

import concourse.bass as bass
from concourse import mybir

F32 = mybir.dt.float32
F32R = mybir.dt.float32r
ALU = mybir.AluOpType
ACT = mybir.ActivationFunctionType
AX_X = mybir.AxisListType.X

P = 128
D_MODEL = 1024
SEQ = 1024
DEC_B, DEC_L = 8, 8
N_SAMPLE = DEC_B * DEC_L
T = SEQ + N_SAMPLE
W_BR = 512
KT = D_MODEL // P
CT = W_BR // P
N_MEM = 256
MT = N_MEM // P
HEADS = 4
HEAD_DIM = D_MODEL // HEADS
D_FF = 4 * D_MODEL
EPS = 1e-6
POOL_H, SCONV_H, CCONV_H = 15, 2, 30
SCONV_K, CCONV_K = 3, 31
TOK_TILES = [(i * P, min(P, T - i * P)) for i in range(9)]

CW = 364
CHUNKS = [(0, CW), (CW, CW), (2 * CW, T - 2 * CW)]
TAIL = SEQ - 2 * CW

VA_CCW, VA_SCW, VA_PSC, VA_CCB, VA_LNG, VA_LNB, VA_N = 0, 31, 34, 35, 36, 37, 38
VB_MIX, VB_X, VB_FFN, VB_MEM, VB_GATE, VB_N = 0, 2, 4, 6, 8, 16

TILE = T * 4
REGION = KT * TILE
EXT_D = CCONV_H + SEQ + DEC_B * (CCONV_H + DEC_L)
EXT_A = POOL_H + SEQ + DEC_B * (POOL_H + DEC_L)
EXT_B = SCONV_H + SEQ + DEC_B * (SCONV_H + DEC_L)

IN_A, IN_BH, IN_BB, IN_BC, IN_CU, IN_CV, IN_DA, IN_DB, IN_G = 0, 4, 8, 12, 16, 20, 24, 28, 32
BRANCHES = [2, 0, 1, 3]

S_CV = 0
S_D = S_CV + 4
S_CU = S_D + 16
S_A = S_CU + 12
S_B = S_A + 4
S_GATE = S_B + 12
S_MIX = S_GATE + 48
S_Q = S_MIX + 8
S_XO = S_Q + 8
S_FF = S_XO + 8
S_END = S_FF + 64

N_P0 = 0
N_CV = N_P0 + 9
N_D = N_CV + 4
N_CU = N_D + 8
N_A = N_CU + 8
N_A_IN = [N_A, N_A + 1, N_A + 3, N_A + 5]
N_A_MAP = [N_A + 2, N_A + 4, N_A + 6, N_A + 8]
N_B_H = [N_A + 7, N_A + 11, N_A + 15, N_A + 19]
N_B_C = [N_A + 9, N_A + 12, N_A + 17, N_A + 20]
N_B_B = [N_A + 10, N_A + 14, N_A + 18, N_A + 21]
N_MEAN, N_VAR = N_A + 13, N_A + 16
N_GATE = N_A + 22
N_MIX = N_GATE + 64
N_Q = N_MIX + 8
N_XO = N_Q + 8
N_FF = N_XO + 8

AUX_ORDER = (["vec", "ws", "pl", "m0", "m1", "cc", "x0", "x1", "x2", "v0a", "v0b", "x3", "x4", "v1a", "v1b", "x5",
              "x6", "v2a", "v2b", "x7", "x8", "v3a", "v3b", "K0", "K1", "tail_d", "V0", "V1", "tail_a", "tail_b",
              "sum0", "sum1"]
             + [f"y{m}{h}" for m in range(KT) for h in "ab"])
AUX = {name: n for n, name in enumerate(AUX_ORDER)}

RING_XT, RING_C, RING_A, RING_B, RING_D = 0, 9, 13, 17, 21
RING_OF = {2: RING_C, 0: RING_A, 1: RING_B, 3: RING_D}

Y_PARTS = [(0, 6 * P), (6 * P, 7 * P), (7 * P, 8 * P)]

TAPS_D, TAPS_CU, TAPS_A, TAPS_B = [4, 15, 17, 17], [9, 9, 9, 7], [4, 3, 1, 0], [14, 5, 10]
assert sum(TAPS_D + TAPS_CU + TAPS_A + TAPS_B) == CT * CCONV_K


class Chain:

    def __init__(self, eng, sem):
        self.eng, self.sem, self.n, self.i, self.per = eng, sem, 0, None, 0

    def link(self, ins):
        self.n += 1
        ins.then_inc(self.sem, 1)
        self.eng.wait_ge(self.sem, self.n if self.i is None else self.i * self.per + self.n)

    def enter(self, i, per):
        self.i, self.per, self.start = i, per, self.n

    def leave(self, count):
        assert self.n - self.start == self.per, (self.n - self.start, self.per)
        self.i = None
        self.n = self.start + self.per * count


def build(nc, a, o, scratch):
    ctx = ExitStack()
    with ctx:
        _build(nc, a, o, scratch, ctx)


def _build(nc, a, o, scratch, ctx):
    base = nc.sbuf_base + (-nc.sbuf_base) % 32

    def at(name, shape, offset, dt=F32):
        return nc.alloc_sbuf_tensor_at(name, shape, dt, offset=base + offset)

    def S(name):
        return ctx.enter_context(nc.semaphore(name))

    Q = [REGION * i for i in range(5)]
    R1 = Q[2]
    o_w = 5 * REGION
    o_t = o_w + 6 * 4096
    o_c = o_t + 3 * TILE

    w_raw = at("w_raw", [P, 2, 1024], o_w)
    w_hi = at("w_hi", [P, 2, 1024], o_w + 8192, F32R)
    w_lo = at("w_lo", [P, 2, 1024], o_w + 16384, F32R)
    tmp = [at(f"tmp{i}", [P, T], o_t + i * TILE) for i in range(3)]
    ident = at("ident", [P, P], o_c)
    vec_b = at("vec_b", [P, VB_N * 4], o_c + 512)
    ones = at("ones", [P, 1], o_c + 768)
    assert o_c + 800 <= nc.sbuf_usable_end - base

    h_hi = at("h_hi", [P, KT, T], Q[0], F32R)
    h_lo = at("h_lo", [P, KT, T], Q[1], F32R)
    x_res = at("x_res", [P, KT, T], Q[0])
    xs_hi = at("xs_hi", [P, KT, T], Q[1], F32R)
    xs_lo = at("xs_lo", [P, KT, T], Q[2], F32R)
    merged = at("merged", [P, KT, T], Q[4])
    br_hi = [at(f"br_hi{i}", [P, CT, T], Q[3 - i], F32R) for i in range(2)]
    br_lo = [at(f"br_lo{i}", [P, CT, T], Q[3 - i] + CT * TILE, F32R) for i in range(2)]
    mv_hi = at("mv_hi", [P, KT, T], Q[3], F32R)
    mv_lo = at("mv_lo", [P, KT, T], Q[4], F32R)

    slots_d = at("slots_d", [P, 5, EXT_D], R1)
    xn = at("xn", [P, 2, 1024], R1)
    fbuf = at("fbuf", [P, 2, 1024], R1 + 8192)
    ws_raw = at("ws_raw", [P, HEADS, P], R1 + 16384)
    bd_raw = at("bd_raw", [N_SAMPLE, HEADS, N_SAMPLE], R1 + 18432)
    cc_raw = at("cc_raw", [120, 2, W_BR], R1 + 19456)
    pl_raw = at("pl_raw", [120, W_BR], R1 + 23552)
    oA = R1 + 27200
    xring = at("xring", [P, 4, 1024], oA)
    ext_a = at("ext_a", [P, 2, EXT_A], oA)
    sums = at("sums", [P, 2, EXT_A], oA + 9792)
    pooled = at("pooled", [P, T], oA + 19584)
    mem_hi = at("mem_hi", [P, KT, N_MEM], oA + 16384, F32R)
    mem_lo = at("mem_lo", [P, KT, N_MEM], oA + 24576, F32R)
    kv_out = at("kv_out", [P, MT, W_BR], oA + 12288)
    tail_d = at("tail_d", [N_SAMPLE, 2, W_BR], oA + 8192)
    tail_a = at("tail_a", [N_SAMPLE, 2, W_BR], oA + 23936)
    tail_b = at("tail_b", [N_SAMPLE, 2, W_BR], oA)
    oV = R1 + 59968
    v_tok = at("v_tok", [P, 9, W_BR], oV)
    b_h = at("b_h", [P, T], Q[4])
    ext_b = at("ext_b", [P, EXT_B], Q[4] + TILE)
    oR = R1 + 78464
    vring = at("vring", [P, 2, T], oR)
    oring = at("oring", [P, 2, T], oR + 2 * TILE)
    oK = oR + 4 * TILE
    ws_t = at("ws_t", [P, HEADS, P], oK)
    bd_t = at("bd_t", [N_SAMPLE, HEADS, N_SAMPLE], oK + 2048)
    st_pool = at("st_pool", [P, CT, 120], oK + 3072)
    st_sc = at("st_sc", [P, CT, 16], oK + 4992)
    vec_a = at("vec_a", [P, VA_N * 4], oK + 5248)
    pool_wt = at("pool_wt", [P, CT, P], oK + 5856)
    small = at("small", [P, 128], oK + 7904)
    assert oK + 8416 <= 5 * REGION
    sc_raw = at("sc_raw", [16, W_BR], o_t)
    vec_raw = at("vec_raw", [VA_N + VB_N, W_BR], o_t + 2048)
    ln_g = at("ln_g", [P, W_BR], o_t)
    ln_b = at("ln_b", [P, W_BR], o_t + 2048)
    bias_s = at("bias_s", [P, HEADS, P], o_t + TILE)
    tailbuf = at("tailbuf", [P, CT, CCONV_H + N_SAMPLE], o_t + TILE + 2048)
    ss = small[:, 0:11]
    bn = small[:, 16:70].rearrange("p (t s) -> p t s", t=9)
    bn_mv = small[:, 72:90].rearrange("p (t s) -> p t s", t=9)
    v_rstd = small[:, 91:100]
    inv_cnt = small[:, 104:119]

    kvring = at("kvring", [P, 4, MT * D_MODEL], Q[1])
    kt_hi = at("kt_hi", [P, KT, N_MEM], Q[1] + 32768, F32R)
    kt_lo = at("kt_lo", [P, KT, N_MEM], Q[1] + 40960, F32R)
    kt_s = at("kt_s", [P, 2, KT, N_MEM], Q[1] + 32768)
    v_hi = at("v_hi", [P, MT, D_MODEL], Q[1] + 49152, F32R)
    v_lo = at("v_lo", [P, MT, D_MODEL], Q[1] + 57344, F32R)
    ptm = at("ptm", [P, DEC_B, 2 * HEADS * N_SAMPLE], Q[1] + 49152)
    p_s = at("p_s", [N_SAMPLE, D_MODEL], Q[1] + 65536)
    pt_hi = [at(f"pt_hi{i}", [P, MT, 512], (o_t + TILE, Q[1])[i], F32R) for i in range(2)]
    pt_lo = [at(f"pt_lo{i}", [P, MT, 512], (o_t + 2 * TILE, Q[1] + 4096)[i], F32R) for i in range(2)]
    qm = [at(f"qm{i}", [P, KT * N_SAMPLE], o_t + TILE + (i // 2) * TILE + (i % 2) * 2048) for i in range(4)]
    probs = at("probs", [P, 4, N_MEM], o_t)
    sm = at("sm", [P, 60], o_t + 4096)

    y_tok = at("y_tok", [P, 9, D_MODEL], Q[1])
    gf = at("gf", [P, D_MODEL], Q[1] + 36864)
    junk = at("junk", [P, 2, D_MODEL], Q[1] + 40960)
    fst = at("fst", [P, 3, 9], Q[1] + 49152)

    PS = ctx.enter_context(nc.psum_tensor("PS", [P, 8, 512], F32))

    def pset(n):
        return PS[:, 3 * (n % 2):3 * (n % 2) + 3, :]

    def flat(ap):
        return ap.rearrange("p a b -> p (a b)")

    def spans(ap):
        return [ap[:, 0:2 * CW].rearrange("p (c n) -> p c n", c=2), ap[:, 2 * CW:T]]

    def pspans(n):
        s = pset(n)
        return [s[:, 0:2, 0:CW], s[:, 2, 0:T - 2 * CW]]

    def pieces(ap):
        return [ap[:, 0:2 * CW].rearrange("p (c n) -> p c n", c=2), ap[:, 2 * CW:SEQ],
                ap[:, SEQ:T].rearrange("p (b l) -> p b l", b=DEC_B)]

    def ppieces(n):
        s = pset(n)
        return [s[:, 0:2, 0:CW], s[:, 2, 0:TAIL],
                s[:, 2, TAIL:TAIL + N_SAMPLE].rearrange("p (b l) -> p b l", b=DEC_B)]

    def epieces(ext, head):
        return [ext[:, head:head + 2 * CW].rearrange("p (c n) -> p c n", c=2), ext[:, head + 2 * CW:head + SEQ],
                eseq(ext, head, head)]

    def eseq(ext, head, first):
        s = ext[:, head + SEQ:head + SEQ + DEC_B * (head + DEC_L)].rearrange("p (b l) -> p b l", b=DEC_B)
        return s[:, :, first:first + DEC_L]

    def eheads(ext, head):
        s = ext[:, head + SEQ:head + SEQ + DEC_B * (head + DEC_L)].rearrange("p (b l) -> p b l", b=DEC_B)
        return s[:, :, 0:head]

    def vb(row, kt):
        return vec_b[:, 4 * row + kt:4 * row + kt + 1]

    def vbd(row, kt):
        return vec_b[:, bass.ds(kt + 4 * row, 1)]

    def va(row, ct):
        return vec_a[:, 4 * row + ct:4 * row + ct + 1]

    ready = [S("acc0_ready"), S("acc1_ready")]
    drained = [S("acc0_drained"), S("acc1_drained")]
    aux_ready, aux_drained = S("aux_ready"), S("aux_drained")
    w_in_dram = [S("w_raw0"), S("w_raw1")]
    w_hi_done, w_split, w_begun = S("w_hi_done"), S("w_split"), S("w_begun")
    act_step, dve_step, pool_step = S("act_step"), S("dve_step"), S("pool_step")
    ident_ready, ones_ready, zeros_ready = S("ident_ready"), S("ones_ready"), S("zeros_ready")
    x_in = [S(f"x_in{i}") for i in range(4)]
    setup_in, vec_in, bd_in, ws_masked = S("setup_in"), S("vec_in"), S("bd_in"), S("ws_masked")
    sq_done, var_done, std_done, xn_ready = S("sq_done"), S("var_done"), S("std_done"), S("xn_ready")
    hhi_done, hlo_done = S("hhi_done"), S("hlo_done")
    late_in, pw_in = S("late_in"), S("pw_in")
    outs = [S("ring_out0"), S("ring_out1")]
    ring_full = S("ring_full")
    state_out = S("state_out")
    v_gelu, v_var, v_std, v_norm = S("v_gelu"), S("v_var"), S("v_std"), S("v_norm")
    sgu_out, conv_done = S("sgu_out"), S("conv_done")
    tails_ready, pool_in_ready = S("tails_ready"), S("pool_in_ready")
    win_a = S("win_a")
    kv_stored, cdma = S("kv_stored"), S("cdma")
    dn_mean, dn_sq, dn_acc, dn_var, dn_std, dn_rstd, dn_y, dn_out = (
        S("dn_mean"), S("dn_sq"), S("dn_acc"), S("dn_var"), S("dn_std"), S("dn_rstd"), S("dn_y"), S("dn_out"))
    stage_in, br_hi_done, br_lo_done = S("stage_in"), S("br_hi_done"), S("br_lo_done")
    gated, mv_hi_done, mv_lo_done = S("gated"), S("mv_hi_done"), S("mv_lo_done")
    xres_in = [S(f"xres_in{i}") for i in range(4)]
    scaled, xs_hi_done, xs_lo_done, res_sq, sumsq = (
        S("scaled"), S("xs_hi_done"), S("xs_lo_done"), S("res_sq"), S("sumsq"))
    r_var, r_std, r_ready = S("r_var"), S("r_std"), S("r_ready")
    kv_in = [S(f"kv_in{i}") for i in range(4)]
    at_t, at_kh, at_kl, at_vh, at_vl = S("at_t"), S("at_kh"), S("at_kl"), S("at_vh"), S("at_vl")
    ks_a, ks_d, hid_hi = S("ks_a"), S("ks_d"), S("hid_hi")
    sc_ready, mx_ready, e_ready, rs_ready, p_ready, pt_ready, pt_hi_done, pt_lo_done, pv_ready, o_hi, o_lo = (
        S("sc_ready"), S("mx_ready"), S("e_ready"), S("rs_ready"), S("p_ready"), S("pt_ready"), S("pt_hi_done"),
        S("pt_lo_done"), S("pv_ready"), S("o_hi"), S("o_lo"))
    qm_ready, ks_t, ks_done, ss_ready, ss_used = S("qm_ready"), S("ks_t"), S("ks_done"), S("ss_ready"), S("ss_used")
    sm_mx, sm_e, sm_p, sm_t, sm_pt, so_ready, so_copied, so_t, so_hi, so_lo = (
        S("sm_mx"), S("sm_e"), S("sm_p"), S("sm_t"), S("sm_pt"), S("so_ready"), S("so_copied"), S("so_t"),
        S("so_hi"), S("so_lo"))
    ptm_zero = S("ptm_zero")
    relu_done, hid_ready = S("relu_done"), S("hid_ready")
    fst_ready, fs_sq, fs_var, fs_std, fs_r, fs_gain, y_even, y_odd = (
        S("fst_ready"), S("fs_sq"), S("fs_var"), S("fs_std"), S("fs_r"), S("fs_gain"), S("y_even"), S("y_odd"))
    y_out = [S(f"y_out{i}") for i in range(4)]
    gf_in = S("gf_in")

    xt_dram, br_dram, kv_dram = scratch["xt"], scratch["branch"], scratch["kv"]
    w_in = a["w_in"][0].rearrange("(k p) n -> p k n", p=P)
    w_branch = a["w_branch"][0].rearrange("b (k p) n -> b p k n", p=P)
    w_sq = {k: a[k][0].rearrange("(k p) n -> p k n", p=P) for k in ("w_mix_out", "w_xq", "w_xk", "w_xv", "w_xo", "w_ff1")}
    w_ff2 = a["w_ff2"][0].rearrange("(c k p) n -> c p k n", p=P, k=KT)
    x_prompt = a["x_prompt"][0]
    x_sample = a["x_sample"].rearrange("b l d -> (b l) d")
    mem = a["mem_prompt"][0]

    def x_rows(t):
        if t < 8:
            return x_prompt[P * t:P * t + P, :]
        return x_sample if t == 8 else mem[P * (t - 9):P * (t - 8), :]

    def x_height(t):
        return N_SAMPLE if t == 8 else P

    def hsplit(t):
        if t < 9:
            t0, tw = TOK_TILES[t]
            return h_hi[:, :, t0:t0 + tw], h_lo[:, :, t0:t0 + tw]
        m0 = (t - 9) * P
        return mem_hi[:, :, m0:m0 + P], mem_lo[:, :, m0:m0 + P]

    def scaled_tile(t):
        if t < 9:
            return drained[(N_P0 + t) % 2], (N_P0 + t) // 2 + 1
        return aux_drained, AUX[f"m{t - 9}"] + 1

    def tile_psum(t):
        return flat(PS[:, 6:8, :]) if t >= 9 else flat(pset(N_P0 + t)[:, 0:2, :])

    def tile_transposed(t):
        if t < 9:
            return ready[(N_P0 + t) % 2], (N_P0 + t) // 2 + 1
        return aux_ready, AUX[f"m{t - 9}"] + 1

    def stage_of(q):
        return vring[:, 1, :] if q == 0 else tmp[0][:, :]

    SETUP, VECTORS = 16 * 6, 16 * 11

    block = ctx.enter_context(nc.Block())

    @block.sync
    def _(sp):
        def slab(z, src, i=None, per=0, kts=KT):
            if i is not None or z >= 2:
                sp.wait_ge(w_split, 2 * (z - 1) if i is None else i * (2 * per) + 2 * (z - 1))
            dst = w_raw[:, z % 2, :].rearrange("p (k n) -> p k n", k=kts)
            sp.dma_start(dst, src).then_inc(w_in_dram[z % 2], 16)

        def load_x(n, t):
            if n >= 4:
                m = n - 4
                if m < 11:
                    sp.wait_ge(xn_ready, m + 1)
                else:
                    sp.wait_ge(aux_ready, AUX[f"x{m - 11}"] + 1)
            sp.dma_start(xring[0:x_height(t), n % 4, :], x_rows(t)).then_inc(x_in[n % 4], 16)

        for n in range(4):
            load_x(n, n)

        def load(dst, src):
            sp.dma_start(dst, src, allow_slow_non_contiguous=True).then_inc(setup_in, 16)

        load(ws_raw[:, :, :], a["sgu_w"][0].rearrange("g t s -> t g s"))
        load(pl_raw[:, :], a["state_pool"][0].rearrange("b l w -> (b l) w"))
        load(sc_raw[:, :], a["state_sconv"][0].rearrange("b l w -> (b l) w"))
        load(cc_raw[:, :, :], a["state_cconv"][0].rearrange("(h b) l w -> (b l) h w", h=2))
        load(pool_wt[:, :, :], a["pool_w"][0].rearrange("g i j -> i g j"))
        load(bias_s[:, :, :], a["sgu_b"][0].unsqueeze(0).broadcast_to([P, HEADS, P]))
        for j in range(2):
            slab(S_CV + j, w_in[:, :, (IN_CV + j) * P:(IN_CV + j + 1) * P])
        for n in range(4, 11):
            load_x(n, n)
        for n in range(11, 20):
            load_x(n, n - 11)
            if n in (13, 15):
                j = (n - 13) // 2 + 2
                slab(S_CV + j, w_in[:, :, (IN_CV + j) * P:(IN_CV + j + 1) * P])
        for ct in range(CT):
            for j, col in enumerate((IN_DB, IN_DA)):
                slab(S_D + 4 * ct + 2 * j, w_in[:, :, (col + ct) * P:(col + ct + 1) * P])
                g, q = ct // 2, 2 * (ct % 2) + j
                slab(S_D + 4 * ct + 2 * j + 1, w_sq["w_xk"][:, 2 * q:2 * q + 2, W_BR * g:W_BR * g + W_BR], kts=2)
        for ct in range(CT):
            slab(S_CU + 3 * ct, w_in[:, :, (IN_CU + ct) * P:(IN_CU + ct + 1) * P])
            for j in range(2):
                g, q = ct // 2, 2 * (ct % 2) + j
                slab(S_CU + 3 * ct + 1 + j, w_sq["w_xv"][:, 2 * q:2 * q + 2, W_BR * g:W_BR * g + W_BR], kts=2)
        for ct in range(CT):
            slab(S_A + ct, w_in[:, :, (IN_A + ct) * P:(IN_A + ct + 1) * P])
        for ct in range(CT):
            for j, col in enumerate((IN_BH, IN_BC, IN_BB)):
                slab(S_B + 3 * ct + j, w_in[:, :, (col + ct) * P:(col + ct + 1) * P])

        def gate_slabs(q, k, i=None, step=0):
            for j, (what, mm) in enumerate((("g", 0), ("g", 1), ("p", 0), ("g", 2), ("g", 3), ("p", 2))):
                z = S_GATE + 12 * q + 6 * step + j
                col = (4 * step + mm) * P + ((IN_G + 8 * k) * P if what == "g" else 0)
                if i is not None:
                    col = sp.snap(i * 4 * P + col)
                if what == "g":
                    slab(z, w_in[:, :, bass.ds(col, P)], i, 6)
                else:
                    slab(z, w_branch[k][:, :, bass.ds(col, 2 * P)], i, 6, kts=CT)

        for q, k in enumerate(BRANCHES):
            if k == 0:
                for step in range(2):
                    gate_slabs(q, k, step=step)
            else:
                with sp.Fori(0, 2) as i:
                    gate_slabs(q, k, i)

        def square(z0, w, m0, m1):
            with sp.Fori(0, (m1 - m0) // 2) as i:
                for j in range(2):
                    col = sp.snap(i * 2 * P + (m0 + j) * P)
                    slab(z0 + m0 + j, w[:, :, bass.ds(col, P)], i, 2)

        square(S_MIX, w_sq["w_mix_out"], 0, 2)
        n = N_GATE + 62
        sp.wait_ge(ready[n % 2], n // 2 + 1)
        for i in range(4):
            sp.dma_start(x_res[:, 2 * i:2 * i + 2, :],
                         xt_dram[2 * i:2 * i + 2].rearrange("k p t -> p k t")).then_inc(xres_in[i], 16)
        square(S_MIX, w_sq["w_mix_out"], 2, 8)
        square(S_Q, w_sq["w_xq"], 0, 8)

        def kv_load(n):
            if n < 2:
                src = kv_dram[n]
            else:
                name = "cache_mem_k" if n < 10 else "cache_mem_v"
                src = a[name][0, (n - 2) % 8].rearrange("m h d -> m (h d)")
            sp.dma_start(kvring[:, n % 4, :].rearrange("p (m d) -> p m d", m=MT),
                         src.rearrange("(m p) d -> p m d", p=P)).then_inc(kv_in[n % 4], 16)

        n = N_Q + 7
        sp.wait_ge(ready[n % 2], n // 2 + 1)
        sp.wait_ge(kv_stored, 8 * 16)
        for n in range(4):
            kv_load(n)
        square(S_XO, w_sq["w_xo"], 0, 2)
        for n in (5, 4, *range(6, 18)):
            if n == 4:
                sp.wait_ge(pv_ready, 16)
            elif n == 5:
                sp.wait_ge(at_vl, 1)
            elif n < 14:
                sp.wait_ge(ks_t, n - 5)
            else:
                sp.wait_ge(so_ready, n - 13)
            kv_load(n)
        square(S_XO, w_sq["w_xo"], 2, 8)
        for c in range(4):
            square(S_FF + 16 * c, w_sq["w_ff1"][:, :, c * D_MODEL:(c + 1) * D_MODEL], 0, 8)
            square(S_FF + 16 * c + 8, w_ff2[c], 0, 8)
        n = N_FF + 16 * 3 + 7
        sp.wait_ge(ready[n % 2], n // 2 + 1)
        sp.dma_start(gf[:, :], a["norm_f_g"].unsqueeze(0).broadcast_to([P, D_MODEL])).then_inc(gf_in, 16)
        for t, (t0, tw) in enumerate(TOK_TILES):
            sp.wait_ge((y_even, y_odd)[t % 2], t // 2 + 1)
            dst = o["y_prompt"][0][t0:t0 + tw, :] if t < 8 else o["y_sample"].rearrange("b l d -> (b l) d")
            sp.dma_start(dst, y_tok[0:tw, t, :]).then_inc(y_out[t % 4], 16)
        for j in range(4):
            sp.wait_ge(y_out[j], 16 * len(range(j, 9, 4)))

    @block.gpsimd
    def _(pool):
        chain = Chain(pool, pool_step)
        pool.wait_ge(ones_ready, 1)
        chain.link(nc.gpsimd.memset(ident[:, :], 0.0))
        nc.gpsimd.affine_select(out=ident[:, :], in_=ident[:, :], compare_op=ALU.not_equal, fill=1.0, base=0,
                                pattern=[[-1, P]], channel_multiplier=1).then_inc(ident_ready, 1)
        chain.link(nc.gpsimd.memset(bd_raw[:, :, :], 0.0))
        pool.wait_ge(pool_step, 2)
        for b in range(DEC_B):
            pool.dma_start(bd_raw[8 * b:8 * b + 8, :, 8 * b:8 * b + 8],
                           a["sgu_w"][0, :, 0:8, 0:8].rearrange("g t s -> t g s"),
                           allow_slow_non_contiguous=True).then_inc(bd_in, 16)
        pool.wait_ge(bd_in, 16 * DEC_B)
        pool.wait_ge(setup_in, SETUP)
        nc.gpsimd.affine_select(out=ws_raw[:, :, :], in_=ws_raw[:, :, :], compare_op=ALU.is_ge, fill=0.0, base=0,
                                pattern=[[0, HEADS], [-1, P]], channel_multiplier=1).then_inc(ws_masked, 1)
        nc.gpsimd.affine_select(out=bd_raw[:, :, :], in_=bd_raw[:, :, :], compare_op=ALU.is_ge, fill=0.0, base=0,
                                pattern=[[0, HEADS], [-1, N_SAMPLE]], channel_multiplier=1).then_inc(ws_masked, 1)

        def split(z, i=None):
            pool.wait_ge(w_in_dram[z % 2], 16 * (z // 2 + 1) if i is None else i * 16 + 16 * (z // 2 + 1))
            if i is not None:
                pool.wait_ge(w_begun, i * 2 + z)
            for half in range(2):
                cols = slice(512 * half, 512 * half + 512)
                nc.gpsimd.tensor_tensor(w_hi[:, z % 2, cols], w_raw[:, z % 2, cols],
                                        ones[:, 0:1].broadcast_to([P, 512]), ALU.mult).then_inc(w_hi_done, 1)
                count = 2 * z + half + 1
                pool.wait_ge(w_hi_done, count if i is None else i * 4 + count)
                nc.gpsimd.tensor_tensor(w_lo[:, z % 2, cols], w_raw[:, z % 2, cols],
                                        w_hi[:, z % 2, cols].bitcast(F32), ALU.subtract).then_inc(w_split, 1)

        split(0)
        for t in range(11):
            pool.wait_ge(hhi_done, t + 1)
            pool.wait_ge(*scaled_tile(t))
            hi, lo = hsplit(t)
            fb = fbuf[:, t % 2, 0:KT * x_height(t)].rearrange("p (k n) -> p k n", k=KT)
            nc.gpsimd.tensor_tensor(lo, fb, hi.bitcast(F32), ALU.subtract).then_inc(hlo_done, 1)
            if t == 8:
                split(1)
        with pool.Fori(0, S_END // 2 - 1) as i:
            for j in range(2):
                split(2 + j, i)

    @block.tensor
    def _(pe):
        tr = nc.tensor.transpose
        mmul = nc.tensor.matmul

        def take(n, i=None, per=0):
            if i is None:
                if n >= 2:
                    pe.wait_ge(drained[n % 2], n // 2)
            else:
                pe.wait_ge(drained[n % 2], i * (per // 2) + n // 2)

        def take_aux(name):
            if AUX[name] > 0:
                pe.wait_ge(aux_drained, AUX[name])

        def terms(slot, ofs, r_hi, r_lo):
            wh, wl = w_hi[:, slot, ofs:ofs + P], w_lo[:, slot, ofs:ofs + P]
            return ((wh, r_hi), (wh, r_lo), (wl, r_hi))

        def wait_half(z, half, i=None, per_z=0):
            count = 2 * z + half + 1
            pe.wait_ge(w_split, count if i is None else i * (2 * per_z) + count)

        def product(n, z, r_hi, r_lo, i=None, per_n=0, per_z=0, kts=KT, ofs=None, wait_slab=True, arrive=None,
                    between=None, signal=True):
            take(n, i, per_n)
            acc = pset(n)
            first = wait_slab
            for kt in range(kts):
                if wait_slab and kt in (0, kts // 2):
                    wait_half(z, int(kt > 0), i, per_z)
                if arrive is not None:
                    pe.wait_ge(arrive[0], arrive[1] + kt + 1)
                o0 = kt * P if ofs is None else ofs(kt)
                for e, (w, r) in enumerate(terms(z % 2, o0, r_hi, r_lo)):
                    for c, (c0, cw) in enumerate(CHUNKS):
                        mm = mmul(acc[:, c, 0:cw], w, r[:, kt, c0:c0 + cw],
                                  start=(kt == 0 and e == 0), stop=(kt == kts - 1 and e == 2))
                        if first:
                            mm.then_inc(w_begun, 1)
                            first = False
                if kt == kts - 1 and signal:
                    mm.then_inc(ready[n % 2], 1)
                if between and kt in between:
                    for work in between[kt]:
                        work()

        def ones_sum(n, tiles, wait):
            take(n)
            pe.wait_ge(*wait)
            for c, (c0, cw) in enumerate(CHUNKS):
                for j, tl in enumerate(tiles):
                    mm = mmul(pset(n)[:, c, 0:cw], ones[:, 0:1].broadcast_to([P, P]), tl[:, c0:c0 + cw],
                              start=(j == 0), stop=(j == len(tiles) - 1))
            mm.then_inc(ready[n % 2], 1)

        def square_sum(name, n, count):
            take_aux(name)
            pe.wait_ge(sumsq, count)
            for c in range(3):
                dst = PS[:, 6 + c, :] if c < 2 else pset(n)[:, 2, CW:CW + N_SAMPLE]
                mm = mmul(dst, ones[:, 0:1].broadcast_to([P, P]), tmp[0][:, 512 * c:min(512 * c + 512, T)],
                          start=True, stop=True)
                if c == 1:
                    mm.then_inc(aux_ready, 1)
            mm.then_inc(ready[n % 2], 1)

        def kv_group(name, z, quarter):
            if quarter == 0:
                take_aux(name)
                pe.wait_ge(hlo_done, 11)
            for kk in range(2):
                wait_half(z, kk)
                kt = 2 * quarter + kk
                for e, (m, w) in enumerate(((mem_hi, w_hi), (mem_lo, w_hi), (mem_hi, w_lo))):
                    for mt in range(MT):
                        mm = mmul(PS[:, 6 + mt, :], m[:, kt, mt * P:(mt + 1) * P],
                                  w[:, z % 2, kk * W_BR:(kk + 1) * W_BR],
                                  start=(kt == 0 and e == 0), stop=(kt == KT - 1 and e == 2))
                        if kk == 0 and e == 0 and mt == 0:
                            mm.then_inc(w_begun, 1)
            if quarter == 3:
                mm.then_inc(aux_ready, 1)

        def x_transposed(t):
            name = f"x{t}"
            take_aux(name)
            n = 11 + t
            pe.wait_ge(x_in[n % 4], 16 * (n // 4 + 1))
            h = x_height(t)
            for kt in range(KT):
                mm = tr(flat(PS[:, 6:8, :])[:, kt * h:kt * h + h], xring[0:h, n % 4, kt * P:(kt + 1) * P],
                        ident[0:h, 0:h])
            mm.then_inc(aux_ready, 1)

        def v_prompt(g):
            take_aux(f"v{g}a")
            pe.wait_ge(drained[(N_CV + g) % 2], (N_CV + g) // 2 + 1)
            for t in range(8):
                mm = tr(flat(PS[:, 6:8, :])[:, t * P:(t + 1) * P], vring[:, g % 2, t * P:(t + 1) * P], ident[:, :])
            mm.then_inc(aux_ready, 1)

        def v_sample(g):
            take_aux(f"v{g}b")
            tr(PS[0:N_SAMPLE, 6, 0:P], vring[:, g % 2, SEQ:T], ident[:, :]).then_inc(aux_ready, 1)

        def tails(name, head, count):
            take_aux(name)
            pe.wait_ge(tails_ready, count)
            for ct in range(CT):
                tr(PS[0:N_SAMPLE, 6, ct * P:(ct + 1) * P], tailbuf[:, ct, CCONV_H:], ident[:, :])
                mm = tr(PS[0:head, 7, ct * P:(ct + 1) * P], tailbuf[:, ct, 0:head], ident[:, :])
            mm.then_inc(aux_ready, 1)

        def normalised(t):
            if t < 9:
                take(N_P0 + t)
            else:
                take_aux(f"m{t - 9}")
            pe.wait_ge(xn_ready, t + 1)
            h = x_height(t)
            for kt in range(KT):
                mm = tr(tile_psum(t)[:, kt * h:kt * h + h], xn[0:h, t % 2, kt * P:(kt + 1) * P], ident[0:h, 0:h])
            mm.then_inc(tile_transposed(t)[0], 1)

        pe.wait_ge(ident_ready, 1)
        for t in range(9):
            normalised(t)
            if t == 0:
                pe.wait_ge(vec_in, VECTORS)
                nv = VA_N + VB_N
                for ct in range(CT):
                    mm = tr(PS[:, 6, ct * nv:(ct + 1) * nv], vec_raw[:, ct * P:(ct + 1) * P], ident[0:nv, 0:nv])
                mm.then_inc(aux_ready, 1)
            if t == 1:
                take_aux("ws")
                pe.wait_ge(ws_masked, 2)
                for g in range(HEADS):
                    tr(PS[:, 6, g * P:(g + 1) * P], ws_raw[:, g, :], ident[:, :])
                    mm = tr(PS[0:N_SAMPLE, 7, g * N_SAMPLE:(g + 1) * N_SAMPLE], bd_raw[:, g, :],
                            ident[0:N_SAMPLE, 0:N_SAMPLE])
                mm.then_inc(aux_ready, 1)
            if t == 3:
                take_aux("pl")
                pe.wait_ge(setup_in, SETUP)
                for ct in range(CT):
                    tr(PS[:, 6, ct * 120:(ct + 1) * 120], pl_raw[:, ct * P:(ct + 1) * P], ident[0:120, 0:120])
                    mm = tr(PS[:, 7, ct * 16:(ct + 1) * 16], sc_raw[:, ct * P:(ct + 1) * P], ident[0:16, 0:16])
                mm.then_inc(aux_ready, 1)

        def conv_states():
            take_aux("cc")
            for half in range(2):
                for ct in range(CT):
                    mm = tr(PS[:, 6 + half, ct * 120:(ct + 1) * 120], cc_raw[:, half, ct * P:(ct + 1) * P],
                            ident[0:120, 0:120])
            mm.then_inc(aux_ready, 1)

        def token_major(g):
            return {1: [lambda: x_transposed(2 * g)], 3: [lambda: v_prompt(g - 1)], 5: [lambda: v_sample(g - 1)],
                    6: [lambda: x_transposed(2 * g + 1)] if g < HEADS else []}

        pe.wait_ge(hlo_done, 9)
        for g in range(HEADS):
            between = token_major(g) if g else {
                0: [lambda: normalised(9)], 2: [lambda: normalised(10)], 4: [conv_states],
                5: [lambda: x_transposed(0)], 7: [lambda: x_transposed(1)]}
            product(N_CV + g, S_CV + g, h_hi, h_lo, between=between)
        for ct in range(CT):
            for j in range(2):
                product(N_D + 2 * ct + j, S_D + 4 * ct + 2 * j, h_hi, h_lo,
                        between=token_major(HEADS) if ct == 0 and j == 0 else None)
                kv_group(f"K{ct // 2}", S_D + 4 * ct + 2 * j + 1, 2 * (ct % 2) + j)
        for g in range(HEADS):
            product(N_CU + 2 * g, S_CU + 3 * g, h_hi, h_lo)
            if g == 0:
                tails("tail_d", CCONV_H, CT)
            for j in range(2):
                kv_group(f"V{g // 2}", S_CU + 3 * g + 1 + j, 2 * (g % 2) + j)
            n = N_CU + 2 * g + 1
            take(n)
            pe.wait_ge(v_norm, 9)
            acc = flat(pset(n))
            for t in range(8):
                mmul(acc[:, t * P:(t + 1) * P], v_tok[:, t, g * P:(g + 1) * P], ws_t[:, g, :], start=True, stop=True)
            mmul(acc[:, SEQ:T], v_tok[0:N_SAMPLE, 8, g * P:(g + 1) * P], bd_t[:, g, :],
                 start=True, stop=True).then_inc(ready[n % 2], 1)
        def pool_map(g):
            n = N_A_MAP[g]
            take(n)
            pe.wait_ge(pool_in_ready, g + 1)
            for c, (c0, cw) in enumerate(CHUNKS):
                mm = mmul(pset(n)[:, c, 0:cw], pool_wt[:, g, :], pooled[:, c0:c0 + cw], start=True, stop=True)
            mm.then_inc(ready[n % 2], 1)

        for g in range(CT):
            product(N_A_IN[g], S_A + g, h_hi, h_lo)
            if g >= 1:
                pool_map(g - 1)
        for ct in range(CT):
            product(N_B_H[ct], S_B + 3 * ct, h_hi, h_lo)
            if ct == 0:
                pool_map(CT - 1)
                tails("tail_a", POOL_H, 2 * CT)
            if ct == 2:
                ones_sum(N_VAR, [tmp[2]], (dn_acc, CT - 1))
            product(N_B_C[ct], S_B + 3 * ct + 1, h_hi, h_lo)
            if ct == 1:
                ones_sum(N_MEAN, [slots_d[:, c, 0:T] for c in range(CT)], (conv_done, CT))
            product(N_B_B[ct], S_B + 3 * ct + 2, h_hi, h_lo)

        tails("tail_b", SCONV_H, 3 * CT)
        for q in range(4):
            bh, bl = br_hi[q % 2], br_lo[q % 2]
            with pe.Fori(0, 2) as i:
                for pair in range(2):
                    z = S_GATE + 12 * q + 3 * pair
                    n = N_GATE + 16 * q + 4 * pair
                    for j in range(2):
                        product(n + j, z + j, h_hi, h_lo, i, 8, 6)
                    pe.wait_ge(br_lo_done, 4 * q + 4)
                    for j in range(2):
                        product(n + 2 + j, z + 2, bh, bl, i, 8, 6, kts=CT,
                                ofs=lambda kt, j=j: (2 * kt + j) * P, wait_slab=(j == 0))

        def products(n0, z0, m0, m1, r_hi, r_lo):
            with pe.Fori(0, (m1 - m0) // 2) as i:
                for j in range(2):
                    product(n0 + m0 + j, z0 + m0 + j, r_hi, r_lo, i, 2, 2)

        product(N_MIX, S_MIX, mv_hi, mv_lo, arrive=(mv_lo_done, 0))
        product(N_MIX + 1, S_MIX + 1, mv_hi, mv_lo)
        products(N_MIX, S_MIX, 2, 8, mv_hi, mv_lo)
        product(N_Q, S_Q, xs_hi, xs_lo, arrive=(xs_lo_done, 0), signal=False)
        square_sum("sum0", N_Q, KT + 1)
        product(N_Q + 1, S_Q + 1, xs_hi, xs_lo)
        products(N_Q, S_Q, 2, 8, xs_hi, xs_lo)

        for st in range(2):
            n = N_Q + 7 - (N_Q + 7 - st) % 2
            pe.wait_ge(drained[st], n // 2 + 1)
        pe.wait_ge(kv_in[0], 16)
        for g in range(4):
            if g >= 2:
                pe.wait_ge(at_kl, g - 1)
            for kk in range(2):
                for mt in range(MT):
                    kt = 2 * g + kk
                    mm = tr(PS[:, 4 + g % 2, (2 * kk + mt) * P:(2 * kk + mt + 1) * P],
                            kvring[:, 0, mt * D_MODEL + kt * P:mt * D_MODEL + (kt + 1) * P], ident[:, :])
            mm.then_inc(at_t, 1)
        pe.wait_ge(at_kl, 4)
        pe.wait_ge(mv_lo_done, 2 * KT)

        def score(u):
            h, tk = u // 8, u % 8
            if u >= 4:
                pe.wait_ge(e_ready, u - 3)
            for dt in range(2):
                d = 2 * h + dt
                for e, (q_, k_) in enumerate(((mv_hi, kt_hi), (mv_lo, kt_hi), (mv_hi, kt_lo))):
                    mm = mmul(PS[:, u % 4, 0:N_MEM], q_[:, d, tk * P:(tk + 1) * P], k_[:, d, :],
                              start=(dt == 0 and e == 0), stop=(dt == 1 and e == 2))
            mm.then_inc(sc_ready, 1)

        for u in range(3):
            score(u)
        def attend(G):
            h = G // 2
            pe.wait_ge(pt_lo_done, 4 * G + 4)
            pe.wait_ge(at_vl, 1)
            if G >= 1:
                pe.wait_ge(o_lo, 2 * G)
            for dt in range(2):
                for mt in range(MT):
                    for e, (v_, p_) in enumerate(((v_hi, pt_hi), (v_lo, pt_hi), (v_hi, pt_lo))):
                        d0 = h * HEAD_DIM + dt * P
                        mm = mmul(PS[:, 6 + dt, :], v_[:, mt, d0:d0 + P], p_[G % 2][:, mt, :],
                                  start=(mt == 0 and e == 0), stop=(mt == 1 and e == 2))
                mm.then_inc(pv_ready, 1)

        for u in range(32 + 3):
            if u + 3 < 32:
                score(u + 3)
            if u < 32:
                pe.wait_ge(p_ready, u + 1)
                if u >= 2:
                    pe.wait_ge(pt_lo_done, u - 1)
                for mt in range(MT):
                    mm = tr(PS[:, 4 + u % 2, mt * P:(mt + 1) * P], probs[:, u % 4, mt * P:(mt + 1) * P],
                            ident[:, :])
                mm.then_inc(pt_ready, 1)
            if u >= 6 and u % 4 == 2:
                attend((u - 6) // 4)

        def sample_scores(b):
            pe.wait_ge(ks_a, b + 1)
            pe.wait_ge(ks_d, b + 1)
            pe.wait_ge(qm_ready, b + 1)
            for h in range(HEADS):
                for dt in range(2):
                    d = 2 * h + dt
                    mm = mmul(PS[0:N_SAMPLE, 4 + h, 0:N_MEM], qm[b % 4][:, d * N_SAMPLE:(d + 1) * N_SAMPLE],
                              kt_s[:, b % 2, d, :], start=(b == 0 and dt == 0), stop=(b == 7 and dt == 1))
            mm.then_inc(ss_ready, 1)

        pe.wait_ge(e_ready, 32)
        for b in range(DEC_B):
            n = 2 + b
            pe.wait_ge(kv_in[n % 4], 16 * (n // 4 + 1))
            if b >= 1:
                pe.wait_ge(ks_a, b)
                pe.wait_ge(ks_d, b)
            for kt in range(KT):
                for mt in range(MT):
                    mm = tr(PS[:, kt // 2, (2 * (kt % 2) + mt) * P:(2 * (kt % 2) + mt + 1) * P],
                            kvring[:, n % 4, mt * D_MODEL + kt * P:mt * D_MODEL + (kt + 1) * P], ident[:, :])
            mm.then_inc(ks_t, 1)
            if b == 0:
                pe.wait_ge(o_lo, 16)
                pe.wait_ge(pt_lo_done, 32)
            else:
                sample_scores(b - 1)
        sample_scores(DEC_B - 1)
        pe.wait_ge(sm_p, 1)
        for j in range(2 * HEADS):
            mm = tr(PS[:, 0, j * N_SAMPLE:(j + 1) * N_SAMPLE], p_s[:, j * P:(j + 1) * P],
                    ident[0:N_SAMPLE, 0:N_SAMPLE])
        mm.then_inc(sm_t, 1)
        for b in range(DEC_B):
            n = 10 + b
            pe.wait_ge(kv_in[n % 4], 16 * (n // 4 + 1))
            if b == 0:
                pe.wait_ge(sm_pt, 1)
            for h in range(HEADS):
                for mt in range(MT):
                    j = 2 * h + mt
                    v0 = mt * D_MODEL + h * HEAD_DIM
                    mm = mmul(PS[0:N_SAMPLE, 4 + h, 0:HEAD_DIM], ptm[:, b, j * N_SAMPLE:(j + 1) * N_SAMPLE],
                              kvring[:, n % 4, v0:v0 + HEAD_DIM], start=(b == 0 and mt == 0),
                              stop=(b == 7 and mt == 1))
            mm.then_inc(so_ready, 1)
        pe.wait_ge(so_copied, 1)
        for kt in range(KT):
            mm = tr(PS[:, 1, kt * N_SAMPLE:(kt + 1) * N_SAMPLE], p_s[:, kt * P:(kt + 1) * P],
                    ident[0:N_SAMPLE, 0:N_SAMPLE])
        mm.then_inc(so_t, 1)

        pe.wait_ge(so_lo, 1)
        products(N_XO, S_XO, 0, 8, mv_hi, mv_lo)
        for c in range(4):
            n1, n2, z = N_FF + 16 * c, N_FF + 16 * c + 8, S_FF + 16 * c
            if c == 0:
                product(n1, z, xs_hi, xs_lo, arrive=(xs_lo_done, KT), signal=False)
                square_sum("sum1", n1, 2 * KT + 2)
                product(n1 + 1, z + 1, xs_hi, xs_lo)
                products(n1, z, 2, 8, xs_hi, xs_lo)
            else:
                products(n1, z, 0, 8, xs_hi, xs_lo)
            product(n2, z + 8, mv_hi, mv_lo, arrive=(hid_ready, KT * c))
            product(n2 + 1, z + 9, mv_hi, mv_lo)
            if c < 3:
                products(n2, z + 8, 2, 8, mv_hi, mv_lo)

        def y_prompt_rows(m):
            n = N_FF + 16 * 3 + 8 + m
            take_aux(f"y{m}a")
            pe.wait_ge(drained[n % 2], n // 2 + 1)
            for t in range(8):
                mm = tr(flat(PS[:, 6:8, :])[:, t * P:(t + 1) * P], x_res[:, m, t * P:(t + 1) * P], ident[:, :])
            mm.then_inc(aux_ready, 1)

        def y_sample_rows(m):
            take_aux(f"y{m}b")
            tr(PS[0:N_SAMPLE, 6, 0:P], x_res[:, m, SEQ:T], ident[:, :]).then_inc(aux_ready, 1)

        for m in range(2, KT):
            between = {1: [lambda: y_prompt_rows(m - 1)], 4: [lambda: y_sample_rows(m - 1)]}
            if m == 2:
                between = {1: [lambda: y_prompt_rows(0)], 3: [lambda: y_sample_rows(0)],
                           5: [lambda: y_prompt_rows(1)], 7: [lambda: y_sample_rows(1)]}
            product(N_FF + 56 + m, S_FF + 56 + m, mv_hi, mv_lo, between=between)
        y_prompt_rows(KT - 1)
        y_sample_rows(KT - 1)

    @block.scalar
    def _(act):
        chain = Chain(act, act_step)

        def copy(out, in_, **kw):
            return nc.scalar.activation(out, in_, ACT.Copy, **kw)

        def wait_ready(n, i=None, per=0):
            act.wait_ge(ready[n % 2], n // 2 + 1 if i is None else i * (per // 2) + n // 2 + 1)

        def drain(n, out, func=ACT.Copy, **kw):
            wait_ready(n)
            for s, d in zip(pspans(n), spans(out)):
                ins = nc.scalar.activation(d, s, func, **kw)
            ins.then_inc(drained[n % 2], 1)

        def load(dst, src, sem):
            act.dma_start(dst, src, allow_slow_non_contiguous=True).then_inc(sem, 16)

        def ring_free(k):
            if k >= 2:
                act.wait_ge(outs[k % 2], 16 * (k // 2))

        for name, row in (("cconv_w", VA_CCW), ("sconv_w", VA_SCW)):
            load(vec_raw[row:row + a[name].shape[1], :], a[name][0], vec_in)
        for name, row in (("pool_scale", VA_PSC), ("cconv_b", VA_CCB), ("cconv_ln_g", VA_LNG), ("cconv_ln_b", VA_LNB)):
            load(vec_raw[row:row + 1, :], a[name], vec_in)
        for name, row in (("norm_mix_g", VB_MIX), ("norm_x_g", VB_X), ("norm_ffn_g", VB_FFN), ("norm_mem_g", VB_MEM)):
            load(vec_raw[VA_N + row:VA_N + row + 2, :], a[name].rearrange("o (r c) -> (o r) c", r=2), vec_in)
        load(vec_raw[VA_N + VB_GATE:VA_N + VB_N, :], a["b_gate"][0].rearrange("b (r c) -> (b r) c", r=2), vec_in)
        def token_square(t):
            h = x_height(t)
            act.wait_ge(x_in[t % 4], 16 * (t // 4 + 1))
            if t >= 2:
                act.wait_ge(sq_done, t - 1)
            nc.scalar.activation(vring[0:h, t % 2, 0:1024], xring[0:h, t % 4, :], ACT.Square,
                                 accum_out=ss[0:h, t:t + 1]).then_inc(sq_done, 1)

        def token_root(t):
            h = x_height(t)
            act.wait_ge(var_done, t + 1)
            nc.scalar.activation(ss[0:h, t:t + 1], ss[0:h, t:t + 1], ACT.Sqrt).then_inc(std_done, 1)

        def token_hi(t):
            act.wait_ge(*scaled_tile(t))
            hi, lo = hsplit(t)
            copy(hi, fbuf[:, t % 2, 0:KT * x_height(t)].rearrange("p (k n) -> p k n", k=KT)).then_inc(hhi_done, 1)

        act.wait_ge(zeros_ready, 1)
        for s_ in range(11 + 3):
            if s_ < 11:
                token_square(s_)
            if 1 <= s_ <= 11:
                token_root(s_ - 1)
            if s_ >= 3:
                token_hi(s_ - 3)
            if s_ == 1:
                act.wait_ge(aux_ready, AUX["vec"] + 1)
                nv = VA_N + VB_N
                tables = PS[:, 6, 0:CT * nv].rearrange("p (c r) -> p r c", c=CT)
                copy(vec_a[:, :].rearrange("p (r c) -> p r c", c=CT), tables[:, 0:VA_N, :])
                copy(vec_b[:, :].rearrange("p (r c) -> p r c", c=CT), tables[:, VA_N:nv, :]).then_inc(aux_drained, 1)
            if s_ == 4:
                act.wait_ge(aux_ready, AUX["ws"] + 1)
                copy(flat(ws_t[:, :, :]), PS[:, 6, :])
                copy(flat(bd_t[:, :, :]), PS[0:N_SAMPLE, 7, 0:HEADS * N_SAMPLE]).then_inc(aux_drained, 1)
            if s_ == 6:
                act.wait_ge(aux_ready, AUX["pl"] + 1)
                copy(flat(st_pool[:, :, :]), PS[:, 6, 0:CT * 120])
                copy(flat(st_sc[:, :, :]), PS[:, 7, 0:CT * 16]).then_inc(aux_drained, 1)
                for dst, name in ((ln_g, "sgu_ln_g"), (ln_b, "sgu_ln_b")):
                    load(dst[:, :], a[name].broadcast_to([P, W_BR]), late_in)
        load(o["new_pool_sample"][0][:, 0:POOL_H - DEC_L, :], a["state_pool"][0][:, DEC_L:, :], state_out)
        load(o["new_cconv_sample"][0][:, 0:CCONV_H - DEC_L, :], a["state_cconv"][0][:, DEC_L:, :], state_out)
        act.wait_ge(hlo_done, 11)
        act.wait_ge(aux_ready, AUX["cc"] + 1)
        for half in range(2):
            for ct in range(CT):
                ins = copy(eheads(slots_d[:, ct + 1, :], CCONV_H)[:, 4 * half:4 * half + 4, :],
                           PS[:, 6 + half, ct * 120:(ct + 1) * 120].rearrange("p (b l) -> p b l", b=4))
        ins.then_inc(aux_drained, 1)

        def x_out(t):
            act.wait_ge(aux_ready, AUX[f"x{t}"] + 1)
            ring_free(t)
            t0, tw = TOK_TILES[t]
            copy(oring[:, t % 2, 0:KT * tw], flat(PS[:, 6:8, :])[:, 0:KT * tw]).then_inc(aux_drained, 1)
            act.wait_ge(aux_drained, AUX[f"x{t}"] + 1)
            act.dma_start(xt_dram[:, :, t0:t0 + tw].rearrange("k p t -> p k t"),
                          oring[:, t % 2, 0:KT * tw].rearrange("p (k t) -> p k t", k=KT)).then_inc(outs[t % 2], 16)

        def v_rows(g):
            act.wait_ge(aux_ready, AUX[f"v{g}a"] + 1)
            copy(v_tok[:, 0:8, g * P:(g + 1) * P],
                 flat(PS[:, 6:8, :]).rearrange("p (t c) -> p t c", t=8)).then_inc(aux_drained, 1)
            act.wait_ge(aux_ready, AUX[f"v{g}b"] + 1)
            copy(v_tok[0:N_SAMPLE, 8, g * P:(g + 1) * P], PS[0:N_SAMPLE, 6, 0:P]).then_inc(aux_drained, 1)

        def store_ring(k, dst, ready_sem, count):
            act.wait_ge(ready_sem, count)
            act.dma_start(dst, oring[:, k % 2, :]).then_inc(outs[k % 2], 16)

        def store_rows(aux_name, stage, head, new, out_prompt, out_sample):
            act.wait_ge(aux_ready, AUX[aux_name] + 1)
            copy(stage[:, 0, :], PS[0:N_SAMPLE, 6, :])
            copy(stage[0:head, 1, :], PS[0:head, 7, :]).then_inc(aux_drained, 1)
            act.wait_ge(aux_drained, AUX[aux_name] + 1)
            act.dma_start(out_prompt[0, 0], stage[0:head, 1, :]).then_inc(state_out, 16)
            for b in range(DEC_B):
                act.dma_start(out_sample[0, b][out_sample.shape[2] - new:, :],
                              stage[DEC_L * (b + 1) - new:DEC_L * (b + 1), 0, :]).then_inc(state_out, 16)

        def kv_rows(which, g):
            name = f"{'KV'[which]}{g}"
            act.wait_ge(aux_ready, AUX[name] + 1)
            n = 2 * which + g
            if n >= 1:
                act.wait_ge(kv_stored, 32 * n)
            copy(flat(kv_out[:, :, :]), flat(PS[:, 6:8, :])).then_inc(aux_drained, 1)
            act.wait_ge(aux_drained, AUX[name] + 1)
            out = o["mem_k_prompt" if which == 0 else "mem_v_prompt"][0, 0].rearrange("m h d -> m (h d)")
            for dst in (out, kv_dram[which]):
                act.dma_start(dst[:, g * W_BR:(g + 1) * W_BR].rearrange("(m p) c -> p m c", p=P),
                              kv_out[:, :, :]).then_inc(kv_stored, 16)

        for g in range(HEADS):
            x_out(2 * g)
            if g >= 1:
                v_rows(g - 1)
            x_out(2 * g + 1)
            drain(N_CV + g, vring[:, g % 2, :], ACT.Gelu_apprx_tanh)
        for ct in range(CT):
            n = N_D + 2 * ct
            if ct >= 1:
                act.wait_ge(drained[(n - 1) % 2], (n - 1) // 2 + 1)
            if ct == 0:
                x_out(8)
                v_rows(3)
            drain(n, tmp[2][:, :], ACT.Sigmoid)
            if ct == 0:
                act.wait_ge(v_var, 1)
                nc.scalar.activation(v_rstd, v_rstd, ACT.Sqrt).then_inc(v_std, 1)
            if ct % 2 == 1:
                kv_rows(0, ct // 2)
        for g in range(HEADS):
            if g >= 2:
                act.wait_ge(sgu_out, g - 1)
            drain(N_CU + 2 * g, vring[:, g % 2, :], ACT.Gelu_apprx_tanh)
            if g == 0:
                store_rows("tail_d", tail_d, CCONV_H, DEC_L, o["new_cconv_prompt"], o["new_cconv_sample"])
                act.dma_start(o["sgu_v_sample"][0].rearrange("b l w -> (b l) w"),
                              v_tok[0:N_SAMPLE, 8, :]).then_inc(state_out, 16)
            if g >= 1:
                store_ring(RING_C + g - 1, br_dram[2, g - 1], sgu_out, g)
            if g % 2 == 1:
                kv_rows(1, g // 2)
        act.wait_ge(kv_stored, 8 * 16)
        act.wait_ge(state_out, 16 * (2 + 9 + 1))
        def extend(g):
            n = N_A_IN[g]
            if g >= 2:
                act.wait_ge(pool_in_ready, g - 1)
            if g == 2:
                act.wait_ge(tails_ready, CT + 1)
            wait_ready(n)
            e = ext_a[:, g % 2, :]
            copy(eheads(e, POOL_H), st_pool[:, g, :].rearrange("p (b l) -> p b l", b=DEC_B))
            for s, d in zip(ppieces(n), epieces(e, POOL_H)):
                ins = copy(d, s)
            ins.then_inc(drained[n % 2], 1)

        extend(0)
        store_ring(RING_C + 3, br_dram[2, 3], sgu_out, 4)
        for g in range(CT):
            if g + 1 < CT:
                extend(g + 1)
            else:
                drain(N_B_H[0], b_h[:, :])
            ring_free(RING_A + g)
            n = N_A_MAP[g]
            drain(n, oring[:, (RING_A + g) % 2, :], scale=va(VA_PSC, g))
            store_ring(RING_A + g, br_dram[0, g], drained[n % 2], n // 2 + 1)

        def stage_load(u, i=None):
            q, ct = u // 4, u % 4
            k = BRANCHES[q]
            if i is None:
                if u >= 1:
                    act.wait_ge(br_lo_done, u)
                act.wait_ge(outs[(RING_OF[k] + ct) % 2], 16 * ((RING_OF[k] + ct) // 2 + 1))
                act.dma_start(stage_of(q), br_dram[k, ct]).then_inc(stage_in, 16)
            else:
                act.wait_ge(br_lo_done, i * 2 + u)
                src = br_dram[k][bass.ds(i * 2 + ct, 1)].rearrange("o p t -> p (o t)")
                act.dma_start(stage_of(q), src).then_inc(stage_in, 16)

        def stage_hi(u, i=None):
            q, ct = u // 4, u % 4
            if i is None:
                act.wait_ge(stage_in, 16 * (u + 1))
                copy(br_hi[q % 2][:, ct, :], stage_of(q)).then_inc(br_hi_done, 1)
            else:
                act.wait_ge(stage_in, i * 32 + 16 * (u + 1))
                copy(flat(br_hi[q % 2][:, bass.ds(i * 2 + ct, 1), :]), stage_of(q)).then_inc(br_hi_done, 1)

        for ct in range(CT):
            if ct == 0:
                store_rows("tail_a", tail_a, POOL_H, DEC_L, o["new_pool_prompt"], o["new_pool_sample"])
            else:
                n = N_B_C[ct - 1]
                act.wait_ge(drained[n % 2], n // 2 + 1)
                drain(N_B_H[ct], b_h[:, :])
            stage_load(ct)
            stage_hi(ct)
            if ct >= 1:
                store_ring(RING_B + ct - 1, br_dram[1, ct - 1], ring_full, ct)
            if ct == 1:
                act.wait_ge(dn_mean, 1)
                for c in range(CT):
                    if c >= 2:
                        act.wait_ge(dn_acc, c - 1)
                    nc.scalar.activation(tmp[2 if c == 0 else 0][:, :], slots_d[:, c, 0:T],
                                         ACT.Square).then_inc(dn_sq, 1)
            if ct == 2:
                act.wait_ge(dn_var, 1)
                nc.scalar.activation(tmp[2][:, :], tmp[2][:, :], ACT.Sqrt).then_inc(dn_std, 1)
        store_ring(RING_B + 3, br_dram[1, 3], ring_full, CT)
        for ct in range(CT):
            k = RING_D + ct
            act.wait_ge(dn_y, ct + 1)
            ring_free(k)
            nc.scalar.activation(oring[:, k % 2, :], slots_d[:, ct, 0:T], ACT.Silu, bias=va(VA_LNB, ct),
                                 scale=va(VA_LNG, ct)).then_inc(dn_out, 1)
            store_ring(k, br_dram[3, ct], dn_out, ct + 1)
        store_rows("tail_b", tail_b, SCONV_H, SCONV_H, o["new_sconv_prompt"], o["new_sconv_sample"])
        act.wait_ge(state_out, 16 * (2 + 9 + 1 + 9 + 9))
        for j in range(2):
            act.wait_ge(outs[j], 16 * len(range(j, 25, 2)))

        for q, k in enumerate(BRANCHES):
            with act.Fori(0, 2) as i:
                for mm_ in range(4):
                    pair, j = mm_ // 2, mm_ % 2
                    n = N_GATE + 16 * q + 4 * pair + j
                    m0 = 8 * q + mm_
                    act.wait_ge(gated, i * 4 + (m0 if m0 else 1))
                    wait_ready(n, i, 8)
                    g_t = tmp[1 + j]
                    for s, d in zip(pspans(n), spans(g_t)):
                        ins = nc.scalar.activation(d, s, ACT.Sigmoid,
                                                   bias=vec_b[:, bass.ds(i * 4 + (4 * VB_GATE + 8 * k + mm_), 1)])
                    ins.then_inc(drained[n % 2], 1)
                    if q < 3:
                        u = 4 * (q + 1) + mm_ // 2
                        if j == 0:
                            stage_load(u, i)
                        else:
                            stage_hi(u, i)
                    if q == 3 and j == 1:
                        for jj in range(2):
                            mj = mm_ - 1 + jj
                            act.wait_ge(gated, i * 4 + (8 * q + mj + 2))
                            copy(flat(mv_hi[:, bass.ds(i * 4 + mj, 1), :]),
                                 flat(merged[:, bass.ds(i * 4 + mj, 1), :])).then_inc(mv_hi_done, 1)

        def residual_tiles(ph, n0):
            with act.Fori(0, 4) as i:
                for j in range(2):
                    n = n0 + j
                    act.wait_ge(drained[n % 2], i + (n // 2 + 1))
                    act.wait_ge(sumsq, i * 2 + (9 * ph + 1 + j))
                    nc.scalar.activation(tmp[2][:, :], flat(x_res[:, bass.ds(i * 2 + j, 1), :]),
                                         ACT.Square).then_inc(res_sq, 1)
                    act.wait_ge(scaled, i * 2 + (8 * ph + j + 1))
                    copy(flat(xs_hi[:, bass.ds(i * 2 + j, 1), :]), tmp[1][:, :]).then_inc(xs_hi_done, 1)

        def root(ph):
            act.wait_ge(r_var, ph + 1)
            nc.scalar.activation(tmp[0][:, :], tmp[0][:, :], ACT.Sqrt).then_inc(r_std, 1)

        residual_tiles(0, N_MIX)
        root(0)

        def query_hi(m, n, i=None):
            act.wait_ge(drained[n % 2], n // 2 + 1 if i is None else i + (n // 2 + 1))
            dst = mv_hi[:, m, :] if i is None else flat(mv_hi[:, bass.ds(i * 2 + m, 1), :])
            copy(dst, tmp[1 + m % 2][:, :]).then_inc(mv_hi_done, 1)

        query_hi(0, N_Q)
        query_hi(1, N_Q + 1)
        with act.Fori(0, 3) as i:
            for j in range(2):
                query_hi(2 + j, N_Q + 2 + j, i)

        for g in range(4):
            act.wait_ge(at_t, g + 1)
            copy(flat(kt_hi[:, 2 * g:2 * g + 2, :]), PS[:, 4 + g % 2, :]).then_inc(at_kh, 1)
        act.wait_ge(kv_in[1], 16)
        copy(flat(v_hi[:, :, :]), kvring[:, 1, :]).then_inc(at_vh, 1)
        scale = HEAD_DIM ** -0.5
        for v in range(32 + 6):
            if v < 32:
                act.wait_ge(mx_ready, v + 1)
                if v >= 4:
                    act.wait_ge(pt_ready, v - 3)
                nc.scalar.activation(probs[:, v % 4, :], PS[:, v % 4, 0:N_MEM], ACT.Exp,
                                     bias=sm[:, 4 + v % 4:5 + v % 4], scale=scale,
                                     accum_out=sm[:, 8 + v % 4:9 + v % 4]).then_inc(e_ready, 1)
            if 1 <= v <= 32:
                u = v - 1
                act.wait_ge(rs_ready, u + 1)
                copy(probs[:, u % 4, :], probs[:, u % 4, :], scale=sm[:, 12 + u % 4:13 + u % 4]).then_inc(p_ready, 1)
            if v >= 9 and v % 4 == 1:
                G = (v - 9) // 4
                h, t0 = G // 2, 512 * (G % 2)
                for dt in range(2):
                    act.wait_ge(pv_ready, 2 * G + dt + 1)
                    copy(mv_hi[:, 2 * h + dt, t0:t0 + 512], PS[:, 6 + dt, :]).then_inc(o_hi, 1)
            if 2 <= v <= 33:
                u = v - 2
                G, c0 = u // 4, (u % 4) * P
                act.wait_ge(pt_ready, u + 1)
                if G >= 2:
                    act.wait_ge(pv_ready, 2 * (G - 1))
                copy(pt_hi[G % 2][:, :, c0:c0 + P],
                     PS[:, 4 + u % 2, 0:2 * P].rearrange("p (m t) -> p m t", m=2)).then_inc(pt_hi_done, 1)
        for b in range(DEC_B):
            act.wait_ge(ks_t, b + 1)
            if b >= 2:
                act.wait_ge(ss_ready, b - 1)
            copy(flat(kt_s[:, b % 2, 0:4, :]), flat(PS[:, 0:2, :])).then_inc(ks_a, 1)
        act.wait_ge(sm_mx, 1)
        for h in range(HEADS):
            nc.scalar.activation(p_s[:, h * N_MEM:(h + 1) * N_MEM], PS[0:N_SAMPLE, 4 + h, 0:N_MEM], ACT.Exp,
                                 bias=sm[0:N_SAMPLE, 20 + h:21 + h], scale=scale,
                                 accum_out=sm[0:N_SAMPLE, 24 + h:25 + h]).then_inc(sm_e, 1)
        act.wait_ge(so_ready, DEC_B)
        copy(p_s[:, :].rearrange("p (h d) -> p h d", h=HEADS), PS[0:N_SAMPLE, 4:8, 0:HEAD_DIM]).then_inc(so_copied, 1)
        act.wait_ge(so_t, 1)
        copy(mv_hi[:, :, SEQ:T], PS[:, 1, :].rearrange("p (k t) -> p k t", k=KT)).then_inc(so_hi, 1)

        residual_tiles(1, N_XO)
        root(1)

        def hidden(m, n, count, i=None):
            act.wait_ge(drained[n % 2], n // 2 + 1 if i is None else i + (n // 2 + 1))
            act.wait_ge(hid_ready, count if i is None else i * 2 + count)
            nc.scalar.activation(tmp[2][:, :], tmp[1][:, :], ACT.Square).then_inc(relu_done, 1)
            act.wait_ge(relu_done, count + 1 if i is None else i * 2 + (count + 1))
            dst = mv_hi[:, m, :] if i is None else flat(mv_hi[:, bass.ds(i * 2 + m, 1), :])
            copy(dst, tmp[2][:, :]).then_inc(hid_hi, 1)

        for c in range(4):
            n1 = N_FF + 16 * c
            m0 = 0
            if c == 0:
                hidden(0, n1, 0)
                hidden(1, n1 + 1, 1)
                m0 = 2
            with act.Fori(0, (8 - m0) // 2) as i:
                for j in range(2):
                    hidden(m0 + j, n1 + m0 + j, 8 * c + m0 + j, i)

        for m in range(KT):
            act.wait_ge(aux_ready, AUX[f"y{m}a"] + 1)
            copy(y_tok[:, 0:8, m * P:(m + 1) * P],
                 flat(PS[:, 6:8, :]).rearrange("p (t c) -> p t c", t=8)).then_inc(aux_drained, 1)
            act.wait_ge(aux_ready, AUX[f"y{m}b"] + 1)
            copy(y_tok[0:N_SAMPLE, 8, m * P:(m + 1) * P], PS[0:N_SAMPLE, 6, 0:P]).then_inc(aux_drained, 1)
            if m >= KT - 3:
                act.wait_ge(aux_drained, AUX[f"y{m}b"] + 1)
                part = m - (KT - 3)
                f0, f1 = Y_PARTS[part]
                act.wait_ge(fst_ready, 1)
                for t, (t0, tw) in enumerate(TOK_TILES):
                    k = 9 * part + t
                    if k >= 2:
                        act.wait_ge(fs_sq, k - 1)
                    nc.scalar.activation(junk[0:tw, k % 2, f0:f1], y_tok[0:tw, t, f0:f1], ACT.Square,
                                         accum_out=fst[0:tw, part, t:t + 1]).then_inc(fs_sq, 1)
        act.wait_ge(fs_var, 1)
        nc.scalar.activation(fst[:, 0, :], fst[:, 0, :], ACT.Sqrt).then_inc(fs_std, 1)
        act.wait_ge(fs_r, 1)
        for t in range(1, 9, 2):
            act.wait_ge(fs_gain, 3)
            copy(y_tok[:, t, :], y_tok[:, t, :], scale=fst[:, 0, t:t + 1]).then_inc(y_odd, 1)

    @block.vector
    def _(dve):
        chain = Chain(dve, dve_step)
        link = chain.link
        v = nc.vector
        taps = [0]

        def wait_ready(n, i=None, per=0):
            dve.wait_ge(ready[n % 2], n // 2 + 1 if i is None else i * (per // 2) + n // 2 + 1)

        v.memset(ones[:, :], 1.0).then_inc(ones_ready, 1)
        v.memset(small[:, :], 1.0).then_inc(zeros_ready, 1)
        dve.wait_ge(zeros_ready, 1)
        for j in range(POOL_H):
            ins = v.memset(small[:, 104 + j:105 + j], 1.0 / (j + 1))
        link(ins)
        def token_scaled(t):
            if t == 0:
                dve.wait_ge(aux_drained, AUX["vec"] + 1)
            dve.wait_ge(*tile_transposed(t))
            if t >= 2:
                dve.wait_ge(hhi_done, t - 1)
                dve.wait_ge(hlo_done, t - 1)
            h = x_height(t)
            row = VB_MIX if t < 9 else VB_MEM
            gain = vec_b[:, 4 * row:4 * row + KT].unsqueeze(2).broadcast_to([P, KT, h])
            v.tensor_tensor(fbuf[:, t % 2, 0:KT * h].rearrange("p (k n) -> p k n", k=KT),
                            tile_psum(t)[:, 0:KT * h].rearrange("p (k n) -> p k n", k=KT),
                            gain, ALU.mult).then_inc(scaled_tile(t)[0], 1)

        def token_normalised(t):
            h = x_height(t)
            dve.wait_ge(std_done, t + 1)
            link(v.reciprocal(ss[0:h, t:t + 1], ss[0:h, t:t + 1]))
            if t >= 2:
                dve.wait_ge(*tile_transposed(t - 2))
            v.tensor_scalar(xn[0:h, t % 2, :], xring[0:h, t % 4, :], ss[0:h, t:t + 1], None,
                            ALU.mult).then_inc(xn_ready, 1)

        for s_ in range(11 + 2):
            if s_ < 11:
                h = x_height(s_)
                dve.wait_ge(sq_done, s_ + 1)
                v.tensor_scalar(ss[0:h, s_:s_ + 1], ss[0:h, s_:s_ + 1], 1.0 / D_MODEL, EPS, ALU.mult,
                                ALU.add).then_inc(var_done, 1)
            if 1 <= s_ <= 11:
                token_normalised(s_ - 1)
            if s_ >= 2:
                token_scaled(s_ - 2)

        dve.wait_ge(hlo_done, 11)
        dve.wait_ge(hhi_done, 11)
        dve.wait_ge(aux_ready, AUX["cc"] + 1)
        for ct in range(CT):
            ins = v.memset(slots_d[:, ct + 1, 0:CCONV_H], 0.0)
        link(ins)

        def conv_taps(count):
            for _ in range(count):
                ct, j = taps[0] // CCONV_K, taps[0] % CCONV_K
                taps[0] += 1
                acc, ext = slots_d[:, ct, 0:T], slots_d[:, ct + 1, :]
                w = va(VA_CCW + j, ct)
                pairs = ((acc[:, 0:SEQ], ext[:, j:j + SEQ]),
                         (acc[:, SEQ:T].rearrange("p (b l) -> p b l", b=DEC_B), eseq(ext, CCONV_H, j)))
                for dst, src in pairs:
                    if j == 0:
                        ins = v.tensor_scalar(dst, src, w, va(VA_CCB, ct), ALU.mult, ALU.add)
                    else:
                        ins = v.scalar_tensor_tensor(out=dst, in0=src, scalar=w, in1=dst, op0=ALU.mult, op1=ALU.add)
                if j == CCONV_K - 1:
                    ins.then_inc(conv_done, 1)
                    dve.wait_ge(conv_done, ct + 1)
                else:
                    link(ins)

        def keep_tails(ext, head, ct):
            v.tensor_copy(tailbuf[:, ct, 0:head], ext[:, SEQ:SEQ + head])
            v.tensor_copy(tailbuf[:, ct, CCONV_H:].rearrange("p (b l) -> p b l", b=DEC_B),
                          eseq(ext, head, head)).then_inc(tails_ready, 1)

        for ct in range(CT):
            n = N_D + 2 * ct + 1
            wait_ready(n)
            dve.wait_ge(drained[(n - 1) % 2], (n - 1) // 2 + 1)
            ext = slots_d[:, ct + 1, :]
            for s, g, d in zip(ppieces(n), pieces(tmp[2]), epieces(ext, CCONV_H)):
                ins = v.tensor_tensor(d, s, g, ALU.mult)
            ins.then_inc(drained[n % 2], 1)
            dve.wait_ge(drained[n % 2], n // 2 + 1)
            keep_tails(ext, CCONV_H, ct)
            if ct == 0:
                dve.wait_ge(aux_drained, AUX["v3b"] + 1)
                for t, (t0, tw) in enumerate(TOK_TILES):
                    ins = v.bn_stats(bn[0:tw, t, :], v_tok[0:tw, t, :])
                link(ins)
                for t, (t0, tw) in enumerate(TOK_TILES):
                    ins = v.bn_aggr(bn_mv[0:tw, t, :], bn[0:tw, t, :])
                link(ins)
                v.tensor_scalar(v_rstd.unsqueeze(2), bn_mv[:, :, 1:2], EPS, None, ALU.add).then_inc(v_var, 1)
                dve.wait_ge(v_std, 1)
                link(v.reciprocal(v_rstd, v_rstd))
                dve.wait_ge(late_in, 32)
            if ct < 3:
                for t in range(3 * ct, 3 * ct + 3):
                    tw = TOK_TILES[t][1]
                    vt = v_tok[0:tw, t, :]
                    link(v.tensor_scalar(vt, vt, bn_mv[0:tw, t, 0:1], v_rstd[0:tw, t:t + 1], ALU.subtract, ALU.mult))
                    link(v.tensor_tensor(vt, vt, ln_g[0:tw, :], ALU.mult))
                    v.tensor_tensor(vt, vt, ln_b[0:tw, :], ALU.add).then_inc(v_norm, 1)
            conv_taps(TAPS_D[ct])

        for g in range(HEADS):
            n = N_CU + 2 * g + 1
            k = RING_C + g
            wait_ready(n)
            dve.wait_ge(drained[(n - 1) % 2], (n - 1) // 2 + 1)
            dve.wait_ge(outs[k % 2], 16 * (k // 2))
            acc, dst = flat(pset(n)), oring[:, k % 2, :]
            v.tensor_tensor(dst[:, 0:SEQ].rearrange("p (n t) -> p n t", n=8),
                            acc[:, 0:SEQ].rearrange("p (n t) -> p n t", n=8),
                            bias_s[:, g, :].unsqueeze(1).broadcast_to([P, 8, P]), ALU.add)
            v.tensor_tensor(dst[:, SEQ:T].rearrange("p (n t) -> p n t", n=DEC_B),
                            acc[:, SEQ:T].rearrange("p (n t) -> p n t", n=DEC_B),
                            bias_s[:, g, 0:DEC_L].unsqueeze(1).broadcast_to([P, DEC_B, DEC_L]),
                            ALU.add).then_inc(drained[n % 2], 1)
            dve.wait_ge(drained[n % 2], n // 2 + 1)
            v.tensor_tensor(dst, dst, vring[:, g % 2, :], ALU.mult).then_inc(sgu_out, 1)
            conv_taps(TAPS_CU[g])

        dve.wait_ge(aux_drained, AUX["V1"] + 1)
        dve.wait_ge(aux_drained, AUX["tail_d"] + 1)
        dve.wait_ge(kv_stored, 8 * 16)
        dve.wait_ge(state_out, 16 * (2 + 9 + 1))
        for j in range(2):
            ins = v.memset(ext_a[:, j, 0:POOL_H], 0.0)
        link(ins)
        for g in range(CT):
            n = N_A_IN[g]
            dve.wait_ge(drained[n % 2], n // 2 + 1)
            e = ext_a[:, g % 2, :]
            keep_tails(e, POOL_H, g)
            src = e
            for lv in range(g + 1):
                s = 1 << lv
                dst = sums[:, lv % 2, :]
                lo = 2 * s - 1
                link(v.tensor_tensor(dst[:, lo:EXT_A], src[:, lo:EXT_A], src[:, lo - s:EXT_A - s], ALU.add))
                src = dst
            if g >= 1:
                wait_ready(N_A_MAP[g - 1])
            w = 1 << (g + 1)
            pairs = ((pooled[:, 0:SEQ], src[:, POOL_H:POOL_H + SEQ], e[:, POOL_H:POOL_H + SEQ]),
                     (pooled[:, SEQ:T].rearrange("p (b l) -> p b l", b=DEC_B), eseq(src, POOL_H, POOL_H),
                      eseq(e, POOL_H, POOL_H)))
            for dst, sm_, x_ in pairs:
                ins = v.scalar_tensor_tensor(out=dst, in0=sm_, scalar=1.0 / w, in1=x_, op0=ALU.mult,
                                             op1=ALU.subtract)
            link(ins)
            link(v.tensor_tensor(pooled[:, 0:w - 1], src[:, POOL_H:POOL_H + w - 1], inv_cnt[:, 0:w - 1], ALU.mult))
            v.tensor_tensor(pooled[:, 0:w - 1], pooled[:, 0:w - 1], e[:, POOL_H:POOL_H + w - 1],
                            ALU.subtract).then_inc(pool_in_ready, 1)
            conv_taps(TAPS_A[g])

        def stage_lo(u, i=None):
            q, ct = u // 4, u % 4
            if i is None:
                dve.wait_ge(br_hi_done, u + 1)
                hi, lo = br_hi[q % 2][:, ct, :], br_lo[q % 2][:, ct, :]
            else:
                dve.wait_ge(br_hi_done, i * 2 + (u + 1))
                hi = flat(br_hi[q % 2][:, bass.ds(i * 2 + ct, 1), :])
                lo = flat(br_lo[q % 2][:, bass.ds(i * 2 + ct, 1), :])
            v.tensor_tensor(lo, stage_of(q), hi.bitcast(F32), ALU.subtract).then_inc(br_lo_done, 1)

        conv_taps(TAPS_B[0])
        dve.wait_ge(aux_ready, AUX["tail_a"] + 1)
        link(v.memset(ext_b[:, 0:SCONV_H], 0.0))
        for ct in range(CT):
            nh, n_c, nb_ = N_B_H[ct], N_B_C[ct], N_B_B[ct]
            wait_ready(n_c)
            dve.wait_ge(drained[nh % 2], nh // 2 + 1)
            v.tensor_copy(eheads(ext_b, SCONV_H), st_sc[:, ct, :].rearrange("p (b l) -> p b l", b=DEC_B))
            for s, g, d in zip(ppieces(n_c), pieces(b_h), epieces(ext_b, SCONV_H)):
                ins = v.tensor_tensor(d, s, g, ALU.mult)
            ins.then_inc(drained[n_c % 2], 1)
            dve.wait_ge(drained[n_c % 2], n_c // 2 + 1)
            keep_tails(ext_b, SCONV_H, ct)
            acc = vring[:, 0, :]
            for j in range(SCONV_K):
                w = va(VA_SCW + j, ct)
                for dst, src in ((acc[:, 0:SEQ], ext_b[:, j:j + SEQ]),
                                 (acc[:, SEQ:T].rearrange("p (b l) -> p b l", b=DEC_B), eseq(ext_b, SCONV_H, j))):
                    if j == 0:
                        ins = v.tensor_scalar(dst, src, w, None, ALU.mult)
                    else:
                        ins = v.scalar_tensor_tensor(out=dst, in0=src, scalar=w, in1=dst, op0=ALU.mult, op1=ALU.add)
                link(ins)
            if ct == 0:
                conv_taps(TAPS_B[1])
            if ct == 1:
                n = N_MEAN
                wait_ready(n)
                for c in range(CT):
                    for s, d in zip(pspans(n), spans(slots_d[:, c, 0:T])):
                        ins = v.scalar_tensor_tensor(out=d, in0=s, scalar=-1.0 / W_BR, in1=d, op0=ALU.mult,
                                                     op1=ALU.add)
                ins.then_inc(drained[n % 2], 1)
                dve.wait_ge(drained[n % 2], n // 2 + 1)
                dve.sem_inc(dn_mean, 1)
            k = RING_B + ct
            dve.wait_ge(outs[k % 2], 16 * (k // 2))
            wait_ready(nb_)
            for s, x_, d in zip(pspans(nb_), spans(acc), spans(oring[:, k % 2, :])):
                ins = v.tensor_tensor(d, s, x_, ALU.mult)
            ins.then_inc(drained[nb_ % 2], 1)
            dve.wait_ge(drained[nb_ % 2], nb_ // 2 + 1)
            dve.sem_inc(ring_full, 1)
            stage_lo(ct)
            if ct == 0:
                conv_taps(TAPS_B[2])
            if ct == 1:
                for c in range(1, CT):
                    dve.wait_ge(dn_sq, c + 1)
                    v.tensor_tensor(tmp[2][:, :], tmp[2][:, :], tmp[0][:, :], ALU.add).then_inc(dn_acc, 1)
                    dve.wait_ge(dn_acc, c)
                n = N_VAR
                wait_ready(n)
                for s, d in zip(pspans(n), spans(tmp[2])):
                    ins = v.tensor_scalar(d, s, 1.0 / W_BR, EPS, ALU.mult, ALU.add)
                ins.then_inc(drained[n % 2], 1)
                dve.wait_ge(drained[n % 2], n // 2 + 1)
                dve.sem_inc(dn_var, 1)
                dve.wait_ge(dn_std, 1)
                link(v.reciprocal(tmp[2][:, :], tmp[2][:, :]))
                for c in range(CT):
                    v.tensor_tensor(slots_d[:, c, 0:T], slots_d[:, c, 0:T], tmp[2][:, :], ALU.mult).then_inc(dn_y, 1)
        assert taps[0] == CT * CCONV_K
        for j in range(2):
            dve.wait_ge(outs[j], 16 * len(range(j, 25, 2)))
        dve.sem_inc(gated, 1)

        for q in range(4):
            with dve.Fori(0, 2) as i:
                for mm_ in range(4):
                    pair, j = mm_ // 2, mm_ % 2
                    ng = N_GATE + 16 * q + 4 * pair + j
                    n = ng + 2
                    g_t = tmp[1 + j]
                    wait_ready(n, i, 8)
                    dve.wait_ge(drained[ng % 2], i * 4 + (ng // 2 + 1))
                    for s, d in zip(pspans(n), spans(g_t)):
                        ins = v.tensor_tensor(d, s, d, ALU.mult)
                    ins.then_inc(drained[n % 2], 1)
                    dve.wait_ge(drained[n % 2], i * 4 + (n // 2 + 1))
                    m_t = flat(merged[:, bass.ds(i * 4 + mm_, 1), :])
                    if q == 0:
                        v.tensor_copy(m_t, g_t[:, :]).then_inc(gated, 1)
                    else:
                        v.tensor_tensor(m_t, m_t, g_t[:, :], ALU.add).then_inc(gated, 1)
                    if q < 3 and j == 1:
                        stage_lo(4 * (q + 1) + mm_ // 2, i)
                    if q == 3:
                        dve.wait_ge(mv_hi_done, i * 4 + (mm_ + 1))
                        v.tensor_tensor(flat(mv_lo[:, bass.ds(i * 4 + mm_, 1), :]), m_t,
                                        flat(mv_hi[:, bass.ds(i * 4 + mm_, 1), :]).bitcast(F32),
                                        ALU.subtract).then_inc(mv_lo_done, 1)

        def residual_tiles(ph, n0, row):
            c0 = 9 * ph + 1
            v.memset(tmp[0][:, :], 0.0).then_inc(sumsq, 1)
            dve.wait_ge(sumsq, c0)
            with dve.Fori(0, 4) as i:
                for j in range(2):
                    n = n0 + j
                    dve.wait_ge(ready[n % 2], i + (n // 2 + 1))
                    x_t = x_res[:, bass.ds(i * 2 + j, 1), :]
                    x_f = flat(x_t)
                    for s, d in zip(pspans(n), spans(x_f)):
                        ins = v.tensor_tensor(d, s, d, ALU.add)
                    ins.then_inc(drained[n % 2], 1)
                    dve.wait_ge(drained[n % 2], i + (n // 2 + 1))
                    v.tensor_scalar(tmp[1][:, :], x_f, vec_b[:, bass.ds(i * 2 + (4 * row + j), 1)], None,
                                    ALU.mult).then_inc(scaled, 1)
                    dve.wait_ge(res_sq, i * 2 + (8 * ph + j + 1))
                    v.tensor_tensor(tmp[0][:, :], tmp[0][:, :], tmp[2][:, :], ALU.add).then_inc(sumsq, 1)
                    dve.wait_ge(sumsq, i * 2 + (c0 + j + 1))
                    dve.wait_ge(scaled, i * 2 + (8 * ph + j + 1))
                    dve.wait_ge(xs_hi_done, i * 2 + (8 * ph + j + 1))
                    v.tensor_tensor(flat(xs_lo[:, bass.ds(i * 2 + j, 1), :]), tmp[1][:, :],
                                    flat(xs_hi[:, bass.ds(i * 2 + j, 1), :]).bitcast(F32),
                                    ALU.subtract).then_inc(xs_lo_done, 1)

        def inverse_rms(ph, n):
            dve.wait_ge(aux_ready, AUX[f"sum{ph}"] + 1)
            v.tensor_scalar(tmp[0][:, 0:SEQ], flat(PS[:, 6:8, :]), 1.0 / D_MODEL, EPS, ALU.mult,
                            ALU.add).then_inc(aux_drained, 1)
            wait_ready(n)
            dve.wait_ge(aux_drained, AUX[f"sum{ph}"] + 1)
            v.tensor_scalar(tmp[0][:, SEQ:T], pset(n)[:, 2, CW:CW + N_SAMPLE], 1.0 / D_MODEL, EPS, ALU.mult,
                            ALU.add).then_inc(r_var, 1)
            dve.wait_ge(r_std, ph + 1)
            v.reciprocal(tmp[0][:, :], tmp[0][:, :]).then_inc(r_ready, 1)
            dve.wait_ge(r_ready, ph + 1)

        for i in range(4):
            dve.wait_ge(xres_in[i], 16)
        residual_tiles(0, N_MIX, VB_X)
        inverse_rms(0, N_Q)

        def query(m, n, count, i=None):
            cnt = n // 2 + 1 if i is None else i + (n // 2 + 1)
            dve.wait_ge(ready[n % 2], cnt)
            t_ = tmp[1 + m % 2]
            for s, r, d in zip(pspans(n), spans(tmp[0]), spans(t_)):
                ins = v.tensor_tensor(d, s, r, ALU.mult)
            ins.then_inc(drained[n % 2], 1)
            dve.wait_ge(drained[n % 2], cnt)
            dve.wait_ge(mv_hi_done, count + 1 if i is None else i * 2 + (count + 1))
            hi = mv_hi[:, m, :] if i is None else flat(mv_hi[:, bass.ds(i * 2 + m, 1), :])
            lo = mv_lo[:, m, :] if i is None else flat(mv_lo[:, bass.ds(i * 2 + m, 1), :])
            v.tensor_tensor(lo, t_[:, :], hi.bitcast(F32), ALU.subtract).then_inc(mv_lo_done, 1)

        query(0, N_Q, KT)
        query(1, N_Q + 1, KT + 1)
        with dve.Fori(0, 3) as i:
            for j in range(2):
                query(2 + j, N_Q + 2 + j, KT + 2 + j, i)

        for g in range(4):
            dve.wait_ge(at_kh, g + 1)
            v.tensor_tensor(flat(kt_lo[:, 2 * g:2 * g + 2, :]), PS[:, 4 + g % 2, :],
                            flat(kt_hi[:, 2 * g:2 * g + 2, :]).bitcast(F32), ALU.subtract).then_inc(at_kl, 1)
        dve.wait_ge(at_vh, 1)
        v.tensor_tensor(flat(v_lo[:, :, :]), kvring[:, 1, :], flat(v_hi[:, :, :]).bitcast(F32),
                        ALU.subtract).then_inc(at_vl, 1)
        scale = HEAD_DIM ** -0.5

        def row_max(u):
            k = u % 4
            dve.wait_ge(sc_ready, u + 1)
            link(v.tensor_reduce(sm[:, k:k + 1], PS[:, k, 0:N_MEM], AX_X, ALU.max))
            v.tensor_scalar(sm[:, 4 + k:5 + k], sm[:, k:k + 1], -scale, None, ALU.mult).then_inc(mx_ready, 1)

        row_max(0)
        for w_ in range(32 + 7):
            if 1 <= w_ <= 32:
                k = (w_ - 1) % 4
                dve.wait_ge(e_ready, w_)
                v.reciprocal(sm[:, 12 + k:13 + k], sm[:, 8 + k:9 + k]).then_inc(rs_ready, 1)
            if w_ + 1 < 32:
                row_max(w_ + 1)
            if w_ >= 10 and w_ % 4 == 2:
                G = (w_ - 10) // 4
                h, t0 = G // 2, 512 * (G % 2)
                for dt in range(2):
                    dve.wait_ge(o_hi, 2 * G + dt + 1)
                    v.tensor_tensor(mv_lo[:, 2 * h + dt, t0:t0 + 512], PS[:, 6 + dt, :],
                                    mv_hi[:, 2 * h + dt, t0:t0 + 512].bitcast(F32), ALU.subtract).then_inc(o_lo, 1)
            if 3 <= w_ <= 34:
                u = w_ - 3
                G, c0 = u // 4, (u % 4) * P
                dve.wait_ge(pt_hi_done, u + 1)
                v.tensor_tensor(pt_lo[G % 2][:, :, c0:c0 + P],
                                PS[:, 4 + u % 2, 0:2 * P].rearrange("p (m t) -> p m t", m=2),
                                pt_hi[G % 2][:, :, c0:c0 + P].bitcast(F32), ALU.subtract).then_inc(pt_lo_done, 1)
        dve.wait_ge(pv_ready, 16)
        for r in range(4):
            ins = v.memset(qm[r][:, :], 0.0)
        link(ins)

        def masked_query(b):
            q3 = qm[b % 4][:, :].rearrange("p (k t) -> p k t", k=KT)
            if b >= 4:
                dve.wait_ge(ss_ready, b - 3)
                link(v.memset(q3[:, :, DEC_L * (b - 4):DEC_L * (b - 3)], 0.0))
            s0 = SEQ + DEC_L * b
            v.tensor_tensor(q3[:, :, DEC_L * b:DEC_L * (b + 1)], mv_hi[:, :, s0:s0 + DEC_L].bitcast(F32),
                            mv_lo[:, :, s0:s0 + DEC_L].bitcast(F32), ALU.add).then_inc(qm_ready, 1)

        for b in range(4):
            masked_query(b)
        for b in range(DEC_B):
            dve.wait_ge(ks_t, b + 1)
            if b >= 2:
                dve.wait_ge(ss_ready, b - 1)
            v.tensor_copy(flat(kt_s[:, b % 2, 4:8, :]), flat(PS[:, 2:4, :])).then_inc(ks_d, 1)
            if b >= 4:
                masked_query(b)
            if b == 2:
                ins = v.memset(ptm[:, :, :], 0.0)
                link(ins)
        dve.wait_ge(ss_ready, DEC_B)
        n64 = N_SAMPLE
        link(v.tensor_reduce(sm[0:n64, 16:20], PS[0:n64, 4:8, 0:N_MEM], AX_X, ALU.max))
        v.tensor_scalar(sm[0:n64, 20:24], sm[0:n64, 16:20], -scale, None, ALU.mult).then_inc(sm_mx, 1)
        dve.wait_ge(sm_e, HEADS)
        link(v.reciprocal(sm[0:n64, 28:32], sm[0:n64, 24:28]))
        for h in range(HEADS):
            ps_h = p_s[:, h * N_MEM:(h + 1) * N_MEM]
            ins = v.tensor_scalar(ps_h, ps_h, sm[0:n64, 28 + h:29 + h], None, ALU.mult)
        ins.then_inc(sm_p, 1)
        dve.wait_ge(sm_t, 1)
        blocks = PS[:, 0, :].rearrange("p (j t) -> p j t", t=n64)
        for b in range(DEC_B):
            ins = v.tensor_copy(ptm[:, b, :].rearrange("p (j t) -> p j t", t=n64)[:, :, DEC_L * b:DEC_L * (b + 1)],
                                blocks[:, :, DEC_L * b:DEC_L * (b + 1)])
        ins.then_inc(sm_pt, 1)
        dve.wait_ge(so_hi, 1)
        v.tensor_tensor(mv_lo[:, :, SEQ:T], PS[:, 1, :].rearrange("p (k t) -> p k t", k=KT),
                        mv_hi[:, :, SEQ:T].bitcast(F32), ALU.subtract).then_inc(so_lo, 1)

        residual_tiles(1, N_XO, VB_FFN)
        inverse_rms(1, N_FF)

        def hidden(m, n, count, i=None):
            cnt = n // 2 + 1 if i is None else i + (n // 2 + 1)
            dve.wait_ge(ready[n % 2], cnt)
            for s, r, d in zip(pspans(n), spans(tmp[0]), spans(tmp[1])):
                ins = v.scalar_tensor_tensor(out=d, in0=s, scalar=0.0, in1=r, op0=ALU.max, op1=ALU.mult)
            ins.then_inc(drained[n % 2], 1)
            dve.wait_ge(hid_hi, count + 1 if i is None else i * 2 + (count + 1))
            hi = mv_hi[:, m, :] if i is None else flat(mv_hi[:, bass.ds(i * 2 + m, 1), :])
            lo = mv_lo[:, m, :] if i is None else flat(mv_lo[:, bass.ds(i * 2 + m, 1), :])
            v.tensor_tensor(lo, tmp[2][:, :], hi.bitcast(F32), ALU.subtract).then_inc(hid_ready, 1)

        for c in range(4):
            n1, n2 = N_FF + 16 * c, N_FF + 16 * c + 8
            m0 = 0
            if c == 0:
                hidden(0, n1, 0)
                hidden(1, n1 + 1, 1)
                m0 = 2
            with dve.Fori(0, (8 - m0) // 2) as i:
                for j in range(2):
                    hidden(m0 + j, n1 + m0 + j, 8 * c + m0 + j, i)
            with dve.Fori(0, 4 if c < 3 else 3) as i:
                for j in range(2):
                    n = n2 + j
                    dve.wait_ge(ready[n % 2], i + (n // 2 + 1))
                    x_f = flat(x_res[:, bass.ds(i * 2 + j, 1), :])
                    for s, d in zip(pspans(n), spans(x_f)):
                        ins = v.tensor_tensor(d, s, d, ALU.add)
                    ins.then_inc(drained[n % 2], 1)

        def gain_part(part):
            f0, f1 = Y_PARTS[part]
            dve.wait_ge(fs_sq, 9 * part + 9)
            for tw, t0, t1 in ((P, 0, 8), (N_SAMPLE, 8, 9)):
                y_ = y_tok[0:tw, t0:t1, f0:f1]
                ins = v.tensor_tensor(y_, y_, gf[0:tw, f0:f1].unsqueeze(1).broadcast_to([tw, t1 - t0, f1 - f0]),
                                      ALU.mult)
            ins.then_inc(fs_gain, 1)

        dve.wait_ge(gf_in, 16)
        v.memset(fst[:, :, :], 1.0).then_inc(fst_ready, 1)
        for m in (6, 7):
            n = N_FF + 56 + m
            wait_ready(n)
            for s, d in zip(pspans(n), spans(x_res[:, m, :])):
                ins = v.tensor_tensor(d, s, d, ALU.add)
            ins.then_inc(drained[n % 2], 1)
            gain_part(m - 6)
        dve.wait_ge(fs_sq, 27)
        link(v.tensor_tensor(fst[:, 0, :], fst[:, 0, :], fst[:, 1, :], ALU.add))
        link(v.tensor_tensor(fst[:, 0, :], fst[:, 0, :], fst[:, 2, :], ALU.add))
        v.tensor_scalar(fst[:, 0, :], fst[:, 0, :], 1.0 / D_MODEL, EPS, ALU.mult, ALU.add).then_inc(fs_var, 1)
        gain_part(2)
        dve.wait_ge(fs_std, 1)
        v.reciprocal(fst[:, 0, :], fst[:, 0, :]).then_inc(fs_r, 1)
        dve.wait_ge(fs_r, 1)
        dve.wait_ge(fs_gain, 3)
        for t in range(0, 9, 2):
            tw = TOK_TILES[t][1]
            v.tensor_scalar(y_tok[0:tw, t, :], y_tok[0:tw, t, :], fst[0:tw, 0, t:t + 1], None,
                            ALU.mult).then_inc(y_even, 1)


_INS = ["x_prompt", "x_sample", "state_pool", "state_sconv", "state_cconv", "cache_mem_k", "cache_mem_v",
        "mem_prompt", "norm_mix_g", "w_in", "pool_w", "pool_scale", "sconv_w", "sgu_ln_g", "sgu_ln_b", "sgu_w",
        "sgu_b", "cconv_w", "cconv_b", "cconv_ln_g", "cconv_ln_b", "w_branch", "b_gate", "w_mix_out", "norm_x_g",
        "norm_mem_g", "w_xq", "w_xk", "w_xv", "w_xo", "norm_ffn_g", "w_ff1", "w_ff2", "norm_f_g"]
_OUTS = {
    "y_prompt": (1, SEQ, D_MODEL),
    "y_sample": (DEC_B, DEC_L, D_MODEL),
    "new_pool_prompt": (1, 1, POOL_H, W_BR),
    "new_sconv_prompt": (1, 1, SCONV_H, W_BR),
    "new_cconv_prompt": (1, 1, CCONV_H, W_BR),
    "mem_k_prompt": (1, 1, N_MEM, HEADS, HEAD_DIM),
    "mem_v_prompt": (1, 1, N_MEM, HEADS, HEAD_DIM),
    "new_pool_sample": (1, DEC_B, POOL_H, W_BR),
    "new_sconv_sample": (1, DEC_B, SCONV_H, W_BR),
    "new_cconv_sample": (1, DEC_B, CCONV_H, W_BR),
    "sgu_v_sample": (1, DEC_B, DEC_L, W_BR),
}


def kernel(**inputs):
    import numpy as _np
    import concourse.bacc as _bacc
    from concourse.bass_utils import run_bass_kernel_spmd as _run

    nc = _bacc.Bacc("TRN2", target_bir_lowering=False, num_devices=1)
    arrays, a, o = {}, {}, {}
    for name in _INS:
        x = _np.ascontiguousarray(inputs[name])
        arrays[f"in_{name}"] = x
        a[name] = nc.dram_tensor(f"in_{name}", x.shape, mybir.dt.from_np(x.dtype), kind="ExternalInput").ap()
    for name, shape in _OUTS.items():
        o[name] = nc.dram_tensor(f"out_{name}", shape, F32, kind="ExternalOutput").ap()
    scratch = {
        "xt": nc.dram_tensor("xt_scratch", (KT, P, T), F32).ap(),
        "branch": nc.dram_tensor("branch_scratch", (4, CT, P, T), F32).ap(),
        "kv": nc.dram_tensor("kv_scratch", (2, N_MEM, D_MODEL), F32).ap(),
    }
    build(nc, a, o, scratch)
    r = _run(nc, [arrays], core_ids=[0])
    return tuple(r.results[0][f"out_{name}"] for name in _OUTS)
```

```python
from contextlib import ExitStack

import concourse.bass as bass
from concourse import mybir

F32 = mybir.dt.float32
F32R = mybir.dt.float32r
ALU = mybir.AluOpType
ACT = mybir.ActivationFunctionType
AX_X = mybir.AxisListType.X

P = 128
D_MODEL = 1024
SEQ = 1024
DEC_B, DEC_L = 8, 8
N_SAMPLE = DEC_B * DEC_L
T = SEQ + N_SAMPLE
W_BR = 512
KT = D_MODEL // P
CT = W_BR // P
N_MEM = 256
MT = N_MEM // P
HEADS = 4
HEAD_DIM = D_MODEL // HEADS
D_FF = 4 * D_MODEL
EPS = 1e-6
POOL_H, SCONV_H, CCONV_H = 15, 2, 30
SCONV_K, CCONV_K = 3, 31
TOK_TILES = [(i * P, min(P, T - i * P)) for i in range(9)]

CW = 364
CHUNKS = [(0, CW), (CW, CW), (2 * CW, T - 2 * CW)]
TAIL = SEQ - 2 * CW

VA_CCW, VA_SCW, VA_PSC, VA_CCB, VA_LNG, VA_LNB, VA_N = 0, 31, 34, 35, 36, 37, 38
VB_MIX, VB_X, VB_FFN, VB_MEM, VB_GATE, VB_N = 0, 2, 4, 6, 8, 16

TILE = T * 4
REGION = KT * TILE
EXT_D = CCONV_H + SEQ + DEC_B * (CCONV_H + DEC_L)
EXT_A = POOL_H + SEQ + DEC_B * (POOL_H + DEC_L)
EXT_B = SCONV_H + SEQ + DEC_B * (SCONV_H + DEC_L)

IN_A, IN_BH, IN_BB, IN_BC, IN_CU, IN_CV, IN_DA, IN_DB, IN_G = 0, 4, 8, 12, 16, 20, 24, 28, 32
BRANCHES = [2, 0, 1, 3]

PHASE1 = ([("D", 0), ("D", 1)] + [("CV", g) for g in range(4)] +
          [("D", 2), ("K", 0), ("K", 1), ("D", 3), ("K", 2), ("D", 4), ("K", 3), ("D", 5), ("K", 4),
           ("D", 6), ("K", 5), ("D", 7), ("K", 6), ("K", 7)])

S_OF = {step: z for z, step in enumerate(PHASE1)}
S_CU = len(PHASE1)
S_A = S_CU + 12
S_B = S_A + 4
S_GATE = S_B + 12
S_MIX = S_GATE + 48
S_Q = S_MIX + 8
S_XO = S_Q + 8
S_FF = S_XO + 8
S_END = S_FF + 64

N_P0 = 0
N_OF = {step: N_P0 + 9 + n for n, step in enumerate(step for step in PHASE1 if step[0] != "K")}
N_CU = N_P0 + 9 + len(N_OF)
N_A = N_CU + 8
N_A_IN = [N_A, N_A + 1, N_A + 3, N_A + 5]
N_A_MAP = [N_A + 2, N_A + 4, N_A + 6, N_A + 8]
N_B_H = [N_A + 7, N_A + 11, N_A + 15, N_A + 19]
N_B_C = [N_A + 9, N_A + 12, N_A + 16, N_A + 20]
N_B_B = [N_A + 10, N_A + 14, N_A + 18, N_A + 21]
N_MEAN, N_VAR = N_A + 13, N_A + 17
N_GATE = N_A + 22
N_MIX = N_GATE + 64
N_Q = N_MIX + 8
N_XO = N_Q + 8
N_FF = N_XO + 8

AUX_ORDER = (["vec", "ws", "pl", "m0", "m1", "cc", "x0", "x1", "x2", "x3", "v0a", "v0b", "x4", "x5",
              "v1a", "v1b", "x6", "v2a", "v2b", "x7", "v3a", "v3b", "x8", "K0", "K1", "tail_d", "V0", "V1",
              "tail_a", "tail_b", "sum0", "sum1"]
             + [f"y{m}{h}" for m in range(KT - 1) for h in "ab"] + ["end"])
AUX = {name: n for n, name in enumerate(AUX_ORDER)}

RING_XT, RING_C, RING_A, RING_B, RING_D = 0, 9, 13, 17, 21
RING_OF = {2: RING_C, 0: RING_A, 1: RING_B, 3: RING_D}

Y_PARTS = [(0, 5 * P), (5 * P, 6 * P), (6 * P, 8 * P)]
Y_GROUPS = [[0, 1], [2, 3, 4], [5, 6, 7, 8]]

ATTEND = {min(4 * G + 6 + 2 * dt, 34 + dt): (G, dt) for G in range(8) for dt in range(2)}

K_BANKS = [6, 7, 4, 5]

TAPS_D, TAPS_CU, TAPS_A, TAPS_B = [31, 10, 11, 11], [10, 10, 10, 10], [5, 4, 0, 0], [12, 0, 0]
assert sum(TAPS_D + TAPS_CU + TAPS_A + TAPS_B) == CT * CCONV_K


class Chain:

    def __init__(self, eng, sem):
        self.eng, self.sem, self.n = eng, sem, 0

    def link(self, ins):
        self.n += 1
        ins.then_inc(self.sem, 1)
        self.eng.wait_ge(self.sem, self.n)


def build(nc, a, o, scratch):
    ctx = ExitStack()
    with ctx:
        _build(nc, a, o, scratch, ctx)


def _build(nc, a, o, scratch, ctx):
    base = nc.sbuf_base + (-nc.sbuf_base) % 32

    def at(name, shape, offset, dt=F32):
        return nc.alloc_sbuf_tensor_at(name, shape, dt, offset=base + offset)

    def S(name):
        return ctx.enter_context(nc.semaphore(name))

    Q = [REGION * i for i in range(5)]
    R1 = Q[2]
    o_w = 5 * REGION
    o_t = o_w + 6 * 4096
    o_c = o_t + 3 * TILE

    w_raw = at("w_raw", [P, 2, 1024], o_w)
    w_hi = at("w_hi", [P, 2, 1024], o_w + 8192, F32R)
    w_lo = at("w_lo", [P, 2, 1024], o_w + 16384, F32R)
    tmp = [at(f"tmp{i}", [P, T], o_t + i * TILE) for i in range(3)]
    ident = at("ident", [P, P], o_c)
    vec_b = at("vec_b", [P, VB_N * 4], o_c + 512)
    ones = at("ones", [P, 1], o_c + 768)
    assert o_c + 800 <= nc.sbuf_usable_end - base

    h_hi = at("h_hi", [P, KT, T], Q[0], F32R)
    h_lo = at("h_lo", [P, KT, T], Q[1], F32R)
    x_res = at("x_res", [P, KT, T], Q[0])
    xs_hi = at("xs_hi", [P, KT, T], Q[1], F32R)
    xs_lo = at("xs_lo", [P, KT, T], Q[2], F32R)
    merged = at("merged", [P, KT, T], Q[4])
    br_hi = [at(f"br_hi{i}", [P, CT, T], Q[3 - i], F32R) for i in range(2)]
    br_lo = [at(f"br_lo{i}", [P, CT, T], Q[3 - i] + CT * TILE, F32R) for i in range(2)]
    mv_hi = at("mv_hi", [P, KT, T], Q[3], F32R)
    mv_lo = at("mv_lo", [P, KT, T], Q[4], F32R)

    slots_d = at("slots_d", [P, 5, EXT_D], R1)
    xn = at("xn", [P, 2, 1024], R1)
    fbuf = at("fbuf", [P, 2, 1024], R1 + 8192)
    ws_raw = at("ws_raw", [P, HEADS, P], R1 + 16384)
    bd_raw = at("bd_raw", [N_SAMPLE, HEADS, N_SAMPLE], R1 + 18432)
    cc_raw = at("cc_raw", [120, 2, W_BR], R1 + 19456)
    pl_raw = at("pl_raw", [120, W_BR], R1 + 23552)
    oA = R1 + 27200
    xring = at("xring", [P, 4, 1024], oA)
    ext_a = at("ext_a", [P, 2, EXT_A], oA)
    sums = at("sums", [P, 2, EXT_A], oA + 9792)
    pooled = at("pooled", [P, T], oA + 19584)
    mem_hi = at("mem_hi", [P, KT, N_MEM], oA + 16384, F32R)
    mem_lo = at("mem_lo", [P, KT, N_MEM], oA + 24576, F32R)
    kv_out = at("kv_out", [P, MT, W_BR], oA + 12288)
    tail_d = at("tail_d", [N_SAMPLE, 2, W_BR], oA + 8192)
    tail_a = at("tail_a", [N_SAMPLE, 2, W_BR], oA + 23936)
    tail_b = at("tail_b", [N_SAMPLE, 2, W_BR], oA)
    oV = R1 + 59968
    v_tok = at("v_tok", [P, 9, W_BR], oV)
    b_h = at("b_h", [P, T], Q[4])
    ext_b = at("ext_b", [P, EXT_B], Q[4] + TILE)
    oR = R1 + 78464
    vring = at("vring", [P, 2, T], oR)
    oring = at("oring", [P, 2, T], oR + 2 * TILE)
    oK = oR + 4 * TILE
    ws_t = at("ws_t", [P, HEADS, P], oK)
    bd_t = at("bd_t", [N_SAMPLE, HEADS, N_SAMPLE], oK + 2048)
    st_pool = at("st_pool", [P, CT, 120], oK + 3072)
    st_sc = at("st_sc", [P, CT, 16], oK + 4992)
    vec_a = at("vec_a", [P, VA_N * 4], oK + 5248)
    pool_wt = at("pool_wt", [P, CT, P], oK + 5856)
    small = at("small", [P, 128], oK + 7904)
    assert oK + 8416 <= 5 * REGION
    sc_raw = at("sc_raw", [16, W_BR], o_t)
    vec_raw = at("vec_raw", [VA_N + VB_N, W_BR], o_t + 2048)
    ln_g = at("ln_g", [P, W_BR], o_t)
    ln_b = at("ln_b", [P, W_BR], o_t + 2048)
    bias_s = at("bias_s", [P, HEADS, P], o_t + TILE)
    tailbuf = at("tailbuf", [P, CT, CCONV_H + N_SAMPLE], o_t + TILE + 2048)
    ss = small[:, 0:11]
    bn = small[:, 16:70].rearrange("p (t s) -> p t s", t=9)
    bn_mv = small[:, 72:90].rearrange("p (t s) -> p t s", t=9)
    v_rstd = small[:, 91:100]
    inv_cnt = small[:, 104:119]

    kvring = at("kvring", [P, 4, MT * D_MODEL], Q[1])
    kt_hi = at("kt_hi", [P, KT, N_MEM], Q[1] + 32768, F32R)
    kt_lo = at("kt_lo", [P, KT, N_MEM], Q[1] + 40960, F32R)
    kt_s = at("kt_s", [P, 2, KT, N_MEM], Q[1] + 32768)
    v_hi = at("v_hi", [P, MT, D_MODEL], Q[1] + 49152, F32R)
    v_lo = at("v_lo", [P, MT, D_MODEL], Q[1] + 57344, F32R)
    ptm = at("ptm", [P, DEC_B, 2 * HEADS * N_SAMPLE], Q[1] + 49152)
    p_s = at("p_s", [N_SAMPLE, D_MODEL], Q[1] + 65536)
    pt_hi = [at(f"pt_hi{i}", [P, MT, 512], (o_t + TILE, Q[1])[i], F32R) for i in range(2)]
    pt_lo = [at(f"pt_lo{i}", [P, MT, 512], (o_t + 2 * TILE, Q[1] + 4096)[i], F32R) for i in range(2)]
    qm = [at(f"qm{i}", [P, KT * N_SAMPLE], o_t + TILE + (i // 2) * TILE + (i % 2) * 2048) for i in range(4)]
    probs = at("probs", [P, 4, N_MEM], o_t)
    sm = at("sm", [P, 60], o_t + 4096)

    y_tok = at("y_tok", [P, 9, D_MODEL], Q[1])
    gf = at("gf", [P, D_MODEL], Q[1] + 36864)
    junk = at("junk", [P, 2, D_MODEL], Q[1] + 40960)
    fst = at("fst", [P, 3, 9], Q[1] + 49152)

    PS = ctx.enter_context(nc.psum_tensor("PS", [P, 8, 512], F32))

    def pset(n):
        k = (n + (N_XO if n >= N_XO else 0)) % 2
        return PS[:, 3 * k:3 * k + 3, :]

    def accumulated(n, sems):
        return sems[n % 2], n // 2 + 1

    def y_bank(G):
        return PS[:, 6 + G, :] if G < 2 else pset(N_FF + 62)[:, 0, :]

    def flat(ap):
        return ap.rearrange("p a b -> p (a b)")

    def spans(ap):
        return [ap[:, 0:2 * CW].rearrange("p (c n) -> p c n", c=2), ap[:, 2 * CW:T]]

    def pspans(n):
        s = pset(n)
        return [s[:, 0:2, 0:CW], s[:, 2, 0:T - 2 * CW]]

    def pieces(ap):
        return [ap[:, 0:2 * CW].rearrange("p (c n) -> p c n", c=2), ap[:, 2 * CW:SEQ],
                ap[:, SEQ:T].rearrange("p (b l) -> p b l", b=DEC_B)]

    def ppieces(n):
        s = pset(n)
        return [s[:, 0:2, 0:CW], s[:, 2, 0:TAIL],
                s[:, 2, TAIL:TAIL + N_SAMPLE].rearrange("p (b l) -> p b l", b=DEC_B)]

    def epieces(ext, head):
        return [ext[:, head:head + 2 * CW].rearrange("p (c n) -> p c n", c=2), ext[:, head + 2 * CW:head + SEQ],
                eseq(ext, head, head)]

    def eseq(ext, head, first):
        s = ext[:, head + SEQ:head + SEQ + DEC_B * (head + DEC_L)].rearrange("p (b l) -> p b l", b=DEC_B)
        return s[:, :, first:first + DEC_L]

    def eheads(ext, head):
        s = ext[:, head + SEQ:head + SEQ + DEC_B * (head + DEC_L)].rearrange("p (b l) -> p b l", b=DEC_B)
        return s[:, :, 0:head]

    def va(row, ct):
        return vec_a[:, 4 * row + ct:4 * row + ct + 1]

    ready = [S("acc0_ready"), S("acc1_ready")]
    drained = [S("acc0_drained"), S("acc1_drained")]
    aux_ready, aux_drained = S("aux_ready"), S("aux_drained")
    w_in_dram = [S("w_raw0"), S("w_raw1")]
    w_hi_done, w_split, w_begun = S("w_hi_done"), S("w_split"), S("w_begun")
    act_step, dve_step, pool_step = S("act_step"), S("dve_step"), S("pool_step")
    ident_ready, ones_ready, zeros_ready = S("ident_ready"), S("ones_ready"), S("zeros_ready")
    x_in = [S(f"x_in{i}") for i in range(4)]
    setup_in, maps_in, vec_in, bd_in, ws_masked = (S("setup_in"), S("maps_in"), S("vec_in"), S("bd_in"),
                                                    S("ws_masked"))
    sq_done, var_done, std_done, xn_ready = S("sq_done"), S("var_done"), S("std_done"), S("xn_ready")
    hhi_done, hlo_done = S("hhi_done"), S("hlo_done")
    late_in = S("late_in")
    outs = [S("ring_out0"), S("ring_out1")]
    ring_full = S("ring_full")
    state_out = S("state_out")
    v_var, v_std, v_norm = S("v_var"), S("v_std"), S("v_norm")
    sgu_out, conv_done = S("sgu_out"), S("conv_done")
    tails_ready, pool_in_ready = S("tails_ready"), S("pool_in_ready")
    kv_stored = S("kv_stored")
    dn_sum, dn_mean, dn_sq, dn_acc, dn_var, dn_std, dn_y, dn_out = (
        S("dn_sum"), S("dn_mean"), S("dn_sq"), S("dn_acc"), S("dn_var"), S("dn_std"), S("dn_y"), S("dn_out"))
    stage_in, br_hi_done, br_lo_done = S("stage_in"), S("br_hi_done"), S("br_lo_done")
    gated, mv_hi_done, mv_lo_done = S("gated"), S("mv_hi_done"), S("mv_lo_done")
    xres_in = [S(f"xres_in{i}") for i in range(4)]
    scaled, xs_hi_done, xs_lo_done, res_sq, sumsq = (
        S("scaled"), S("xs_hi_done"), S("xs_lo_done"), S("res_sq"), S("sumsq"))
    r_var, r_std, r_ready = S("r_var"), S("r_std"), S("r_ready")
    xs_used = S("xs_used")
    kv_in = [S(f"kv_in{i}") for i in range(4)]
    at_t, at_kh, at_kl, at_vh, at_vl = S("at_t"), S("at_kh"), S("at_kl"), S("at_vh"), S("at_vl")
    ks_a, ks_d, hid_hi = S("ks_a"), S("ks_d"), S("hid_hi")
    sc_ready, mx_ready, e_ready, rs_ready, p_ready, pt_ready, pt_hi_done, pt_lo_done, pv_ready, o_hi, o_lo = (
        S("sc_ready"), S("mx_ready"), S("e_ready"), S("rs_ready"), S("p_ready"), S("pt_ready"), S("pt_hi_done"),
        S("pt_lo_done"), S("pv_ready"), S("o_hi"), S("o_lo"))
    qm_zero, ptm_zero = S("qm_zero"), S("ptm_zero")
    qm_ready, ks_t, ss_ready = S("qm_ready"), S("ks_t"), S("ss_ready")
    sm_mx, sm_e, sm_p, sm_t, sm_pt, so_ready, so_copied, so_t, so_hi, so_lo = (
        S("sm_mx"), S("sm_e"), S("sm_p"), S("sm_t"), S("sm_pt"), S("so_ready"), S("so_copied"), S("so_t"),
        S("so_hi"), S("so_lo"))
    relu_done, hid_ready = S("relu_done"), S("hid_ready")
    last_ready, last_added, last_rows_ready, last_copied = (S("last_ready"), S("last_added"), S("last_rows_ready"),
                                                            S("last_copied"))
    fst_ready, fs_sq, fs_var, fs_std, y_ready = S("fst_ready"), S("fs_sq"), S("fs_var"), S("fs_std"), S("y_ready")
    y_out = [S(f"y_out{i}") for i in range(4)]
    gf_in = S("gf_in")

    xt_dram, br_dram, kv_dram = scratch["xt"], scratch["branch"], scratch["kv"]
    w_in = a["w_in"][0].rearrange("(k p) n -> p k n", p=P)
    w_branch = a["w_branch"][0].rearrange("b (k p) n -> b p k n", p=P)
    w_sq = {k: a[k][0].rearrange("(k p) n -> p k n", p=P)
            for k in ("w_mix_out", "w_xq", "w_xk", "w_xv", "w_xo", "w_ff1")}
    w_ff2 = a["w_ff2"][0].rearrange("(c k p) n -> c p k n", p=P, k=KT)
    x_prompt = a["x_prompt"][0]
    x_sample = a["x_sample"].rearrange("b l d -> (b l) d")
    mem = a["mem_prompt"][0]

    def x_rows(t):
        if t < 8:
            return x_prompt[P * t:P * t + P, :]
        return x_sample if t == 8 else mem[P * (t - 9):P * (t - 8), :]

    def x_height(t):
        return N_SAMPLE if t == 8 else P

    def hsplit(t):
        if t < 9:
            t0, tw = TOK_TILES[t]
            return h_hi[:, :, t0:t0 + tw], h_lo[:, :, t0:t0 + tw]
        m0 = (t - 9) * P
        return mem_hi[:, :, m0:m0 + P], mem_lo[:, :, m0:m0 + P]

    def scaled_tile(t):
        if t < 9:
            return drained[(N_P0 + t) % 2], (N_P0 + t) // 2 + 1
        return aux_drained, AUX[f"m{t - 9}"] + 1

    def tile_psum(t):
        return flat(PS[:, 0:2, :]) if t < 9 and t % 2 == 0 else flat(PS[:, 6:8, :])

    def tile_transposed(t):
        if t < 9:
            return ready[(N_P0 + t) % 2], (N_P0 + t) // 2 + 1
        return aux_ready, AUX[f"m{t - 9}"] + 1

    def stage_of(q):
        return vring[:, 1, :] if q == 0 else tmp[0][:, :]

    SETUP, VECTORS = 16 * 4, 16 * 11

    block = ctx.enter_context(nc.Block())

    @block.sync
    def _(sp):
        def slab(z, src, i=None, per=0, kts=KT):
            if i is not None or z >= 2:
                sp.wait_ge(w_split, 2 * (z - 1) if i is None else i * (2 * per) + 2 * (z - 1))
            dst = w_raw[:, z % 2, :].rearrange("p (k n) -> p k n", k=kts)
            sp.dma_start(dst, src).then_inc(w_in_dram[z % 2], 16)

        def load_x(n, t):
            if n >= 4:
                m = n - 4
                if m < 11:
                    sp.wait_ge(xn_ready, m + 1)
                else:
                    sp.wait_ge(aux_ready, AUX[f"x{m - 11}"] + 1)
            sp.dma_start(xring[0:x_height(t), n % 4, :], x_rows(t)).then_inc(x_in[n % 4], 16)

        for n in range(4):
            load_x(n, n)

        def load(dst, src, sem=setup_in):
            sp.dma_start(dst, src, allow_slow_non_contiguous=True).then_inc(sem, 16)

        def first_slab(z):
            kind, j = PHASE1[z]
            if kind == "K":
                g, q = j // 4, j % 4
                slab(z, w_sq["w_xk"][:, 2 * q:2 * q + 2, W_BR * g:W_BR * g + W_BR], kts=2)
            else:
                col = IN_CV + j if kind == "CV" else (IN_DB, IN_DA)[j % 2] + j // 2
                slab(z, w_in[:, :, col * P:(col + 1) * P])

        first_slab(0)
        load(ws_raw[:, :, :], a["sgu_w"][0].rearrange("g t s -> t g s"))
        load(pl_raw[:, :], a["state_pool"][0].rearrange("b l w -> (b l) w"))
        load(sc_raw[:, :], a["state_sconv"][0].rearrange("b l w -> (b l) w"))
        load(cc_raw[:, :, :], a["state_cconv"][0].rearrange("(h b) l w -> (b l) h w", h=2))
        for n in range(4, 11):
            load_x(n, n)
            if n == 5:
                first_slab(1)
        load(pool_wt[:, :, :], a["pool_w"][0].rearrange("g i j -> i g j"), maps_in)
        load(bias_s[:, :, :], a["sgu_b"][0].unsqueeze(0).broadcast_to([P, HEADS, P]), maps_in)
        slabs_after = {13: 2, 15: 3, 18: 4}
        for n in range(11, 20):
            load_x(n, n - 11)
            if n in slabs_after:
                first_slab(slabs_after[n])
        for z in range(5, len(PHASE1)):
            first_slab(z)
        for ct in range(CT):
            slab(S_CU + 3 * ct, w_in[:, :, (IN_CU + ct) * P:(IN_CU + ct + 1) * P])
            for j in range(2):
                g, q = ct // 2, 2 * (ct % 2) + j
                slab(S_CU + 3 * ct + 1 + j, w_sq["w_xv"][:, 2 * q:2 * q + 2, W_BR * g:W_BR * g + W_BR], kts=2)
        for ct in range(CT):
            slab(S_A + ct, w_in[:, :, (IN_A + ct) * P:(IN_A + ct + 1) * P])
        for ct in range(CT):
            for j, col in enumerate((IN_BH, IN_BC, IN_BB)):
                slab(S_B + 3 * ct + j, w_in[:, :, (col + ct) * P:(col + ct + 1) * P])

        def gate_slabs(q, k, i=None, step=0):
            for j, (what, mm) in enumerate((("g", 0), ("g", 1), ("p", 0), ("g", 2), ("g", 3), ("p", 2))):
                z = S_GATE + 12 * q + 6 * step + j
                col = (4 * step + mm) * P + ((IN_G + 8 * k) * P if what == "g" else 0)
                if i is not None:
                    col = sp.snap(i * 4 * P + col)
                if what == "g":
                    slab(z, w_in[:, :, bass.ds(col, P)], i, 6)
                else:
                    slab(z, w_branch[k][:, :, bass.ds(col, 2 * P)], i, 6, kts=CT)

        for q, k in enumerate(BRANCHES):
            if k == 0:
                for step in range(2):
                    gate_slabs(q, k, step=step)
            else:
                with sp.Fori(0, 2) as i:
                    gate_slabs(q, k, i)

        def square(z0, w, m0, m1):
            with sp.Fori(0, (m1 - m0) // 2) as i:
                for j in range(2):
                    col = sp.snap(i * 2 * P + (m0 + j) * P)
                    slab(z0 + m0 + j, w[:, :, bass.ds(col, P)], i, 2)

        square(S_MIX, w_sq["w_mix_out"], 0, 2)
        n = N_GATE + 62
        sp.wait_ge(ready[n % 2], n // 2 + 1)
        for i in range(4):
            sp.dma_start(x_res[:, 2 * i:2 * i + 2, :],
                         xt_dram[2 * i:2 * i + 2].rearrange("k p t -> p k t")).then_inc(xres_in[i], 16)
        square(S_MIX, w_sq["w_mix_out"], 2, 8)
        square(S_Q, w_sq["w_xq"], 0, 8)

        def kv_load(n):
            if n < 2:
                src = kv_dram[n]
            else:
                name = "cache_mem_k" if n < 10 else "cache_mem_v"
                src = a[name][0, (n - 2) % 8].rearrange("m h d -> m (h d)")
            sp.dma_start(kvring[:, n % 4, :].rearrange("p (m d) -> p m d", m=MT),
                         src.rearrange("(m p) d -> p m d", p=P)).then_inc(kv_in[n % 4], 16)

        sp.wait_ge(kv_stored, 8 * 16)
        for n in range(4):
            if n < 3:
                sp.wait_ge(xs_used, n + 1)
            else:
                sp.wait_ge(ready[(N_Q + 7) % 2], (N_Q + 7) // 2 + 1)
            kv_load(n)
        square(S_XO, w_sq["w_xo"], 0, 2)
        for n in (5, 4, *range(6, 18)):
            if n == 4:
                sp.wait_ge(pv_ready, 16)
            elif n == 5:
                sp.wait_ge(at_vl, 1)
            elif n < 14:
                sp.wait_ge(ks_t, n - 5)
            else:
                sp.wait_ge(so_ready, n - 13)
            kv_load(n)
        square(S_XO, w_sq["w_xo"], 2, 8)
        for c in range(4):
            square(S_FF + 16 * c, w_sq["w_ff1"][:, :, c * D_MODEL:(c + 1) * D_MODEL], 0, 8)
            if c < 3:
                square(S_FF + 16 * c + 8, w_ff2[c], 0, 8)
        square(S_FF + 56, w_ff2[3], 0, 2)
        n = N_FF + 16 * 3 + 7
        sp.wait_ge(ready[n % 2], n // 2 + 1)
        sp.dma_start(gf[:, :], a["norm_f_g"].unsqueeze(0).broadcast_to([P, D_MODEL])).then_inc(gf_in, 16)
        square(S_FF + 56, w_ff2[3], 2, 8)
        for t, (t0, tw) in enumerate(TOK_TILES):
            sp.wait_ge(y_ready, t + 1)
            dst = o["y_prompt"][0][t0:t0 + tw, :] if t < 8 else o["y_sample"].rearrange("b l d -> (b l) d")
            sp.dma_start(dst, y_tok[0:tw, t, :]).then_inc(y_out[t % 4], 16)
        for j in range(4):
            sp.wait_ge(y_out[j], 16 * len(range(j, 9, 4)))

    @block.gpsimd
    def _(pool):
        chain = Chain(pool, pool_step)
        pool.wait_ge(ones_ready, 1)
        chain.link(nc.gpsimd.memset(ident[:, :], 0.0))
        nc.gpsimd.affine_select(out=ident[:, :], in_=ident[:, :], compare_op=ALU.not_equal, fill=1.0, base=0,
                                pattern=[[-1, P]], channel_multiplier=1).then_inc(ident_ready, 1)
        chain.link(nc.gpsimd.memset(bd_raw[:, :, :], 0.0))
        pool.wait_ge(pool_step, 2)
        for b in range(DEC_B):
            pool.dma_start(bd_raw[8 * b:8 * b + 8, :, 8 * b:8 * b + 8],
                           a["sgu_w"][0, :, 0:8, 0:8].rearrange("g t s -> t g s"),
                           allow_slow_non_contiguous=True).then_inc(bd_in, 16)
        def split(z, i=None):
            pool.wait_ge(w_in_dram[z % 2], 16 * (z // 2 + 1) if i is None else i * 16 + 16 * (z // 2 + 1))
            if i is not None:
                pool.wait_ge(w_begun, i * 2 + z)
            for half in range(2):
                cols = slice(512 * half, 512 * half + 512)
                nc.gpsimd.tensor_tensor(w_hi[:, z % 2, cols], w_raw[:, z % 2, cols],
                                        ones[:, 0:1].broadcast_to([P, 512]), ALU.mult).then_inc(w_hi_done, 1)
                count = 2 * z + half + 1
                pool.wait_ge(w_hi_done, count if i is None else i * 4 + count)
                nc.gpsimd.tensor_tensor(w_lo[:, z % 2, cols], w_raw[:, z % 2, cols],
                                        w_hi[:, z % 2, cols].bitcast(F32), ALU.subtract).then_inc(w_split, 1)

        split(0)
        pool.wait_ge(bd_in, 16 * DEC_B)
        pool.wait_ge(setup_in, SETUP)
        nc.gpsimd.affine_select(out=ws_raw[:, :, :], in_=ws_raw[:, :, :], compare_op=ALU.is_ge, fill=0.0, base=0,
                                pattern=[[0, HEADS], [-1, P]], channel_multiplier=1).then_inc(ws_masked, 1)
        nc.gpsimd.affine_select(out=bd_raw[:, :, :], in_=bd_raw[:, :, :], compare_op=ALU.is_ge, fill=0.0, base=0,
                                pattern=[[0, HEADS], [-1, N_SAMPLE]], channel_multiplier=1).then_inc(ws_masked, 1)

        for t in range(11):
            pool.wait_ge(hhi_done, t + 1)
            pool.wait_ge(*scaled_tile(t))
            hi, lo = hsplit(t)
            fb = fbuf[:, t % 2, 0:KT * x_height(t)].rearrange("p (k n) -> p k n", k=KT)
            nc.gpsimd.tensor_tensor(lo, fb, hi.bitcast(F32), ALU.subtract).then_inc(hlo_done, 1)
            if t == 8:
                split(1)
        with pool.Fori(0, S_XO // 2 - 1) as i:
            for j in range(2):
                split(2 + j, i)
        pool.wait_ge(kv_in[1], 16)
        pool.wait_ge(ready[(N_Q + 7) % 2], (N_Q + 7) // 2 + 1)
        nc.gpsimd.tensor_tensor(flat(v_hi[:, :, :]), kvring[:, 1, :], ones[:, 0:1].broadcast_to([P, MT * D_MODEL]),
                                ALU.mult).then_inc(at_vh, 1)
        pool.wait_ge(at_vh, 1)
        nc.gpsimd.tensor_tensor(flat(v_lo[:, :, :]), kvring[:, 1, :], flat(v_hi[:, :, :]).bitcast(F32),
                                ALU.subtract).then_inc(at_vl, 1)
        pool.wait_ge(pv_ready, 14)
        for r in range(4):
            ins = nc.gpsimd.memset(qm[r][:, :], 0.0)
        ins.then_inc(qm_zero, 1)
        pool.wait_ge(pv_ready, 16)
        nc.gpsimd.memset(ptm[:, :, :], 0.0).then_inc(ptm_zero, 1)
        with pool.Fori(0, (S_END - S_XO) // 2) as i:
            for j in range(2):
                split(S_XO + j, i)

    @block.tensor
    def _(pe):
        tr = nc.tensor.transpose
        mmul = nc.tensor.matmul

        def take(n, i=None, per=0):
            if i is None:
                if n >= 2:
                    pe.wait_ge(drained[n % 2], n // 2)
            else:
                pe.wait_ge(drained[n % 2], i * (per // 2) + n // 2)

        def take_aux(name):
            if AUX[name] > 0:
                pe.wait_ge(aux_drained, AUX[name])

        def terms(slot, ofs, r_hi, r_lo):
            wh, wl = w_hi[:, slot, ofs:ofs + P], w_lo[:, slot, ofs:ofs + P]
            return ((wh, r_hi), (wh, r_lo), (wl, r_hi))

        def wait_half(z, half, i=None, per_z=0):
            count = 2 * z + half + 1
            pe.wait_ge(w_split, count if i is None else i * (2 * per_z) + count)

        def product(n, z, r_hi, r_lo, i=None, per_n=0, per_z=0, kts=KT, ofs=None, wait_slab=True, arrive=None,
                    between=None, signal=True, used=None):
            take(n, i, per_n)
            acc = pset(n)
            first = wait_slab
            for kt in range(kts):
                if wait_slab and kt in (0, kts // 2):
                    wait_half(z, int(kt > 0), i, per_z)
                if arrive is not None:
                    pe.wait_ge(arrive[0], arrive[1] + kt + 1)
                o0 = kt * P if ofs is None else ofs(kt)
                for e, (w, r) in enumerate(terms(z % 2, o0, r_hi, r_lo)):
                    for c, (c0, cw) in enumerate(CHUNKS):
                        mm = mmul(acc[:, c, 0:cw], w, r[:, kt, c0:c0 + cw],
                                  start=(kt == 0 and e == 0), stop=(kt == kts - 1 and e == 2))
                        if first:
                            mm.then_inc(w_begun, 1)
                            first = False
                if used is not None and kt % 2 == 1 and kt < kts - 1:
                    mm.then_inc(used, 1)
                if kt == kts - 1 and signal:
                    mm.then_inc(ready[n % 2], 1)
                if between and kt in between:
                    for work in between[kt]:
                        work()

        def ones_sum(n, tile, wait):
            take(n)
            pe.wait_ge(*wait)
            for c, (c0, cw) in enumerate(CHUNKS):
                mm = mmul(pset(n)[:, c, 0:cw], ones[:, 0:1].broadcast_to([P, P]), tile[:, c0:c0 + cw],
                          start=True, stop=True)
            mm.then_inc(ready[n % 2], 1)

        def product_chunk(n, z, c, r_hi, r_lo, between=None, kts=range(KT), free=False):
            c0, cw = CHUNKS[c]
            if c == 0 and not free:
                take(n)
            for kt in kts:
                if c == 0 and kt in (0, KT // 2):
                    wait_half(z, int(kt > 0))
                for e, (w, r) in enumerate(terms(z % 2, kt * P, r_hi, r_lo)):
                    mm = mmul(pset(n)[:, c, 0:cw], w, r[:, kt, c0:c0 + cw],
                              start=(kt == 0 and e == 0), stop=(kt == KT - 1 and e == 2))
                    if c == 0 and kt == 0 and e == 0:
                        mm.then_inc(w_begun, 1)
                if between and kt in between:
                    between[kt]()
            return mm

        def square_sum(name, n, count):
            take_aux(name)
            pe.wait_ge(sumsq, count)
            for c in range(3):
                dst = PS[:, 6 + c, :] if c < 2 else pset(n)[:, 2, CW:CW + N_SAMPLE]
                mm = mmul(dst, ones[:, 0:1].broadcast_to([P, P]), tmp[0][:, 512 * c:min(512 * c + 512, T)],
                          start=True, stop=True)
                if c == 1:
                    mm.then_inc(aux_ready, 1)
            mm.then_inc(ready[n % 2], 1)

        def kv_group(name, z, quarter):
            if quarter == 0:
                take_aux(name)
                pe.wait_ge(hlo_done, 11)
            for kk in range(2):
                wait_half(z, kk)
                kt = 2 * quarter + kk
                for e, (m, w) in enumerate(((mem_hi, w_hi), (mem_lo, w_hi), (mem_hi, w_lo))):
                    for mt in range(MT):
                        mm = mmul(PS[:, 6 + mt, :], m[:, kt, mt * P:(mt + 1) * P],
                                  w[:, z % 2, kk * W_BR:(kk + 1) * W_BR],
                                  start=(kt == 0 and e == 0), stop=(kt == KT - 1 and e == 2))
                        if kk == 0 and e == 0 and mt == 0:
                            mm.then_inc(w_begun, 1)
            if quarter == 3:
                mm.then_inc(aux_ready, 1)

        def x_transposed(t):
            name = f"x{t}"
            take_aux(name)
            n = 11 + t
            pe.wait_ge(x_in[n % 4], 16 * (n // 4 + 1))
            h = x_height(t)
            for kt in range(KT):
                mm = tr(flat(PS[:, 6:8, :])[:, kt * h:kt * h + h], xring[0:h, n % 4, kt * P:(kt + 1) * P],
                        ident[0:h, 0:h])
            mm.then_inc(aux_ready, 1)

        def v_prompt(g):
            take_aux(f"v{g}a")
            n = N_OF["CV", g]
            pe.wait_ge(drained[n % 2], n // 2 + 1)
            for t in range(8):
                mm = tr(flat(PS[:, 6:8, :])[:, t * P:(t + 1) * P], vring[:, g % 2, t * P:(t + 1) * P], ident[:, :])
            mm.then_inc(aux_ready, 1)

        def v_sample(g):
            take_aux(f"v{g}b")
            tr(PS[0:N_SAMPLE, 6, 0:P], vring[:, g % 2, SEQ:T], ident[:, :]).then_inc(aux_ready, 1)

        def tails(name, head, count):
            take_aux(name)
            pe.wait_ge(tails_ready, count)
            for ct in range(CT):
                tr(PS[0:N_SAMPLE, 6, ct * P:(ct + 1) * P], tailbuf[:, ct, CCONV_H:], ident[:, :])
                mm = tr(PS[0:head, 7, ct * P:(ct + 1) * P], tailbuf[:, ct, 0:head], ident[:, :])
            mm.then_inc(aux_ready, 1)

        def normalised(t):
            if t < 9:
                take(N_P0 + t)
            else:
                take_aux(f"m{t - 9}")
            pe.wait_ge(xn_ready, t + 1)
            h = x_height(t)
            for kt in range(KT):
                mm = tr(tile_psum(t)[:, kt * h:kt * h + h], xn[0:h, t % 2, kt * P:(kt + 1) * P], ident[0:h, 0:h])
            mm.then_inc(tile_transposed(t)[0], 1)

        def vector_tables():
            pe.wait_ge(vec_in, VECTORS)
            nv = VA_N + VB_N
            for ct in range(CT):
                mm = tr(PS[:, 2, ct * nv:(ct + 1) * nv], vec_raw[:, ct * P:(ct + 1) * P], ident[0:nv, 0:nv])
            mm.then_inc(aux_ready, 1)

        def spatial_weights():
            take_aux("ws")
            pe.wait_ge(ws_masked, 2)
            for g in range(HEADS):
                tr(PS[:, 2, g * P:(g + 1) * P], ws_raw[:, g, :], ident[:, :])
                mm = tr(PS[0:N_SAMPLE, 5, g * N_SAMPLE:(g + 1) * N_SAMPLE], bd_raw[:, g, :],
                        ident[0:N_SAMPLE, 0:N_SAMPLE])
            mm.then_inc(aux_ready, 1)

        def short_states():
            take_aux("pl")
            pe.wait_ge(setup_in, SETUP)
            for ct in range(CT):
                tr(PS[:, 2, ct * 120:(ct + 1) * 120], pl_raw[:, ct * P:(ct + 1) * P], ident[0:120, 0:120])
                mm = tr(PS[:, 5, ct * 16:(ct + 1) * 16], sc_raw[:, ct * P:(ct + 1) * P], ident[0:16, 0:16])
            mm.then_inc(aux_ready, 1)

        n_first = N_OF["D", 0]

        def first_chunk(c, half=None):
            pe.wait_ge(hlo_done, (3, 6, 9)[c])
            if c == 2:
                take_aux("m0")
            kts = range(KT) if half is None else range(4 * half, 4 * half + 4)
            return product_chunk(n_first, 0, c, h_hi, h_lo, kts=kts, free=True)

        pe.wait_ge(ident_ready, 1)
        extra = {0: vector_tables, 3: spatial_weights, 5: short_states}
        for t in range(9):
            normalised(t)
            if t in extra:
                extra[t]()
            if t in (5, 6):
                first_chunk(0, t - 5)
            if t in (7, 8):
                first_chunk(1, t - 7)
        first_chunk(2).then_inc(ready[n_first % 2], 1)

        def conv_states():
            take_aux("cc")
            for half in range(2):
                for ct in range(CT):
                    mm = tr(PS[:, 6 + half, ct * 120:(ct + 1) * 120], cc_raw[:, half, ct * P:(ct + 1) * P],
                            ident[0:120, 0:120])
            mm.then_inc(aux_ready, 1)

        def v_rows(g, *x_tiles):
            work = {1: [lambda: v_prompt(g)], 3: [lambda: v_sample(g)]}
            for kt, t in zip((5, 7), x_tiles):
                work[kt] = [lambda t=t: x_transposed(t)]
            return work

        between = {("D", 1): {0: [lambda: normalised(9)], 2: [lambda: normalised(10)], 4: [conv_states],
                              5: [lambda: x_transposed(0)], 7: [lambda: x_transposed(1)]},
                   ("CV", 0): {1: [lambda: x_transposed(2)], 4: [lambda: x_transposed(3)]},
                   ("CV", 1): v_rows(0, 4, 5), ("CV", 2): v_rows(1, 6), ("CV", 3): v_rows(2, 7),
                   ("D", 2): v_rows(3, 8)}
        pe.wait_ge(aux_drained, AUX["m0"])
        for z, (kind, j) in enumerate(PHASE1):
            if kind == "K":
                kv_group(f"K{j // 4}", z, j % 4)
            elif z > 0:
                product(N_OF[kind, j], z, h_hi, h_lo, between=between.get((kind, j)))
        for g in range(HEADS):
            product(N_CU + 2 * g, S_CU + 3 * g, h_hi, h_lo)
            if g == 0:
                tails("tail_d", CCONV_H, CT)
            kv_group(f"V{g // 2}", S_CU + 3 * g + 1, 2 * (g % 2))
            n = N_CU + 2 * g + 1
            take(n)
            pe.wait_ge(v_norm, 9)
            acc = flat(pset(n))
            for t in range(8):
                mmul(acc[:, t * P:(t + 1) * P], v_tok[:, t, g * P:(g + 1) * P], ws_t[:, g, :], start=True, stop=True)
            mmul(acc[:, SEQ:T], v_tok[0:N_SAMPLE, 8, g * P:(g + 1) * P], bd_t[:, g, :],
                 start=True, stop=True).then_inc(ready[n % 2], 1)
            kv_group(f"V{g // 2}", S_CU + 3 * g + 2, 2 * (g % 2) + 1)
        def pool_map(g):
            n = N_A_MAP[g]
            take(n)
            pe.wait_ge(maps_in, 32)
            pe.wait_ge(pool_in_ready, g + 1)
            for c, (c0, cw) in enumerate(CHUNKS):
                mm = mmul(pset(n)[:, c, 0:cw], pool_wt[:, g, :], pooled[:, c0:c0 + cw], start=True, stop=True)
            mm.then_inc(ready[n % 2], 1)

        for g in range(CT):
            product(N_A_IN[g], S_A + g, h_hi, h_lo)
            if g >= 1:
                pool_map(g - 1)
        for ct in range(CT):
            product(N_B_H[ct], S_B + 3 * ct, h_hi, h_lo)
            if ct == 0:
                pool_map(CT - 1)
                tails("tail_a", POOL_H, 2 * CT)
            product(N_B_C[ct], S_B + 3 * ct + 1, h_hi, h_lo)
            if ct == 2:
                ones_sum(N_VAR, tmp[2], (dn_acc, CT - 1))
            if ct == 1:
                ones_sum(N_MEAN, tmp[2], (dn_sum, 1))
            product(N_B_B[ct], S_B + 3 * ct + 2, h_hi, h_lo)

        tails("tail_b", SCONV_H, 3 * CT)
        for q in range(4):
            bh, bl = br_hi[q % 2], br_lo[q % 2]
            with pe.Fori(0, 2) as i:
                for pair in range(2):
                    z = S_GATE + 12 * q + 3 * pair
                    n = N_GATE + 16 * q + 4 * pair
                    for j in range(2):
                        product(n + j, z + j, h_hi, h_lo, i, 8, 6)
                    pe.wait_ge(br_lo_done, 4 * q + 4)
                    for j in range(2):
                        product(n + 2 + j, z + 2, bh, bl, i, 8, 6, kts=CT,
                                ofs=lambda kt, j=j: (2 * kt + j) * P, wait_slab=(j == 0))

        def products(n0, z0, m0, m1, r_hi, r_lo):
            with pe.Fori(0, (m1 - m0) // 2) as i:
                for j in range(2):
                    product(n0 + m0 + j, z0 + m0 + j, r_hi, r_lo, i, 2, 2)

        product(N_MIX, S_MIX, mv_hi, mv_lo, arrive=(mv_lo_done, 0))
        product(N_MIX + 1, S_MIX + 1, mv_hi, mv_lo)
        products(N_MIX, S_MIX, 2, 8, mv_hi, mv_lo)
        product(N_Q, S_Q, xs_hi, xs_lo, arrive=(xs_lo_done, 0), signal=False)
        square_sum("sum0", N_Q, KT + 1)
        product(N_Q + 1, S_Q + 1, xs_hi, xs_lo)
        products(N_Q, S_Q, 2, 6, xs_hi, xs_lo)
        product(N_Q + 6, S_Q + 6, xs_hi, xs_lo)
        product(N_Q + 7, S_Q + 7, xs_hi, xs_lo, used=xs_used)

        pe.wait_ge(aux_drained, AUX["sum0"] + 1)
        pe.wait_ge(kv_in[0], 16)
        for g in range(4):
            if g == 2:
                pe.wait_ge(*accumulated(N_Q + 6, drained))
            for kk in range(2):
                for mt in range(MT):
                    kt = 2 * g + kk
                    mm = tr(PS[:, K_BANKS[g], (2 * kk + mt) * P:(2 * kk + mt + 1) * P],
                            kvring[:, 0, mt * D_MODEL + kt * P:mt * D_MODEL + (kt + 1) * P], ident[:, :])
            mm.then_inc(at_t, 1)
        pe.wait_ge(*accumulated(N_Q + 7, drained))

        def score(u):
            h, tk = u // 8, u % 8
            if u >= 4:
                pe.wait_ge(e_ready, u - 3)
            if tk == 0:
                pe.wait_ge(at_kl, h + 1)
                pe.wait_ge(mv_lo_done, KT + 2 * h + 2)
            for dt in range(2):
                d = 2 * h + dt
                for e, (q_, k_) in enumerate(((mv_hi, kt_hi), (mv_lo, kt_hi), (mv_hi, kt_lo))):
                    mm = mmul(PS[:, u % 4, 0:N_MEM], q_[:, d, tk * P:(tk + 1) * P], k_[:, d, :],
                              start=(dt == 0 and e == 0), stop=(dt == 1 and e == 2))
            mm.then_inc(sc_ready, 1)

        for u in range(3):
            score(u)
        def attend(G, dt):
            pe.wait_ge(pt_lo_done, 4 * G + 4)
            pe.wait_ge(at_vl, 1)
            if G >= 1:
                pe.wait_ge(o_lo, 2 * G - 1 + dt)
            d0 = (G // 2) * HEAD_DIM + dt * P
            for mt in range(MT):
                for e, (v_, p_) in enumerate(((v_hi, pt_hi), (v_lo, pt_hi), (v_hi, pt_lo))):
                    mm = mmul(PS[:, 6 + dt, :], v_[:, mt, d0:d0 + P], p_[G % 2][:, mt, :],
                              start=(mt == 0 and e == 0), stop=(mt == 1 and e == 2))
            mm.then_inc(pv_ready, 1)

        for u in range(32 + 4):
            if u + 3 < 32:
                score(u + 3)
            if u < 32:
                pe.wait_ge(p_ready, u + 1)
                if u == 0:
                    pe.wait_ge(at_kl, 4)
                if u >= 2:
                    pe.wait_ge(pt_lo_done, u - 1)
                for mt in range(MT):
                    mm = tr(PS[:, 4 + u % 2, mt * P:(mt + 1) * P], probs[:, u % 4, mt * P:(mt + 1) * P],
                            ident[:, :])
                mm.then_inc(pt_ready, 1)
            if u in ATTEND:
                attend(*ATTEND[u])

        def sample_scores(b):
            pe.wait_ge(ks_a, b + 1)
            pe.wait_ge(ks_d, b + 1)
            pe.wait_ge(qm_ready, b + 1)
            for h in range(HEADS):
                for dt in range(2):
                    d = 2 * h + dt
                    mm = mmul(PS[0:N_SAMPLE, 4 + h, 0:N_MEM], qm[b % 4][:, d * N_SAMPLE:(d + 1) * N_SAMPLE],
                              kt_s[:, b % 2, d, :], start=(b == 0 and dt == 0), stop=(b == 7 and dt == 1))
            mm.then_inc(ss_ready, 1)

        pe.wait_ge(e_ready, 32)
        for b in range(DEC_B):
            n = 2 + b
            pe.wait_ge(kv_in[n % 4], 16 * (n // 4 + 1))
            if b >= 1:
                pe.wait_ge(ks_a, b)
                pe.wait_ge(ks_d, b)
            for kt in range(KT):
                for mt in range(MT):
                    mm = tr(PS[:, kt // 2, (2 * (kt % 2) + mt) * P:(2 * (kt % 2) + mt + 1) * P],
                            kvring[:, n % 4, mt * D_MODEL + kt * P:mt * D_MODEL + (kt + 1) * P], ident[:, :])
            mm.then_inc(ks_t, 1)
            if b == 1:
                pe.wait_ge(o_lo, 16)
                pe.wait_ge(pt_lo_done, 32)
            if b >= 1:
                sample_scores(b - 1)
        sample_scores(DEC_B - 1)
        product_chunk(N_XO, S_XO, 0, mv_hi, mv_lo)
        pe.wait_ge(sm_p, 1)
        for j in range(2 * HEADS):
            mm = tr(PS[:, 3, j * N_SAMPLE:(j + 1) * N_SAMPLE], p_s[:, j * P:(j + 1) * P],
                    ident[0:N_SAMPLE, 0:N_SAMPLE])
        mm.then_inc(sm_t, 1)
        for b in range(DEC_B):
            n = 10 + b
            pe.wait_ge(kv_in[n % 4], 16 * (n // 4 + 1))
            if b == 0:
                pe.wait_ge(sm_pt, 1)
            for h in range(HEADS):
                for mt in range(MT):
                    j = 2 * h + mt
                    v0 = mt * D_MODEL + h * HEAD_DIM
                    mm = mmul(PS[0:N_SAMPLE, 4 + h, 0:HEAD_DIM], ptm[:, b, j * N_SAMPLE:(j + 1) * N_SAMPLE],
                              kvring[:, n % 4, v0:v0 + HEAD_DIM], start=(b == 0 and mt == 0),
                              stop=(b == 7 and mt == 1))
            mm.then_inc(so_ready, 1)
        product_chunk(N_XO, S_XO, 1, mv_hi, mv_lo)
        pe.wait_ge(so_copied, 1)
        for kt in range(KT):
            mm = tr(PS[:, 3, kt * N_SAMPLE:(kt + 1) * N_SAMPLE], p_s[:, kt * P:(kt + 1) * P],
                    ident[0:N_SAMPLE, 0:N_SAMPLE])
        mm.then_inc(so_t, 1)

        pe.wait_ge(so_lo, 1)
        product_chunk(N_XO, S_XO, 2, mv_hi, mv_lo).then_inc(ready[N_XO % 2], 1)
        product(N_XO + 1, S_XO + 1, mv_hi, mv_lo)
        products(N_XO, S_XO, 2, 8, mv_hi, mv_lo)
        for c in range(4):
            n1, n2, z = N_FF + 16 * c, N_FF + 16 * c + 8, S_FF + 16 * c
            if c == 0:
                product(n1, z, xs_hi, xs_lo, arrive=(xs_lo_done, KT), signal=False)
                square_sum("sum1", n1, 2 * KT + 2)
                product(n1 + 1, z + 1, xs_hi, xs_lo)
                products(n1, z, 2, 8, xs_hi, xs_lo)
            else:
                products(n1, z, 0, 8, xs_hi, xs_lo)
            product(n2, z + 8, mv_hi, mv_lo, arrive=(hid_ready, KT * c))
            product(n2 + 1, z + 9, mv_hi, mv_lo)
            if c < 3:
                products(n2, z + 8, 2, 8, mv_hi, mv_lo)

        def y_prompt_rows(m):
            n = N_FF + 16 * 3 + 8 + m
            take_aux(f"y{m}a")
            pe.wait_ge(drained[n % 2], n // 2 + 1)
            for t in range(8):
                mm = tr(flat(PS[:, 6:8, :])[:, t * P:(t + 1) * P], x_res[:, m, t * P:(t + 1) * P], ident[:, :])
            mm.then_inc(aux_ready, 1)

        def y_sample_rows(m):
            take_aux(f"y{m}b")
            tr(PS[0:N_SAMPLE, 6, 0:P], x_res[:, m, SEQ:T], ident[:, :]).then_inc(aux_ready, 1)

        for m in range(2, KT - 1):
            between = {1: [lambda: y_prompt_rows(m - 1)], 4: [lambda: y_sample_rows(m - 1)]}
            if m == 2:
                between = {1: [lambda: y_prompt_rows(0)], 3: [lambda: y_sample_rows(0)],
                           5: [lambda: y_prompt_rows(1)], 7: [lambda: y_sample_rows(1)]}
            product(N_FF + 56 + m, S_FF + 56 + m, mv_hi, mv_lo, between=between)
        def last_rows(G):
            pe.wait_ge(last_added, G + 1)
            for t in Y_GROUPS[G]:
                t0, tw = TOK_TILES[t]
                c0 = (t - Y_GROUPS[G][0]) * P
                mm = tr(y_bank(G)[0:tw, c0:c0 + P], x_res[:, KT - 1, t0:t0 + tw], ident[:, :])
            mm.then_inc(last_rows_ready, 1)

        def first_group():
            take_aux("end")
            last_rows(0)

        n, z = N_FF + 63, S_FF + 63
        product_chunk(n, z, 0, mv_hi, mv_lo, {3: lambda: y_prompt_rows(KT - 2),
                                              6: lambda: y_sample_rows(KT - 2)}).then_inc(last_ready, 1)
        product_chunk(n, z, 1, mv_hi, mv_lo, {1: first_group}).then_inc(last_ready, 1)
        product_chunk(n, z, 2, mv_hi, mv_lo, {3: lambda: last_rows(1)}).then_inc(last_ready, 1)
        last_rows(2)

    @block.scalar
    def _(act):
        chain = Chain(act, act_step)

        def copy(out, in_, **kw):
            return nc.scalar.activation(out, in_, ACT.Copy, **kw)

        def wait_ready(n, i=None, per=0):
            act.wait_ge(ready[n % 2], n // 2 + 1 if i is None else i * (per // 2) + n // 2 + 1)

        def drain(n, out, func=ACT.Copy, **kw):
            wait_ready(n)
            for s, d in zip(pspans(n), spans(out)):
                ins = nc.scalar.activation(d, s, func, **kw)
            ins.then_inc(drained[n % 2], 1)

        def load(dst, src, sem):
            act.dma_start(dst, src, allow_slow_non_contiguous=True).then_inc(sem, 16)

        def ring_free(k):
            if k >= 2:
                act.wait_ge(outs[k % 2], 16 * (k // 2))

        vectors = [(vec_raw[row:row + a[name].shape[1], :], a[name][0])
                   for name, row in (("cconv_w", VA_CCW), ("sconv_w", VA_SCW))]
        vectors += [(vec_raw[row:row + 1, :], a[name]) for name, row in (
            ("pool_scale", VA_PSC), ("cconv_b", VA_CCB), ("cconv_ln_g", VA_LNG), ("cconv_ln_b", VA_LNB))]
        vectors += [(vec_raw[VA_N + row:VA_N + row + 2, :], a[name].rearrange("o (r c) -> (o r) c", r=2))
                    for name, row in (("norm_mix_g", VB_MIX), ("norm_x_g", VB_X), ("norm_ffn_g", VB_FFN),
                                      ("norm_mem_g", VB_MEM))]
        vectors += [(vec_raw[VA_N + VB_GATE:VA_N + VB_N, :], a["b_gate"][0].rearrange("b (r c) -> (b r) c", r=2))]
        for dst, src in vectors[:4]:
            load(dst, src, vec_in)

        def token_square(t):
            h = x_height(t)
            act.wait_ge(x_in[t % 4], 16 * (t // 4 + 1))
            if t >= 2:
                act.wait_ge(sq_done, t - 1)
            nc.scalar.activation(vring[0:h, t % 2, 0:1024], xring[0:h, t % 4, :], ACT.Square,
                                 accum_out=ss[0:h, t:t + 1]).then_inc(sq_done, 1)

        def token_root(t):
            h = x_height(t)
            act.wait_ge(var_done, t + 1)
            nc.scalar.activation(ss[0:h, t:t + 1], ss[0:h, t:t + 1], ACT.Sqrt).then_inc(std_done, 1)

        def token_hi(t):
            act.wait_ge(*scaled_tile(t))
            hi, lo = hsplit(t)
            copy(hi, fbuf[:, t % 2, 0:KT * x_height(t)].rearrange("p (k n) -> p k n", k=KT)).then_inc(hhi_done, 1)

        act.wait_ge(zeros_ready, 1)
        for s_ in range(9 + 3):
            if s_ < 11:
                token_square(s_)
            if 1 <= s_ <= 11:
                token_root(s_ - 1)
            if s_ < 2:
                for dst, src in (vectors[4:7], vectors[7:])[s_]:
                    load(dst, src, vec_in)
            if 3 <= s_ < 12:
                token_hi(s_ - 3)
            if s_ == 2:
                act.wait_ge(aux_ready, AUX["vec"] + 1)
                nv = VA_N + VB_N
                tables = PS[:, 2, 0:CT * nv].rearrange("p (c r) -> p r c", c=CT)
                copy(vec_a[:, :].rearrange("p (r c) -> p r c", c=CT), tables[:, 0:VA_N, :])
                copy(vec_b[:, :].rearrange("p (r c) -> p r c", c=CT), tables[:, VA_N:nv, :]).then_inc(aux_drained, 1)
            if s_ == 6:
                act.wait_ge(aux_ready, AUX["ws"] + 1)
                copy(flat(ws_t[:, :, :]), PS[:, 2, :])
                copy(flat(bd_t[:, :, :]), PS[0:N_SAMPLE, 5, 0:HEADS * N_SAMPLE]).then_inc(aux_drained, 1)
            if s_ == 8:
                act.wait_ge(aux_ready, AUX["pl"] + 1)
                copy(flat(st_pool[:, :, :]), PS[:, 2, 0:CT * 120])
                copy(flat(st_sc[:, :, :]), PS[:, 5, 0:CT * 16]).then_inc(aux_drained, 1)
                for dst, name in ((ln_g, "sgu_ln_g"), (ln_b, "sgu_ln_b")):
                    load(dst[:, :], a[name].broadcast_to([P, W_BR]), late_in)
        load(o["new_pool_sample"][0][:, 0:POOL_H - DEC_L, :], a["state_pool"][0][:, DEC_L:, :], state_out)
        load(o["new_cconv_sample"][0][:, 0:CCONV_H - DEC_L, :], a["state_cconv"][0][:, DEC_L:, :], state_out)
        def memory_hi_and_states():
            token_hi(9)
            token_hi(10)
            act.wait_ge(hlo_done, 11)
            act.wait_ge(aux_ready, AUX["cc"] + 1)
            for half in range(2):
                for ct in range(CT):
                    ins = copy(eheads(slots_d[:, ct + 1, :], CCONV_H)[:, 4 * half:4 * half + 4, :],
                               PS[:, 6 + half, ct * 120:(ct + 1) * 120].rearrange("p (b l) -> p b l", b=4))
            ins.then_inc(aux_drained, 1)

        def x_out(t):
            act.wait_ge(aux_ready, AUX[f"x{t}"] + 1)
            ring_free(t)
            t0, tw = TOK_TILES[t]
            copy(oring[:, t % 2, 0:KT * tw], flat(PS[:, 6:8, :])[:, 0:KT * tw]).then_inc(aux_drained, 1)
            act.wait_ge(aux_drained, AUX[f"x{t}"] + 1)
            act.dma_start(xt_dram[:, :, t0:t0 + tw].rearrange("k p t -> p k t"),
                          oring[:, t % 2, 0:KT * tw].rearrange("p (k t) -> p k t", k=KT)).then_inc(outs[t % 2], 16)

        def v_rows(g):
            act.wait_ge(aux_ready, AUX[f"v{g}a"] + 1)
            copy(v_tok[:, 0:8, g * P:(g + 1) * P],
                 flat(PS[:, 6:8, :]).rearrange("p (t c) -> p t c", t=8)).then_inc(aux_drained, 1)
            act.wait_ge(aux_ready, AUX[f"v{g}b"] + 1)
            copy(v_tok[0:N_SAMPLE, 8, g * P:(g + 1) * P], PS[0:N_SAMPLE, 6, 0:P]).then_inc(aux_drained, 1)

        def store_ring(k, dst, ready_sem, count):
            act.wait_ge(ready_sem, count)
            act.dma_start(dst, oring[:, k % 2, :]).then_inc(outs[k % 2], 16)

        def store_rows(aux_name, stage, head, new, out_prompt, out_sample):
            act.wait_ge(aux_ready, AUX[aux_name] + 1)
            copy(stage[:, 0, :], PS[0:N_SAMPLE, 6, :])
            copy(stage[0:head, 1, :], PS[0:head, 7, :]).then_inc(aux_drained, 1)
            act.wait_ge(aux_drained, AUX[aux_name] + 1)
            act.dma_start(out_prompt[0, 0], stage[0:head, 1, :]).then_inc(state_out, 16)
            for b in range(DEC_B):
                act.dma_start(out_sample[0, b][out_sample.shape[2] - new:, :],
                              stage[DEC_L * (b + 1) - new:DEC_L * (b + 1), 0, :]).then_inc(state_out, 16)

        def kv_rows(which, g):
            name = f"{'KV'[which]}{g}"
            act.wait_ge(aux_ready, AUX[name] + 1)
            n = 2 * which + g
            if n >= 1:
                act.wait_ge(kv_stored, 32 * n)
            copy(flat(kv_out[:, :, :]), flat(PS[:, 6:8, :])).then_inc(aux_drained, 1)
            act.wait_ge(aux_drained, AUX[name] + 1)
            out = o["mem_k_prompt" if which == 0 else "mem_v_prompt"][0, 0].rearrange("m h d -> m (h d)")
            for dst in (out, kv_dram[which]):
                act.dma_start(dst[:, g * W_BR:(g + 1) * W_BR].rearrange("(m p) c -> p m c", p=P),
                              kv_out[:, :, :]).then_inc(kv_stored, 16)

        for kind, j in PHASE1:
            if kind == "D" and j % 2 == 0:
                if j > 0:
                    n = N_OF["D", j - 1]
                    act.wait_ge(drained[n % 2], n // 2 + 1)
                if j == 2:
                    v_rows(3)
                    x_out(8)
                drain(N_OF["D", j], tmp[2][:, :], ACT.Sigmoid)
                if j == 0:
                    memory_hi_and_states()
                    x_out(0)
                    x_out(1)
                if j == 2:
                    act.wait_ge(v_var, 1)
                    nc.scalar.activation(v_rstd, v_rstd, ACT.Sqrt).then_inc(v_std, 1)
            if kind == "CV":
                if j == 0:
                    x_out(2)
                    x_out(3)
                else:
                    v_rows(j - 1)
                    for t in {1: (4, 5), 2: (6,), 3: (7,)}[j]:
                        x_out(t)
                drain(N_OF["CV", j], vring[:, j % 2, :], ACT.Gelu_apprx_tanh)
            if kind == "K" and j % 4 == 3:
                kv_rows(0, j // 4)
        for g in range(HEADS):
            if g >= 2:
                act.wait_ge(sgu_out, g - 1)
            drain(N_CU + 2 * g, vring[:, g % 2, :], ACT.Gelu_apprx_tanh)
            if g == 0:
                store_rows("tail_d", tail_d, CCONV_H, DEC_L, o["new_cconv_prompt"], o["new_cconv_sample"])
                act.wait_ge(v_norm, 9)
                act.dma_start(o["sgu_v_sample"][0].rearrange("b l w -> (b l) w"),
                              v_tok[0:N_SAMPLE, 8, :]).then_inc(state_out, 16)
            if g >= 1:
                store_ring(RING_C + g - 1, br_dram[2, g - 1], sgu_out, g)
            if g % 2 == 1:
                kv_rows(1, g // 2)
        act.wait_ge(kv_stored, 8 * 16)
        act.wait_ge(state_out, 16 * (2 + 9 + 1))
        def extend(g):
            n = N_A_IN[g]
            if g >= 2:
                act.wait_ge(pool_in_ready, g - 1)
            if g == 2:
                act.wait_ge(tails_ready, CT + 1)
            wait_ready(n)
            e = ext_a[:, g % 2, :]
            copy(eheads(e, POOL_H), st_pool[:, g, :].rearrange("p (b l) -> p b l", b=DEC_B))
            for s, d in zip(ppieces(n), epieces(e, POOL_H)):
                ins = copy(d, s)
            ins.then_inc(drained[n % 2], 1)

        extend(0)
        store_ring(RING_C + 3, br_dram[2, 3], sgu_out, 4)
        for g in range(CT):
            if g + 1 < CT:
                extend(g + 1)
            else:
                drain(N_B_H[0], b_h[:, :])
            ring_free(RING_A + g)
            n = N_A_MAP[g]
            drain(n, oring[:, (RING_A + g) % 2, :], scale=va(VA_PSC, g))
            store_ring(RING_A + g, br_dram[0, g], drained[n % 2], n // 2 + 1)

        def stage_load(u, i=None):
            q, ct = u // 4, u % 4
            k = BRANCHES[q]
            if i is None:
                if u >= 1:
                    act.wait_ge(br_lo_done, u)
                act.wait_ge(outs[(RING_OF[k] + ct) % 2], 16 * ((RING_OF[k] + ct) // 2 + 1))
                act.dma_start(stage_of(q), br_dram[k, ct]).then_inc(stage_in, 16)
            else:
                act.wait_ge(br_lo_done, i * 2 + u)
                src = br_dram[k][bass.ds(i * 2 + ct, 1)].rearrange("o p t -> p (o t)")
                act.dma_start(stage_of(q), src).then_inc(stage_in, 16)

        def stage_hi(u, i=None):
            q, ct = u // 4, u % 4
            if i is None:
                act.wait_ge(stage_in, 16 * (u + 1))
                copy(br_hi[q % 2][:, ct, :], stage_of(q)).then_inc(br_hi_done, 1)
            else:
                act.wait_ge(stage_in, i * 32 + 16 * (u + 1))
                copy(flat(br_hi[q % 2][:, bass.ds(i * 2 + ct, 1), :]), stage_of(q)).then_inc(br_hi_done, 1)

        for ct in range(CT):
            if ct == 0:
                store_rows("tail_a", tail_a, POOL_H, DEC_L, o["new_pool_prompt"], o["new_pool_sample"])
            else:
                n = N_B_C[ct - 1]
                act.wait_ge(drained[n % 2], n // 2 + 1)
                drain(N_B_H[ct], b_h[:, :])
            stage_load(ct)
            stage_hi(ct)
            if ct >= 1:
                store_ring(RING_B + ct - 1, br_dram[1, ct - 1], ring_full, ct)
            if ct == 1:
                act.wait_ge(dn_mean, 1)
                for c in range(CT):
                    if c >= 2:
                        act.wait_ge(dn_acc, c - 1)
                    nc.scalar.activation(tmp[2 if c == 0 else 0][:, :], slots_d[:, c, 0:T],
                                         ACT.Square).then_inc(dn_sq, 1)
            if ct == 2:
                act.wait_ge(dn_var, 1)
                nc.scalar.activation(tmp[2][:, :], tmp[2][:, :], ACT.Sqrt).then_inc(dn_std, 1)
        store_ring(RING_B + 3, br_dram[1, 3], ring_full, CT)
        for ct in range(CT):
            k = RING_D + ct
            act.wait_ge(dn_y, ct + 1)
            ring_free(k)
            nc.scalar.activation(oring[:, k % 2, :], slots_d[:, ct, 0:T], ACT.Silu, bias=va(VA_LNB, ct),
                                 scale=va(VA_LNG, ct)).then_inc(dn_out, 1)
            store_ring(k, br_dram[3, ct], dn_out, ct + 1)
        store_rows("tail_b", tail_b, SCONV_H, SCONV_H, o["new_sconv_prompt"], o["new_sconv_sample"])
        act.wait_ge(state_out, 16 * (2 + 9 + 1 + 9 + 9))
        for j in range(2):
            act.wait_ge(outs[j], 16 * len(range(j, 25, 2)))

        for q, k in enumerate(BRANCHES):
            with act.Fori(0, 2) as i:
                for mm_ in range(4):
                    pair, j = mm_ // 2, mm_ % 2
                    n = N_GATE + 16 * q + 4 * pair + j
                    m0 = 8 * q + mm_
                    act.wait_ge(gated, i * 4 + (m0 if m0 else 1))
                    wait_ready(n, i, 8)
                    g_t = tmp[1 + j]
                    for s, d in zip(pspans(n), spans(g_t)):
                        ins = nc.scalar.activation(d, s, ACT.Sigmoid,
                                                   bias=vec_b[:, bass.ds(i * 4 + (4 * VB_GATE + 8 * k + mm_), 1)])
                    ins.then_inc(drained[n % 2], 1)
                    if q < 3:
                        u = 4 * (q + 1) + mm_ // 2
                        if j == 0:
                            stage_load(u, i)
                        else:
                            stage_hi(u, i)
                    if q == 3 and j == 1:
                        for jj in range(2):
                            mj = mm_ - 1 + jj
                            act.wait_ge(gated, i * 4 + (8 * q + mj + 2))
                            copy(flat(mv_hi[:, bass.ds(i * 4 + mj, 1), :]),
                                 flat(merged[:, bass.ds(i * 4 + mj, 1), :])).then_inc(mv_hi_done, 1)

        def residual_tiles(ph, n0):
            with act.Fori(0, 4) as i:
                for j in range(2):
                    n = n0 + j
                    act.wait_ge(drained[n % 2], i + (n // 2 + 1))
                    act.wait_ge(sumsq, i * 2 + (9 * ph + 1 + j))
                    nc.scalar.activation(tmp[2][:, :], flat(x_res[:, bass.ds(i * 2 + j, 1), :]),
                                         ACT.Square).then_inc(res_sq, 1)
                    act.wait_ge(scaled, i * 2 + (8 * ph + j + 1))
                    copy(flat(xs_hi[:, bass.ds(i * 2 + j, 1), :]), tmp[1][:, :]).then_inc(xs_hi_done, 1)

        def root(ph):
            act.wait_ge(r_var, ph + 1)
            nc.scalar.activation(tmp[0][:, :], tmp[0][:, :], ACT.Sqrt).then_inc(r_std, 1)

        residual_tiles(0, N_MIX)
        root(0)

        def query_hi(m, n, i=None):
            act.wait_ge(drained[n % 2], n // 2 + 1 if i is None else i + (n // 2 + 1))
            dst = mv_hi[:, m, :] if i is None else flat(mv_hi[:, bass.ds(i * 2 + m, 1), :])
            copy(dst, tmp[1 + m % 2][:, :]).then_inc(mv_hi_done, 1)

        query_hi(0, N_Q)
        query_hi(1, N_Q + 1)
        with act.Fori(0, 2) as i:
            for j in range(2):
                query_hi(2 + j, N_Q + 2 + j, i)
        query_hi(6, N_Q + 6)

        for g in range(4):
            act.wait_ge(at_t, g + 1)
            copy(flat(kt_hi[:, 2 * g:2 * g + 2, :]), PS[:, K_BANKS[g], :]).then_inc(at_kh, 1)
            if g == 0:
                query_hi(7, N_Q + 7)
        scale = HEAD_DIM ** -0.5
        for v in range(32 + 7):
            if v < 32:
                act.wait_ge(mx_ready, v + 1)
                if v >= 4:
                    act.wait_ge(pt_ready, v - 3)
                nc.scalar.activation(probs[:, v % 4, :], PS[:, v % 4, 0:N_MEM], ACT.Exp,
                                     bias=sm[:, 4 + v % 4:5 + v % 4], scale=scale,
                                     accum_out=sm[:, 8 + v % 4:9 + v % 4]).then_inc(e_ready, 1)
            if 1 <= v <= 32:
                u = v - 1
                act.wait_ge(rs_ready, u + 1)
                copy(probs[:, u % 4, :], probs[:, u % 4, :], scale=sm[:, 12 + u % 4:13 + u % 4]).then_inc(p_ready, 1)
            if v - 3 in ATTEND:
                G, dt = ATTEND[v - 3]
                h, t0 = G // 2, 512 * (G % 2)
                act.wait_ge(pv_ready, 2 * G + dt + 1)
                copy(mv_hi[:, 2 * h + dt, t0:t0 + 512], PS[:, 6 + dt, :]).then_inc(o_hi, 1)
            if 2 <= v <= 33:
                u = v - 2
                G, c0 = u // 4, (u % 4) * P
                act.wait_ge(pt_ready, u + 1)
                if G >= 2:
                    act.wait_ge(pv_ready, 2 * (G - 1))
                copy(pt_hi[G % 2][:, :, c0:c0 + P],
                     PS[:, 4 + u % 2, 0:2 * P].rearrange("p (m t) -> p m t", m=2)).then_inc(pt_hi_done, 1)
        for b in range(DEC_B):
            act.wait_ge(ks_t, b + 1)
            if b >= 2:
                act.wait_ge(ss_ready, b - 1)
            copy(flat(kt_s[:, b % 2, 0:4, :]), flat(PS[:, 0:2, :])).then_inc(ks_a, 1)
        act.wait_ge(sm_mx, 1)
        for h in range(HEADS):
            nc.scalar.activation(p_s[:, h * N_MEM:(h + 1) * N_MEM], PS[0:N_SAMPLE, 4 + h, 0:N_MEM], ACT.Exp,
                                 bias=sm[0:N_SAMPLE, 20 + h:21 + h], scale=scale,
                                 accum_out=sm[0:N_SAMPLE, 24 + h:25 + h]).then_inc(sm_e, 1)
        act.wait_ge(so_ready, DEC_B)
        copy(p_s[:, :].rearrange("p (h d) -> p h d", h=HEADS), PS[0:N_SAMPLE, 4:8, 0:HEAD_DIM]).then_inc(so_copied, 1)
        act.wait_ge(so_t, 1)
        copy(mv_hi[:, :, SEQ:T], PS[:, 3, :].rearrange("p (k t) -> p k t", k=KT)).then_inc(so_hi, 1)

        residual_tiles(1, N_XO)
        root(1)

        def hidden(m, n, count, i=None):
            act.wait_ge(drained[n % 2], n // 2 + 1 if i is None else i + (n // 2 + 1))
            act.wait_ge(hid_ready, count if i is None else i * 2 + count)
            nc.scalar.activation(tmp[2][:, :], tmp[1][:, :], ACT.Square).then_inc(relu_done, 1)
            act.wait_ge(relu_done, count + 1 if i is None else i * 2 + (count + 1))
            dst = mv_hi[:, m, :] if i is None else flat(mv_hi[:, bass.ds(i * 2 + m, 1), :])
            copy(dst, tmp[2][:, :]).then_inc(hid_hi, 1)

        for c in range(4):
            n1 = N_FF + 16 * c
            m0 = 0
            if c == 0:
                hidden(0, n1, 0)
                hidden(1, n1 + 1, 1)
                m0 = 2
            with act.Fori(0, (8 - m0) // 2) as i:
                for j in range(2):
                    hidden(m0 + j, n1 + m0 + j, 8 * c + m0 + j, i)


        def y_squares(part, tiles):
            f0, f1 = Y_PARTS[part]
            for t in tiles:
                tw, k = TOK_TILES[t][1], 9 * part + t
                if k >= 2:
                    act.wait_ge(fs_sq, k - 1)
                nc.scalar.activation(junk[0:tw, k % 2, f0:f1], y_tok[0:tw, t, f0:f1], ACT.Square,
                                     accum_out=fst[0:tw, part, t:t + 1]).then_inc(fs_sq, 1)

        for m in range(KT - 1):
            act.wait_ge(aux_ready, AUX[f"y{m}a"] + 1)
            copy(y_tok[:, 0:8, m * P:(m + 1) * P],
                 flat(PS[:, 6:8, :]).rearrange("p (t c) -> p t c", t=8)).then_inc(aux_drained, 1)
            act.wait_ge(aux_ready, AUX[f"y{m}b"] + 1)
            copy(y_tok[0:N_SAMPLE, 8, m * P:(m + 1) * P], PS[0:N_SAMPLE, 6, 0:P]).then_inc(aux_drained, 1)
            if m in (4, 5):
                act.wait_ge(aux_drained, AUX[f"y{m}b"] + 1)
                act.wait_ge(fst_ready, 1)
                y_squares(m - 4, range(9))
        m = KT - 1
        for G, tiles in enumerate(Y_GROUPS):
            act.wait_ge(last_rows_ready, G + 1)
            whole = [t for t in tiles if t < 8]
            ins = copy(y_tok[:, whole[0]:whole[-1] + 1, m * P:(m + 1) * P],
                       y_bank(G)[:, 0:len(whole) * P].rearrange("p (t c) -> p t c", c=P))
            if 8 in tiles:
                c0 = len(whole) * P
                ins = copy(y_tok[0:N_SAMPLE, 8, m * P:(m + 1) * P], y_bank(G)[0:N_SAMPLE, c0:c0 + P])
            ins.then_inc(last_copied, 1)
            act.wait_ge(last_copied, G + 1)
            y_squares(2, tiles)
            act.wait_ge(fs_var, G + 1)
            f = fst[:, 0, tiles[0]:tiles[-1] + 1]
            nc.scalar.activation(f, f, ACT.Sqrt).then_inc(fs_std, 1)

    @block.vector
    def _(dve):
        chain = Chain(dve, dve_step)
        link = chain.link
        v = nc.vector
        taps = [0]

        def wait_ready(n, i=None, per=0):
            dve.wait_ge(ready[n % 2], n // 2 + 1 if i is None else i * (per // 2) + n // 2 + 1)

        v.memset(ones[:, :], 1.0).then_inc(ones_ready, 1)
        v.memset(small[:, :], 1.0).then_inc(zeros_ready, 1)
        dve.wait_ge(zeros_ready, 1)
        for j in range(POOL_H):
            ins = v.memset(small[:, 104 + j:105 + j], 1.0 / (j + 1))
        link(ins)
        def token_scaled(t):
            if t == 0:
                dve.wait_ge(aux_drained, AUX["vec"] + 1)
            dve.wait_ge(*tile_transposed(t))
            if t >= 2:
                dve.wait_ge(hhi_done, t - 1)
                dve.wait_ge(hlo_done, t - 1)
            h = x_height(t)
            row = VB_MIX if t < 9 else VB_MEM
            gain = vec_b[:, 4 * row:4 * row + KT].unsqueeze(2).broadcast_to([P, KT, h])
            v.tensor_tensor(fbuf[:, t % 2, 0:KT * h].rearrange("p (k n) -> p k n", k=KT),
                            tile_psum(t)[:, 0:KT * h].rearrange("p (k n) -> p k n", k=KT),
                            gain, ALU.mult).then_inc(scaled_tile(t)[0], 1)

        def token_normalised(t):
            h = x_height(t)
            dve.wait_ge(std_done, t + 1)
            link(v.reciprocal(ss[0:h, t:t + 1], ss[0:h, t:t + 1]))
            if t >= 2:
                dve.wait_ge(*tile_transposed(t - 2))
            v.tensor_scalar(xn[0:h, t % 2, :], xring[0:h, t % 4, :], ss[0:h, t:t + 1], None,
                            ALU.mult).then_inc(xn_ready, 1)

        for s_ in range(11 + 2):
            if s_ < 11:
                h = x_height(s_)
                dve.wait_ge(sq_done, s_ + 1)
                v.tensor_scalar(ss[0:h, s_:s_ + 1], ss[0:h, s_:s_ + 1], 1.0 / D_MODEL, EPS, ALU.mult,
                                ALU.add).then_inc(var_done, 1)
            if 1 <= s_ <= 11:
                token_normalised(s_ - 1)
            if s_ >= 2:
                token_scaled(s_ - 2)

        dve.wait_ge(hlo_done, 11)
        dve.wait_ge(hhi_done, 11)
        dve.wait_ge(aux_ready, AUX["cc"] + 1)
        for ct in range(CT):
            ins = v.memset(slots_d[:, ct + 1, 0:CCONV_H], 0.0)
        link(ins)

        def conv_taps(count):
            for _ in range(count):
                ct, j = taps[0] // CCONV_K, taps[0] % CCONV_K
                taps[0] += 1
                acc, ext = slots_d[:, ct, 0:T], slots_d[:, ct + 1, :]
                w = va(VA_CCW + j, ct)
                pairs = ((acc[:, 0:SEQ], ext[:, j:j + SEQ]),
                         (acc[:, SEQ:T].rearrange("p (b l) -> p b l", b=DEC_B), eseq(ext, CCONV_H, j)))
                for dst, src in pairs:
                    if j == 0:
                        ins = v.tensor_scalar(dst, src, w, va(VA_CCB, ct), ALU.mult, ALU.add)
                    else:
                        ins = v.scalar_tensor_tensor(out=dst, in0=src, scalar=w, in1=dst, op0=ALU.mult, op1=ALU.add)
                if j == CCONV_K - 1:
                    ins.then_inc(conv_done, 1)
                    dve.wait_ge(conv_done, ct + 1)
                else:
                    link(ins)

        def keep_tails(ext, head, ct):
            v.tensor_copy(tailbuf[:, ct, 0:head], ext[:, SEQ:SEQ + head])
            v.tensor_copy(tailbuf[:, ct, CCONV_H:].rearrange("p (b l) -> p b l", b=DEC_B),
                          eseq(ext, head, head)).then_inc(tails_ready, 1)

        for ct in range(CT):
            n, n_b = N_OF["D", 2 * ct + 1], N_OF["D", 2 * ct]
            wait_ready(n)
            dve.wait_ge(drained[n_b % 2], n_b // 2 + 1)
            ext = slots_d[:, ct + 1, :]
            for s, g, d in zip(ppieces(n), pieces(tmp[2]), epieces(ext, CCONV_H)):
                ins = v.tensor_tensor(d, s, g, ALU.mult)
            ins.then_inc(drained[n % 2], 1)
            dve.wait_ge(drained[n % 2], n // 2 + 1)
            keep_tails(ext, CCONV_H, ct)
            if ct == 1:
                dve.wait_ge(aux_drained, AUX["v3b"] + 1)
                for t, (t0, tw) in enumerate(TOK_TILES):
                    ins = v.bn_stats(bn[0:tw, t, :], v_tok[0:tw, t, :])
                link(ins)
                for t, (t0, tw) in enumerate(TOK_TILES):
                    ins = v.bn_aggr(bn_mv[0:tw, t, :], bn[0:tw, t, :])
                link(ins)
                v.tensor_scalar(v_rstd.unsqueeze(2), bn_mv[:, :, 1:2], EPS, None, ALU.add).then_inc(v_var, 1)
                dve.wait_ge(v_std, 1)
                link(v.reciprocal(v_rstd, v_rstd))
                dve.wait_ge(late_in, 32)
            if ct >= 1:
                for t in range(3 * ct - 3, 3 * ct):
                    tw = TOK_TILES[t][1]
                    vt = v_tok[0:tw, t, :]
                    link(v.tensor_scalar(vt, vt, bn_mv[0:tw, t, 0:1], v_rstd[0:tw, t:t + 1], ALU.subtract, ALU.mult))
                    link(v.tensor_tensor(vt, vt, ln_g[0:tw, :], ALU.mult))
                    v.tensor_tensor(vt, vt, ln_b[0:tw, :], ALU.add).then_inc(v_norm, 1)
            conv_taps(TAPS_D[ct])

        dve.wait_ge(maps_in, 32)
        for g in range(HEADS):
            n = N_CU + 2 * g + 1
            k = RING_C + g
            wait_ready(n)
            dve.wait_ge(drained[(n - 1) % 2], (n - 1) // 2 + 1)
            dve.wait_ge(outs[k % 2], 16 * (k // 2))
            acc, dst = flat(pset(n)), oring[:, k % 2, :]
            v.tensor_tensor(dst[:, 0:SEQ].rearrange("p (n t) -> p n t", n=8),
                            acc[:, 0:SEQ].rearrange("p (n t) -> p n t", n=8),
                            bias_s[:, g, :].unsqueeze(1).broadcast_to([P, 8, P]), ALU.add)
            v.tensor_tensor(dst[:, SEQ:T].rearrange("p (n t) -> p n t", n=DEC_B),
                            acc[:, SEQ:T].rearrange("p (n t) -> p n t", n=DEC_B),
                            bias_s[:, g, 0:DEC_L].unsqueeze(1).broadcast_to([P, DEC_B, DEC_L]),
                            ALU.add).then_inc(drained[n % 2], 1)
            dve.wait_ge(drained[n % 2], n // 2 + 1)
            v.tensor_tensor(dst, dst, vring[:, g % 2, :], ALU.mult).then_inc(sgu_out, 1)
            conv_taps(TAPS_CU[g])

        dve.wait_ge(aux_drained, AUX["V1"] + 1)
        dve.wait_ge(aux_drained, AUX["tail_d"] + 1)
        dve.wait_ge(kv_stored, 8 * 16)
        dve.wait_ge(state_out, 16 * (2 + 9 + 1))
        for j in range(2):
            ins = v.memset(ext_a[:, j, 0:POOL_H], 0.0)
        link(ins)
        for g in range(CT):
            n = N_A_IN[g]
            dve.wait_ge(drained[n % 2], n // 2 + 1)
            e = ext_a[:, g % 2, :]
            keep_tails(e, POOL_H, g)
            src = e
            for lv in range(g + 1):
                s = 1 << lv
                dst = sums[:, lv % 2, :]
                lo = 2 * s - 1
                link(v.tensor_tensor(dst[:, lo:EXT_A], src[:, lo:EXT_A], src[:, lo - s:EXT_A - s], ALU.add))
                src = dst
            if g >= 1:
                wait_ready(N_A_MAP[g - 1])
            w = 1 << (g + 1)
            pairs = ((pooled[:, 0:SEQ], src[:, POOL_H:POOL_H + SEQ], e[:, POOL_H:POOL_H + SEQ]),
                     (pooled[:, SEQ:T].rearrange("p (b l) -> p b l", b=DEC_B), eseq(src, POOL_H, POOL_H),
                      eseq(e, POOL_H, POOL_H)))
            for dst, sm_, x_ in pairs:
                ins = v.scalar_tensor_tensor(out=dst, in0=sm_, scalar=1.0 / w, in1=x_, op0=ALU.mult,
                                             op1=ALU.subtract)
            link(ins)
            link(v.tensor_tensor(pooled[:, 0:w - 1], src[:, POOL_H:POOL_H + w - 1], inv_cnt[:, 0:w - 1], ALU.mult))
            v.tensor_tensor(pooled[:, 0:w - 1], pooled[:, 0:w - 1], e[:, POOL_H:POOL_H + w - 1],
                            ALU.subtract).then_inc(pool_in_ready, 1)
            conv_taps(TAPS_A[g])

        def stage_lo(u, i=None):
            q, ct = u // 4, u % 4
            if i is None:
                dve.wait_ge(br_hi_done, u + 1)
                hi, lo = br_hi[q % 2][:, ct, :], br_lo[q % 2][:, ct, :]
            else:
                dve.wait_ge(br_hi_done, i * 2 + (u + 1))
                hi = flat(br_hi[q % 2][:, bass.ds(i * 2 + ct, 1), :])
                lo = flat(br_lo[q % 2][:, bass.ds(i * 2 + ct, 1), :])
            v.tensor_tensor(lo, stage_of(q), hi.bitcast(F32), ALU.subtract).then_inc(br_lo_done, 1)

        conv_taps(TAPS_B[0])
        dve.wait_ge(aux_ready, AUX["tail_a"] + 1)
        link(v.memset(ext_b[:, 0:SCONV_H], 0.0))
        for ct in range(CT):
            nh, n_c, nb_ = N_B_H[ct], N_B_C[ct], N_B_B[ct]
            wait_ready(n_c)
            dve.wait_ge(drained[nh % 2], nh // 2 + 1)
            v.tensor_copy(eheads(ext_b, SCONV_H), st_sc[:, ct, :].rearrange("p (b l) -> p b l", b=DEC_B))
            for s, g, d in zip(ppieces(n_c), pieces(b_h), epieces(ext_b, SCONV_H)):
                ins = v.tensor_tensor(d, s, g, ALU.mult)
            ins.then_inc(drained[n_c % 2], 1)
            dve.wait_ge(drained[n_c % 2], n_c // 2 + 1)
            keep_tails(ext_b, SCONV_H, ct)
            acc = vring[:, 0, :]
            for j in range(SCONV_K):
                w = va(VA_SCW + j, ct)
                for dst, src in ((acc[:, 0:SEQ], ext_b[:, j:j + SEQ]),
                                 (acc[:, SEQ:T].rearrange("p (b l) -> p b l", b=DEC_B), eseq(ext_b, SCONV_H, j))):
                    if j == 0:
                        ins = v.tensor_scalar(dst, src, w, None, ALU.mult)
                    else:
                        ins = v.scalar_tensor_tensor(out=dst, in0=src, scalar=w, in1=dst, op0=ALU.mult, op1=ALU.add)
                link(ins)
            if ct == 0:
                conv_taps(TAPS_B[1])
                for c in range(1, CT):
                    ins = v.tensor_tensor(tmp[2][:, :], slots_d[:, 0, 0:T] if c == 1 else tmp[2][:, :],
                                          slots_d[:, c, 0:T], ALU.add)
                    if c < CT - 1:
                        link(ins)
                ins.then_inc(dn_sum, 1)
            if ct == 1:
                n = N_MEAN
                wait_ready(n)
                for c in range(CT):
                    for s, d in zip(pspans(n), spans(slots_d[:, c, 0:T])):
                        ins = v.scalar_tensor_tensor(out=d, in0=s, scalar=-1.0 / W_BR, in1=d, op0=ALU.mult,
                                                     op1=ALU.add)
                ins.then_inc(drained[n % 2], 1)
                dve.wait_ge(drained[n % 2], n // 2 + 1)
                dve.sem_inc(dn_mean, 1)
            if ct == 2:
                n = N_VAR
                wait_ready(n)
                for s, d in zip(pspans(n), spans(tmp[2])):
                    ins = v.tensor_scalar(d, s, 1.0 / W_BR, EPS, ALU.mult, ALU.add)
                ins.then_inc(drained[n % 2], 1)
                dve.wait_ge(drained[n % 2], n // 2 + 1)
                dve.sem_inc(dn_var, 1)
            k = RING_B + ct
            dve.wait_ge(outs[k % 2], 16 * (k // 2))
            wait_ready(nb_)
            for s, x_, d in zip(pspans(nb_), spans(acc), spans(oring[:, k % 2, :])):
                ins = v.tensor_tensor(d, s, x_, ALU.mult)
            ins.then_inc(drained[nb_ % 2], 1)
            dve.wait_ge(drained[nb_ % 2], nb_ // 2 + 1)
            dve.sem_inc(ring_full, 1)
            stage_lo(ct)
            if ct == 2:
                dve.wait_ge(dn_std, 1)
                link(v.reciprocal(tmp[2][:, :], tmp[2][:, :]))
                for c in range(CT):
                    v.tensor_tensor(slots_d[:, c, 0:T], slots_d[:, c, 0:T], tmp[2][:, :], ALU.mult).then_inc(dn_y, 1)
            if ct == 0:
                conv_taps(TAPS_B[2])
            if ct == 1:
                for c in range(1, CT):
                    dve.wait_ge(dn_sq, c + 1)
                    v.tensor_tensor(tmp[2][:, :], tmp[2][:, :], tmp[0][:, :], ALU.add).then_inc(dn_acc, 1)
                    dve.wait_ge(dn_acc, c)
        assert taps[0] == CT * CCONV_K
        for j in range(2):
            dve.wait_ge(outs[j], 16 * len(range(j, 25, 2)))
        dve.sem_inc(gated, 1)

        for q in range(4):
            with dve.Fori(0, 2) as i:
                for mm_ in range(4):
                    pair, j = mm_ // 2, mm_ % 2
                    ng = N_GATE + 16 * q + 4 * pair + j
                    n = ng + 2
                    g_t = tmp[1 + j]
                    wait_ready(n, i, 8)
                    dve.wait_ge(drained[ng % 2], i * 4 + (ng // 2 + 1))
                    for s, d in zip(pspans(n), spans(g_t)):
                        ins = v.tensor_tensor(d, s, d, ALU.mult)
                    ins.then_inc(drained[n % 2], 1)
                    dve.wait_ge(drained[n % 2], i * 4 + (n // 2 + 1))
                    m_t = flat(merged[:, bass.ds(i * 4 + mm_, 1), :])
                    if q == 0:
                        v.tensor_copy(m_t, g_t[:, :]).then_inc(gated, 1)
                    else:
                        v.tensor_tensor(m_t, m_t, g_t[:, :], ALU.add).then_inc(gated, 1)
                    if q < 3 and j == 1:
                        stage_lo(4 * (q + 1) + mm_ // 2, i)
                    if q == 3:
                        dve.wait_ge(mv_hi_done, i * 4 + (mm_ + 1))
                        v.tensor_tensor(flat(mv_lo[:, bass.ds(i * 4 + mm_, 1), :]), m_t,
                                        flat(mv_hi[:, bass.ds(i * 4 + mm_, 1), :]).bitcast(F32),
                                        ALU.subtract).then_inc(mv_lo_done, 1)

        def residual_tiles(ph, n0, row):
            c0 = 9 * ph + 1
            v.memset(tmp[0][:, :], 0.0).then_inc(sumsq, 1)
            dve.wait_ge(sumsq, c0)
            with dve.Fori(0, 4) as i:
                for j in range(2):
                    n = n0 + j
                    dve.wait_ge(ready[n % 2], i + (n // 2 + 1))
                    x_t = x_res[:, bass.ds(i * 2 + j, 1), :]
                    x_f = flat(x_t)
                    for s, d in zip(pspans(n), spans(x_f)):
                        ins = v.tensor_tensor(d, s, d, ALU.add)
                    ins.then_inc(drained[n % 2], 1)
                    dve.wait_ge(drained[n % 2], i + (n // 2 + 1))
                    v.tensor_scalar(tmp[1][:, :], x_f, vec_b[:, bass.ds(i * 2 + (4 * row + j), 1)], None,
                                    ALU.mult).then_inc(scaled, 1)
                    dve.wait_ge(res_sq, i * 2 + (8 * ph + j + 1))
                    v.tensor_tensor(tmp[0][:, :], tmp[0][:, :], tmp[2][:, :], ALU.add).then_inc(sumsq, 1)
                    dve.wait_ge(sumsq, i * 2 + (c0 + j + 1))
                    dve.wait_ge(scaled, i * 2 + (8 * ph + j + 1))
                    dve.wait_ge(xs_hi_done, i * 2 + (8 * ph + j + 1))
                    v.tensor_tensor(flat(xs_lo[:, bass.ds(i * 2 + j, 1), :]), tmp[1][:, :],
                                    flat(xs_hi[:, bass.ds(i * 2 + j, 1), :]).bitcast(F32),
                                    ALU.subtract).then_inc(xs_lo_done, 1)

        def inverse_rms(ph, n):
            dve.wait_ge(aux_ready, AUX[f"sum{ph}"] + 1)
            v.tensor_scalar(tmp[0][:, 0:SEQ], flat(PS[:, 6:8, :]), 1.0 / D_MODEL, EPS, ALU.mult,
                            ALU.add).then_inc(aux_drained, 1)
            wait_ready(n)
            dve.wait_ge(aux_drained, AUX[f"sum{ph}"] + 1)
            v.tensor_scalar(tmp[0][:, SEQ:T], pset(n)[:, 2, CW:CW + N_SAMPLE], 1.0 / D_MODEL, EPS, ALU.mult,
                            ALU.add).then_inc(r_var, 1)
            dve.wait_ge(r_std, ph + 1)
            v.reciprocal(tmp[0][:, :], tmp[0][:, :]).then_inc(r_ready, 1)
            dve.wait_ge(r_ready, ph + 1)

        for i in range(4):
            dve.wait_ge(xres_in[i], 16)
        residual_tiles(0, N_MIX, VB_X)
        inverse_rms(0, N_Q)

        def query(m, n, count, i=None):
            cnt = n // 2 + 1 if i is None else i + (n // 2 + 1)
            dve.wait_ge(ready[n % 2], cnt)
            t_ = tmp[1 + m % 2]
            for s, r, d in zip(pspans(n), spans(tmp[0]), spans(t_)):
                ins = v.tensor_tensor(d, s, r, ALU.mult)
            ins.then_inc(drained[n % 2], 1)
            dve.wait_ge(drained[n % 2], cnt)
            dve.wait_ge(mv_hi_done, count + 1 if i is None else i * 2 + (count + 1))
            hi = mv_hi[:, m, :] if i is None else flat(mv_hi[:, bass.ds(i * 2 + m, 1), :])
            lo = mv_lo[:, m, :] if i is None else flat(mv_lo[:, bass.ds(i * 2 + m, 1), :])
            v.tensor_tensor(lo, t_[:, :], hi.bitcast(F32), ALU.subtract).then_inc(mv_lo_done, 1)

        query(0, N_Q, KT)
        query(1, N_Q + 1, KT + 1)
        with dve.Fori(0, 3) as i:
            for j in range(2):
                query(2 + j, N_Q + 2 + j, KT + 2 + j, i)

        for g in range(4):
            dve.wait_ge(at_kh, g + 1)
            v.tensor_tensor(flat(kt_lo[:, 2 * g:2 * g + 2, :]), PS[:, K_BANKS[g], :],
                            flat(kt_hi[:, 2 * g:2 * g + 2, :]).bitcast(F32), ALU.subtract).then_inc(at_kl, 1)
        scale = HEAD_DIM ** -0.5

        def row_max(u):
            k = u % 4
            dve.wait_ge(sc_ready, u + 1)
            link(v.tensor_reduce(sm[:, k:k + 1], PS[:, k, 0:N_MEM], AX_X, ALU.max))
            v.tensor_scalar(sm[:, 4 + k:5 + k], sm[:, k:k + 1], -scale, None, ALU.mult).then_inc(mx_ready, 1)

        def masked_query(b):
            q3 = qm[b % 4][:, :].rearrange("p (k t) -> p k t", k=KT)
            if b >= 4:
                dve.wait_ge(ss_ready, b - 3)
                link(v.memset(q3[:, :, DEC_L * (b - 4):DEC_L * (b - 3)], 0.0))
            s0 = SEQ + DEC_L * b
            v.tensor_tensor(q3[:, :, DEC_L * b:DEC_L * (b + 1)], mv_hi[:, :, s0:s0 + DEC_L].bitcast(F32),
                            mv_lo[:, :, s0:s0 + DEC_L].bitcast(F32), ALU.add).then_inc(qm_ready, 1)

        row_max(0)
        for w_ in range(32 + 8):
            if 1 <= w_ <= 32:
                k = (w_ - 1) % 4
                dve.wait_ge(e_ready, w_)
                v.reciprocal(sm[:, 12 + k:13 + k], sm[:, 8 + k:9 + k]).then_inc(rs_ready, 1)
            if w_ + 1 < 32:
                row_max(w_ + 1)
            if w_ == 36:
                dve.wait_ge(qm_zero, 1)
                for b in range(4):
                    masked_query(b)
            if w_ - 4 in ATTEND:
                G, dt = ATTEND[w_ - 4]
                h, t0 = G // 2, 512 * (G % 2)
                dve.wait_ge(o_hi, 2 * G + dt + 1)
                v.tensor_tensor(mv_lo[:, 2 * h + dt, t0:t0 + 512], PS[:, 6 + dt, :],
                                mv_hi[:, 2 * h + dt, t0:t0 + 512].bitcast(F32), ALU.subtract).then_inc(o_lo, 1)
            if 3 <= w_ <= 34:
                u = w_ - 3
                G, c0 = u // 4, (u % 4) * P
                dve.wait_ge(pt_hi_done, u + 1)
                v.tensor_tensor(pt_lo[G % 2][:, :, c0:c0 + P],
                                PS[:, 4 + u % 2, 0:2 * P].rearrange("p (m t) -> p m t", m=2),
                                pt_hi[G % 2][:, :, c0:c0 + P].bitcast(F32), ALU.subtract).then_inc(pt_lo_done, 1)
        for b in range(DEC_B):
            dve.wait_ge(ks_t, b + 1)
            if b >= 2:
                dve.wait_ge(ss_ready, b - 1)
            v.tensor_copy(flat(kt_s[:, b % 2, 4:8, :]), flat(PS[:, 2:4, :])).then_inc(ks_d, 1)
            if b >= 4:
                masked_query(b)
        dve.wait_ge(ss_ready, DEC_B)
        n64 = N_SAMPLE
        link(v.tensor_reduce(sm[0:n64, 16:20], PS[0:n64, 4:8, 0:N_MEM], AX_X, ALU.max))
        v.tensor_scalar(sm[0:n64, 20:24], sm[0:n64, 16:20], -scale, None, ALU.mult).then_inc(sm_mx, 1)
        dve.wait_ge(sm_e, HEADS)
        link(v.reciprocal(sm[0:n64, 28:32], sm[0:n64, 24:28]))
        for h in range(HEADS):
            ps_h = p_s[:, h * N_MEM:(h + 1) * N_MEM]
            ins = v.tensor_scalar(ps_h, ps_h, sm[0:n64, 28 + h:29 + h], None, ALU.mult)
        ins.then_inc(sm_p, 1)
        dve.wait_ge(sm_t, 1)
        dve.wait_ge(ptm_zero, 1)
        blocks = PS[:, 3, :].rearrange("p (j t) -> p j t", t=n64)
        for b in range(DEC_B):
            ins = v.tensor_copy(ptm[:, b, :].rearrange("p (j t) -> p j t", t=n64)[:, :, DEC_L * b:DEC_L * (b + 1)],
                                blocks[:, :, DEC_L * b:DEC_L * (b + 1)])
        ins.then_inc(sm_pt, 1)
        dve.wait_ge(so_hi, 1)
        v.tensor_tensor(mv_lo[:, :, SEQ:T], PS[:, 3, :].rearrange("p (k t) -> p k t", k=KT),
                        mv_hi[:, :, SEQ:T].bitcast(F32), ALU.subtract).then_inc(so_lo, 1)

        residual_tiles(1, N_XO, VB_FFN)
        inverse_rms(1, N_FF)

        def hidden(m, n, count, i=None):
            cnt = n // 2 + 1 if i is None else i + (n // 2 + 1)
            dve.wait_ge(ready[n % 2], cnt)
            for s, r, d in zip(pspans(n), spans(tmp[0]), spans(tmp[1])):
                ins = v.scalar_tensor_tensor(out=d, in0=s, scalar=0.0, in1=r, op0=ALU.max, op1=ALU.mult)
            ins.then_inc(drained[n % 2], 1)
            dve.wait_ge(hid_hi, count + 1 if i is None else i * 2 + (count + 1))
            hi = mv_hi[:, m, :] if i is None else flat(mv_hi[:, bass.ds(i * 2 + m, 1), :])
            lo = mv_lo[:, m, :] if i is None else flat(mv_lo[:, bass.ds(i * 2 + m, 1), :])
            v.tensor_tensor(lo, tmp[2][:, :], hi.bitcast(F32), ALU.subtract).then_inc(hid_ready, 1)

        for c in range(4):
            n1, n2 = N_FF + 16 * c, N_FF + 16 * c + 8
            m0 = 0
            if c == 0:
                hidden(0, n1, 0)
                hidden(1, n1 + 1, 1)
                m0 = 2
            with dve.Fori(0, (8 - m0) // 2) as i:
                for j in range(2):
                    hidden(m0 + j, n1 + m0 + j, 8 * c + m0 + j, i)
            if c == 3:
                dve.wait_ge(gf_in, 16)
                v.memset(fst[:, :, :], 1.0).then_inc(fst_ready, 1)
            with dve.Fori(0, 4 if c < 3 else 3) as i:
                for j in range(2):
                    n = n2 + j
                    dve.wait_ge(ready[n % 2], i + (n // 2 + 1))
                    x_f = flat(x_res[:, bass.ds(i * 2 + j, 1), :])
                    for s, d in zip(pspans(n), spans(x_f)):
                        ins = v.tensor_tensor(d, s, d, ALU.add)
                    ins.then_inc(drained[n % 2], 1)

        n = N_FF + 62
        wait_ready(n)
        for s, d in zip(pspans(n), spans(x_res[:, KT - 2, :])):
            ins = v.tensor_tensor(d, s, d, ALU.add)
        ins.then_inc(drained[n % 2], 1)

        def add_last(c):
            c0, cw = CHUNKS[c]
            dve.wait_ge(last_ready, c + 1)
            x_ = x_res[:, KT - 1, c0:c0 + cw]
            v.tensor_tensor(x_, pset(N_FF + 63)[:, c, 0:cw], x_, ALU.add).then_inc(last_added, 1)

        def y_root(G):
            tiles = Y_GROUPS[G]
            dve.wait_ge(fs_sq, 18 + tiles[-1] + 1)
            f = [fst[:, part, tiles[0]:tiles[-1] + 1] for part in range(3)]
            link(v.tensor_tensor(f[0], f[0], f[1], ALU.add))
            link(v.tensor_tensor(f[0], f[0], f[2], ALU.add))
            v.tensor_scalar(f[0], f[0], 1.0 / D_MODEL, EPS, ALU.mult, ALU.add).then_inc(fs_var, 1)
            dve.wait_ge(fs_std, G + 1)
            link(v.reciprocal(f[0], f[0]))

        def y_scaled(G):
            for t in Y_GROUPS[G]:
                tw = TOK_TILES[t][1]
                y_ = y_tok[0:tw, t, :]
                v.scalar_tensor_tensor(out=y_, in0=y_, scalar=fst[0:tw, 0, t:t + 1], in1=gf[0:tw, :],
                                       op0=ALU.mult, op1=ALU.mult).then_inc(y_ready, 1)

        add_last(0)
        y_root(0)
        add_last(1)
        y_scaled(0)
        y_root(1)
        add_last(2)
        y_scaled(1)
        y_root(2)
        y_scaled(2)


_INS = ["x_prompt", "x_sample", "state_pool", "state_sconv", "state_cconv", "cache_mem_k", "cache_mem_v",
        "mem_prompt", "norm_mix_g", "w_in", "pool_w", "pool_scale", "sconv_w", "sgu_ln_g", "sgu_ln_b", "sgu_w",
        "sgu_b", "cconv_w", "cconv_b", "cconv_ln_g", "cconv_ln_b", "w_branch", "b_gate", "w_mix_out", "norm_x_g",
        "norm_mem_g", "w_xq", "w_xk", "w_xv", "w_xo", "norm_ffn_g", "w_ff1", "w_ff2", "norm_f_g"]
_OUTS = {
    "y_prompt": (1, SEQ, D_MODEL),
    "y_sample": (DEC_B, DEC_L, D_MODEL),
    "new_pool_prompt": (1, 1, POOL_H, W_BR),
    "new_sconv_prompt": (1, 1, SCONV_H, W_BR),
    "new_cconv_prompt": (1, 1, CCONV_H, W_BR),
    "mem_k_prompt": (1, 1, N_MEM, HEADS, HEAD_DIM),
    "mem_v_prompt": (1, 1, N_MEM, HEADS, HEAD_DIM),
    "new_pool_sample": (1, DEC_B, POOL_H, W_BR),
    "new_sconv_sample": (1, DEC_B, SCONV_H, W_BR),
    "new_cconv_sample": (1, DEC_B, CCONV_H, W_BR),
    "sgu_v_sample": (1, DEC_B, DEC_L, W_BR),
}


def kernel(**inputs):
    import numpy as _np
    import concourse.bacc as _bacc
    from concourse.bass_utils import run_bass_kernel_spmd as _run

    nc = _bacc.Bacc("TRN2", target_bir_lowering=False, num_devices=1)
    arrays, a, o = {}, {}, {}
    for name in _INS:
        x = _np.ascontiguousarray(inputs[name])
        arrays[f"in_{name}"] = x
        a[name] = nc.dram_tensor(f"in_{name}", x.shape, mybir.dt.from_np(x.dtype), kind="ExternalInput").ap()
    for name, shape in _OUTS.items():
        o[name] = nc.dram_tensor(f"out_{name}", shape, F32, kind="ExternalOutput").ap()
    scratch = {
        "xt": nc.dram_tensor("xt_scratch", (KT, P, T), F32).ap(),
        "branch": nc.dram_tensor("branch_scratch", (4, CT, P, T), F32).ap(),
        "kv": nc.dram_tensor("kv_scratch", (2, N_MEM, D_MODEL), F32).ap(),
    }
    build(nc, a, o, scratch)
    r = _run(nc, [arrays], core_ids=[0])
    return tuple(r.results[0][f"out_{name}"] for name in _OUTS)
```
